# Optimizing a Trainium2 kernel written in Bass

```python
import math
import jax, jax.numpy as jnp
from jax import lax
import numpy as np

D_MODEL = 1024
BATCH = 1
SEQ = 512
DEPTH = 2
DEC_BATCH = 8
DEC_SEQ = 4
PAST_LEN = 4096
PAGE_SIZE = 128

N_MIXERS = 2
N_LRU = (DEPTH + 1) // 2
N_GDN = DEPTH // 2
CONV_W = 4
LRU_WIDTH = D_MODEL
LRU_BLOCKS = 4
LRU_BW = LRU_WIDTH // LRU_BLOCKS
LRU_C = 8.0
GDN_HEADS = 8
GDN_DK = 128
GDN_DV = 128
GDN_QK = GDN_HEADS * GDN_DK
GDN_VW = GDN_HEADS * GDN_DV
GDN_CONV_DIM = 2 * GDN_QK + GDN_VW
GDN_IN_DIM = GDN_CONV_DIM + GDN_VW + 2 * GDN_HEADS
GDN_CHUNK = 64
MEM_LEN = 256
XA_HEADS = 4
XA_HD = D_MODEL // XA_HEADS
D_FF = 3 * D_MODEL
N_EXPERTS = 8
TOP_K = 2
D_FF_EXPERT = D_FF // 2
DN_ALPHA = (2 * DEPTH) ** 0.25
DN_BETA = (8 * DEPTH) ** -0.25
LN_EPS = 1e-5
RMS_EPS = 1e-6

kernel_name = "hybrid_rglru_gdn_memxattn_decode_step"

def _layer_norm(x, g, b):
    xf = x.astype(jnp.float32)
    mu = jnp.mean(xf, axis=-1, keepdims=True)
    var = jnp.mean(jnp.square(xf - mu), axis=-1, keepdims=True)
    return ((xf - mu) * lax.rsqrt(var + LN_EPS) * g + b).astype(x.dtype)

def _causal_conv(x, buf, w, b=None):
    T = x.shape[1]
    xp = jnp.concatenate([buf.astype(x.dtype), x], axis=1)
    out = xp[:, 0:T] * w[0]
    for j in range(1, CONV_W):
        out = out + xp[:, j:j + T] * w[j]
    if b is not None:
        out = out + b
    return out, xp[:, T:]

def _rglru_mixer(x, h0, conv0, w_in, conv_w, conv_b, gate_w, gate_b, lam, w_out):
    B, T, _ = x.shape
    gu = x @ w_in
    gate_branch, rec = gu[..., :LRU_WIDTH], gu[..., LRU_WIDTH:]
    rec, conv_new = _causal_conv(rec, conv0, conv_w, conv_b)
    xb = rec.reshape(B, T, LRU_BLOCKS, LRU_BW)
    gates = (jnp.einsum('btnc,ncg->btng', xb, gate_w) + gate_b).astype(jnp.float32)
    r = jax.nn.sigmoid(gates[..., :LRU_BW]).reshape(B, T, LRU_WIDTH)
    i = jax.nn.sigmoid(gates[..., LRU_BW:]).reshape(B, T, LRU_WIDTH)
    log_a = -LRU_C * r * jax.nn.softplus(-lam.astype(jnp.float32))
    a = jnp.exp(log_a)
    mult = jnp.sqrt(-jnp.expm1(2.0 * log_a))
    bterm = mult * i * rec.astype(jnp.float32)
    bterm = bterm.at[:, 0].add(a[:, 0] * h0.astype(jnp.float32))

    def comb(left, right):
        a1, b1 = left
        a2, b2 = right
        return a1 * a2, a2 * b1 + b2

    _, h = lax.associative_scan(comb, (a, bterm), axis=1)
    y = h.astype(x.dtype) * jax.nn.gelu(gate_branch)
    return y @ w_out, h[:, -1].astype(h0.dtype), conv_new.astype(conv0.dtype)

def _l2norm(t):
    return t * lax.rsqrt(jnp.sum(t * t, axis=-1, keepdims=True) + RMS_EPS)

def _chunk_gated_delta(q, k, v, g, beta, s0):
    B, T, H, _ = q.shape
    C = min(GDN_CHUNK, T)
    pad = (-T) % C
    def pad_t(t):
        return jnp.pad(t, [(0, 0), (0, pad)] + [(0, 0)] * (t.ndim - 2))
    q, k, v, g, beta = pad_t(q), pad_t(k), pad_t(v), pad_t(g), pad_t(beta)
    N = (T + pad) // C
    q = q * (GDN_DK ** -0.5)
    def chunks4(t):
        return t.reshape(B, N, C, H, t.shape[-1]).transpose(1, 0, 3, 2, 4)
    def chunks3(t):
        return t.reshape(B, N, C, H).transpose(1, 0, 3, 2)
    q, k, v = chunks4(q), chunks4(k), chunks4(v)
    g, beta = chunks3(g), chunks3(beta)
    gc = jnp.cumsum(g, axis=-1)
    lower_incl = jnp.tril(jnp.ones((C, C), dtype=bool))
    strict_lower = jnp.tril(jnp.ones((C, C), dtype=bool), -1)
    decay = jnp.exp(jnp.where(lower_incl, gc[..., :, None] - gc[..., None, :], -jnp.inf))
    kb = k * beta[..., None]
    vb = v * beta[..., None]
    A = jnp.where(strict_lower, jnp.einsum('nbhid,nbhjd->nbhij', kb, k) * decay, 0.0)
    eye = jnp.eye(C, dtype=jnp.float32)
    Tinv = lax.linalg.triangular_solve(A + eye, jnp.broadcast_to(eye, A.shape),
                                       left_side=True, lower=True, unit_diagonal=True)
    u = Tinv @ vb
    w = Tinv @ (kb * jnp.exp(gc)[..., None])
    attn = jnp.where(lower_incl, jnp.einsum('nbhid,nbhjd->nbhij', q, k) * decay, 0.0)

    def step(S, inp):
        q_i, k_i, u_i, w_i, gc_i, attn_i = inp
        v_new = u_i - w_i @ S
        o = (q_i * jnp.exp(gc_i)[..., None]) @ S + attn_i @ v_new
        g_last = gc_i[..., -1]
        S = S * jnp.exp(g_last)[..., None, None] + jnp.einsum(
            'bhcd,bhce->bhde', k_i * jnp.exp(g_last[..., None] - gc_i)[..., None], v_new)
        return S, o

    S_fin, o = lax.scan(step, s0.astype(jnp.float32), (q, k, u, w, gc, attn))
    o = o.transpose(1, 0, 3, 2, 4).reshape(B, N * C, H, GDN_DV)[:, :T]
    return o, S_fin

def _gdn_mixer(x, s0, conv0, w_in, conv_w, a_log, dt_bias, norm_g, w_out):
    B, T, _ = x.shape
    proj = x @ w_in
    qkv = proj[..., :GDN_CONV_DIM]
    z = proj[..., GDN_CONV_DIM:GDN_CONV_DIM + GDN_VW]
    b_in = proj[..., GDN_CONV_DIM + GDN_VW:GDN_CONV_DIM + GDN_VW + GDN_HEADS]
    a_in = proj[..., GDN_CONV_DIM + GDN_VW + GDN_HEADS:]
    qkv, conv_new = _causal_conv(qkv, conv0, conv_w)
    qkv = jax.nn.silu(qkv).astype(jnp.float32)
    q = _l2norm(qkv[..., :GDN_QK].reshape(B, T, GDN_HEADS, GDN_DK))
    k = _l2norm(qkv[..., GDN_QK:2 * GDN_QK].reshape(B, T, GDN_HEADS, GDN_DK))
    v = qkv[..., 2 * GDN_QK:].reshape(B, T, GDN_HEADS, GDN_DV)
    beta = jax.nn.sigmoid(b_in.astype(jnp.float32))
    g = -jnp.exp(a_log.astype(jnp.float32)) * jax.nn.softplus(
        a_in.astype(jnp.float32) + dt_bias.astype(jnp.float32))
    o, s_new = _chunk_gated_delta(q, k, v, g, beta, s0)
    o = o * lax.rsqrt(jnp.mean(o * o, axis=-1, keepdims=True) + RMS_EPS) * norm_g
    o = o * jax.nn.silu(z.astype(jnp.float32).reshape(B, T, GDN_HEADS, GDN_DV))
    y = o.reshape(B, T, GDN_VW).astype(x.dtype) @ w_out
    return y, s_new.astype(s0.dtype), conv_new.astype(conv0.dtype)

def _mem_attention(x, mk, mv, wq, wo):
    B, T, _ = x.shape
    q = (x @ wq).reshape(B, T, XA_HEADS, XA_HD)
    s = jnp.einsum('bthd,bmhd->bhtm', q, mk.astype(x.dtype)).astype(jnp.float32) * (XA_HD ** -0.5)
    p = jax.nn.softmax(s, axis=-1).astype(x.dtype)
    o = jnp.einsum('bhtm,bmhd->bthd', p, mv.astype(x.dtype)).reshape(B, T, XA_HEADS * XA_HD)
    return o @ wo

def _swiglu(x, w_gu, w_down, f):
    gu = x @ w_gu
    return (jax.nn.silu(gu[..., :f]) * gu[..., f:]) @ w_down

def _moe_ffn(x, router, w_gu, w_down):
    logits = (x @ router).astype(jnp.float32)
    top_v, top_i = lax.top_k(logits, TOP_K)
    wts = jax.nn.softmax(top_v, axis=-1)
    gate = jnp.sum(jax.nn.one_hot(top_i, N_EXPERTS, dtype=jnp.float32) * wts[..., None], axis=-2)
    gate = gate.astype(x.dtype)
    y = jnp.zeros_like(x)
    for e in range(N_EXPERTS):
        y = y + gate[..., e:e + 1] * _swiglu(x, w_gu[e], w_down[e], D_FF_EXPERT)
    return y

def _trunk(x, mem_k, mem_v, lru_h, lru_conv, gdn_s, gdn_conv, p):
    new_h, new_lc, new_s, new_gc = [], [], [], []
    for i in range(DEPTH):
        j = i // N_MIXERS
        if i % N_MIXERS == 0:
            mix, h, c = _rglru_mixer(x, lru_h[j], lru_conv[j], p['lru_w_in'][j], p['lru_conv_w'][j],
                                     p['lru_conv_b'][j], p['lru_gate_w'][j], p['lru_gate_b'][j],
                                     p['lru_lambda'][j], p['lru_w_out'][j])
            new_h.append(h)
            new_lc.append(c)
        else:
            mix, s, c = _gdn_mixer(x, gdn_s[j], gdn_conv[j], p['gdn_w_in'][j], p['gdn_conv_w'][j],
                                   p['gdn_a_log'][j], p['gdn_dt_bias'][j], p['gdn_norm_g'][j],
                                   p['gdn_w_out'][j])
            new_s.append(s)
            new_gc.append(c)
        x = _layer_norm(DN_ALPHA * x + mix, p['ln_g'][i, 0], p['ln_b'][i, 0])
        xa = _mem_attention(x, mem_k[i], mem_v[i], p['xa_wq'][i], p['xa_wo'][i])
        x = _layer_norm(DN_ALPHA * x + xa, p['ln_g'][i, 1], p['ln_b'][i, 1])
        if i % 2 == 0:
            ff = _swiglu(x, p['ffn_w_gu'][j], p['ffn_w_down'][j], D_FF)
        else:
            ff = _moe_ffn(x, p['moe_router'][j], p['moe_w_gu'][j], p['moe_w_down'][j])
        x = _layer_norm(DN_ALPHA * x + ff, p['ln_g'][i, 2], p['ln_b'][i, 2])
    return x, jnp.stack(new_h), jnp.stack(new_lc), jnp.stack(new_s), jnp.stack(new_gc)

def setup_inputs(seed: int = 0) -> dict:
    key = jax.random.key(seed)
    ks = jax.random.split(key, 40)
    f32 = jnp.float32
    def nrm(k, shape, scale):
        return jax.random.normal(k, shape, f32) * scale

    x_prompt = nrm(ks[0], (BATCH, SEQ, D_MODEL), 1.0)
    x_sample = nrm(ks[1], (DEC_BATCH, DEC_SEQ, D_MODEL), 1.0)
    mem_prompt = nrm(ks[2], (BATCH, MEM_LEN, D_MODEL), 1.0)
    state_lru_h = nrm(ks[3], (N_LRU, DEC_BATCH, LRU_WIDTH), 0.5)
    state_lru_conv = nrm(ks[4], (N_LRU, DEC_BATCH, CONV_W - 1, LRU_WIDTH), 1.0)
    state_gdn_s = nrm(ks[5], (N_GDN, DEC_BATCH, GDN_HEADS, GDN_DK, GDN_DV), 0.05)
    state_gdn_conv = nrm(ks[6], (N_GDN, DEC_BATCH, CONV_W - 1, GDN_CONV_DIM), 1.0)
    cache_mem_k = nrm(ks[7], (DEPTH, DEC_BATCH, MEM_LEN, XA_HEADS, XA_HD), 1.0)
    cache_mem_v = nrm(ks[8], (DEPTH, DEC_BATCH, MEM_LEN, XA_HEADS, XA_HD), 1.0)

    ln_g = 1.0 + nrm(ks[9], (DEPTH, 3, D_MODEL), 0.02)
    ln_b = nrm(ks[10], (DEPTH, 3, D_MODEL), 0.02)
    xa_w = XA_HEADS * XA_HD
    xa_wq = nrm(ks[11], (DEPTH, D_MODEL, xa_w), D_MODEL ** -0.5)
    xa_wk = nrm(ks[12], (DEPTH, D_MODEL, xa_w), D_MODEL ** -0.5)
    xa_wv = nrm(ks[13], (DEPTH, D_MODEL, xa_w), DN_BETA * D_MODEL ** -0.5)
    xa_wo = nrm(ks[14], (DEPTH, xa_w, D_MODEL), DN_BETA * xa_w ** -0.5)

    lru_w_in = nrm(ks[15], (N_LRU, D_MODEL, 2 * LRU_WIDTH), D_MODEL ** -0.5)
    lru_conv_w = nrm(ks[16], (N_LRU, CONV_W, LRU_WIDTH), CONV_W ** -0.5)
    lru_conv_b = nrm(ks[17], (N_LRU, LRU_WIDTH), 0.01)
    lru_gate_w = nrm(ks[18], (N_LRU, LRU_BLOCKS, LRU_BW, 2 * LRU_BW), LRU_BW ** -0.5)
    lru_gate_b = nrm(ks[19], (N_LRU, LRU_BLOCKS, 2 * LRU_BW), 0.01)
    a_target = jax.random.uniform(ks[20], (N_LRU, LRU_WIDTH), f32, 0.9, 0.999)
    s_root = a_target ** (1.0 / LRU_C)
    lru_lambda = jnp.log(s_root) - jnp.log1p(-s_root)
    lru_w_out = nrm(ks[21], (N_LRU, LRU_WIDTH, D_MODEL), DN_BETA * LRU_WIDTH ** -0.5)

    gdn_w_in = nrm(ks[22], (N_GDN, D_MODEL, GDN_IN_DIM), D_MODEL ** -0.5)
    gdn_conv_w = nrm(ks[23], (N_GDN, CONV_W, GDN_CONV_DIM), CONV_W ** -0.5)
    gdn_a_log = jnp.log(jax.random.uniform(ks[24], (N_GDN, GDN_HEADS), f32, 1.0, 16.0))
    dt = jnp.exp(jax.random.uniform(ks[25], (N_GDN, GDN_HEADS), f32, math.log(1e-3), math.log(1e-1)))
    gdn_dt_bias = dt + jnp.log(-jnp.expm1(-dt))
    gdn_norm_g = 1.0 + nrm(ks[26], (N_GDN, GDN_DV), 0.02)
    gdn_w_out = nrm(ks[27], (N_GDN, GDN_VW, D_MODEL), DN_BETA * GDN_VW ** -0.5)

    ffn_w_gu = nrm(ks[28], (N_LRU, D_MODEL, 2 * D_FF), D_MODEL ** -0.5)
    ffn_w_down = nrm(ks[29], (N_LRU, D_FF, D_MODEL), DN_BETA * D_FF ** -0.5)
    moe_router = nrm(ks[30], (N_GDN, D_MODEL, N_EXPERTS), D_MODEL ** -0.5)
    moe_w_gu = nrm(ks[31], (N_GDN, N_EXPERTS, D_MODEL, 2 * D_FF_EXPERT), D_MODEL ** -0.5)
    moe_w_down = nrm(ks[32], (N_GDN, N_EXPERTS, D_FF_EXPERT, D_MODEL), DN_BETA * D_FF_EXPERT ** -0.5)

    return {"x_prompt": x_prompt, "x_sample": x_sample, "mem_prompt": mem_prompt,
            "state_lru_h": state_lru_h, "state_lru_conv": state_lru_conv,
            "state_gdn_s": state_gdn_s, "state_gdn_conv": state_gdn_conv,
            "cache_mem_k": cache_mem_k, "cache_mem_v": cache_mem_v,
            "ln_g": ln_g, "ln_b": ln_b,
            "xa_wq": xa_wq, "xa_wk": xa_wk, "xa_wv": xa_wv, "xa_wo": xa_wo,
            "lru_w_in": lru_w_in, "lru_conv_w": lru_conv_w, "lru_conv_b": lru_conv_b,
            "lru_gate_w": lru_gate_w, "lru_gate_b": lru_gate_b, "lru_lambda": lru_lambda,
            "lru_w_out": lru_w_out,
            "gdn_w_in": gdn_w_in, "gdn_conv_w": gdn_conv_w, "gdn_a_log": gdn_a_log,
            "gdn_dt_bias": gdn_dt_bias, "gdn_norm_g": gdn_norm_g, "gdn_w_out": gdn_w_out,
            "ffn_w_gu": ffn_w_gu, "ffn_w_down": ffn_w_down,
            "moe_router": moe_router, "moe_w_gu": moe_w_gu, "moe_w_down": moe_w_down}

def reference(x_prompt, x_sample, mem_prompt, state_lru_h, state_lru_conv, state_gdn_s, state_gdn_conv,
              cache_mem_k, cache_mem_v, ln_g, ln_b, xa_wq, xa_wk, xa_wv, xa_wo,
              lru_w_in, lru_conv_w, lru_conv_b, lru_gate_w, lru_gate_b, lru_lambda, lru_w_out,
              gdn_w_in, gdn_conv_w, gdn_a_log, gdn_dt_bias, gdn_norm_g, gdn_w_out,
              ffn_w_gu, ffn_w_down, moe_router, moe_w_gu, moe_w_down):
    p = dict(ln_g=ln_g, ln_b=ln_b, xa_wq=xa_wq, xa_wo=xa_wo,
             lru_w_in=lru_w_in, lru_conv_w=lru_conv_w, lru_conv_b=lru_conv_b, lru_gate_w=lru_gate_w,
             lru_gate_b=lru_gate_b, lru_lambda=lru_lambda, lru_w_out=lru_w_out,
             gdn_w_in=gdn_w_in, gdn_conv_w=gdn_conv_w, gdn_a_log=gdn_a_log, gdn_dt_bias=gdn_dt_bias,
             gdn_norm_g=gdn_norm_g, gdn_w_out=gdn_w_out,
             ffn_w_gu=ffn_w_gu, ffn_w_down=ffn_w_down,
             moe_router=moe_router, moe_w_gu=moe_w_gu, moe_w_down=moe_w_down)
    B = x_prompt.shape[0]
    mem_k_p = jnp.einsum('bmd,lde->lbme', mem_prompt, xa_wk).reshape(DEPTH, B, MEM_LEN, XA_HEADS, XA_HD)
    mem_v_p = jnp.einsum('bmd,lde->lbme', mem_prompt, xa_wv).reshape(DEPTH, B, MEM_LEN, XA_HEADS, XA_HD)
    h0 = jnp.zeros((N_LRU, B, LRU_WIDTH), state_lru_h.dtype)
    lc0 = jnp.zeros((N_LRU, B, CONV_W - 1, LRU_WIDTH), state_lru_conv.dtype)
    s0 = jnp.zeros((N_GDN, B, GDN_HEADS, GDN_DK, GDN_DV), state_gdn_s.dtype)
    gc0 = jnp.zeros((N_GDN, B, CONV_W - 1, GDN_CONV_DIM), state_gdn_conv.dtype)
    y_prompt, lru_h_p, lru_conv_p, gdn_s_p, gdn_conv_p = _trunk(
        x_prompt, mem_k_p, mem_v_p, h0, lc0, s0, gc0, p)
    y_sample, lru_h_s, lru_conv_s, gdn_s_s, gdn_conv_s = _trunk(
        x_sample, cache_mem_k, cache_mem_v, state_lru_h, state_lru_conv, state_gdn_s, state_gdn_conv, p)
    return (y_prompt, y_sample, lru_h_p, lru_conv_p, gdn_s_p, gdn_conv_p, mem_k_p, mem_v_p,
            lru_h_s, lru_conv_s, gdn_s_s, gdn_conv_s)


_drawn_inputs = setup_inputs


def setup_inputs(seed=0):
    import zlib

    import numpy as np

    out = dict(_drawn_inputs(seed))
    spreads = {}
    factors = {'lru_gate_b': 8.0, 'gdn_norm_g': 17.264}
    for name, (base, spread) in spreads.items():
        noise = np.random.default_rng([zlib.crc32(name.encode()), seed]).standard_normal(out[name].shape)
        drawn = base * np.exp(spread * noise) if base else spread * noise
        out[name] = __import__('jax').numpy.asarray(drawn.astype(out[name].dtype))
    for name, factor in factors.items():
        out[name] = (out[name] * factor).astype(out[name].dtype)
    return out
```

```python
import concourse.bass as bass
from concourse import mybir
from contextlib import ExitStack

P = 128
D, KT = 1024, 8
TP, NB, TS = 512, 8, 4
NS = NB * TS
T = TP + NS
HT = T // 2
CW, HIST = 4, 3
EXTP = HIST + TP
SEG = HIST + TS
EXT = EXTP + NB * SEG
CONV = EXT - HIST
NL, NLN = 2, 6
XH, XD, MEM, MT = 4, 256, 256, 2
GH, C, NC = 8, 128, 4
NT = NC + 1
NE, FF, FT = 8, 1536, 12
HALVES = 2
KV_EARLY = 3
LEVELS = 7
SLEVELS = 2
BLK = 4
ALPHA = float((2 * NL) ** 0.25)
LRU_C = 8.0
RAW, SPLIT = 4, 2
SLOTS = 16 + 8 + 4 * 8 + HALVES * 36 + GH * 4 + 8 + 4 * 8 + NE * 36
NEG = -1.0e30

_COLS = [("lcw", 8 * 4), ("lcb", 8), ("lgb", 16), ("lam", 8), ("h0", 64), ("lhist", 192),
         ("lng", 48), ("lnb", 48), ("gcw", 96), ("ng", 1), ("router", 64), ("wba", 128),
         ("dtb", 1), ("alog", 1), ("eps5", 1), ("eps6", 1), ("iota", 8)]
PO, _n = {}, 0
for _name, _w in _COLS:
    PO[_name] = (_n, _n + _w)
    _n += _w
NPAR = _n
_TABS = [("ident", 128), ("ones", 128), ("mincl", 128), ("levels", LEVELS * 128), ("smincl", 32), ("smask", NB)]
TO, _n = {}, 0
for _name, _w in _TABS:
    TO[_name] = (_n, _n + _w)
    _n += _w
NTAB = _n


class Serial:

    def __init__(self, eng, sem):
        self.eng, self.sem, self.base, self.k, self.total = eng, sem, 0, 0, 0

    def __call__(self, ins, sem=None, val=None):
        if sem is None:
            self.k += 1
            self.total += 1
            ins.then_inc(self.sem, 1)
            self.eng.wait_ge(self.sem, self.base + self.k)
        else:
            ins.then_inc(sem, 1)
            self.eng.wait_ge(sem, val)


def repeat(eng, n, body, chain=None, inner=None):
    if chain is None:
        body(0)
        if n > 1:
            with eng.Fori(1, n) as i:
                body(i)
        return
    start, before = chain.base + chain.k, chain.total
    chain.base, chain.k = start, 0
    body(0)
    length = chain.total - before
    if inner is not None:
        eng.sem_inc(inner, 1)
    if n > 1:
        with eng.Fori(1, n) as i:
            chain.base, chain.k = start + i * length, 0
            body(i)
    chain.base, chain.k, chain.total = start + n * length, 0, before + n * length


def ge(eng, sem, val):
    if isinstance(val, int) and val <= 0:
        return
    eng.wait_ge(sem, val)


def trunk(nc, I, O):
    F, R = mybir.dt.float32, mybir.dt.float32r
    ALU, ACT, AX = mybir.AluOpType, mybir.ActivationFunctionType, mybir.AxisListType
    MUL, ADD, SUB = ALU.mult, ALU.add, ALU.subtract
    ds = bass.ds

    with ExitStack() as ctx:
        def sb(name, shape, dt=F):
            return ctx.enter_context(nc.sbuf_tensor(name, shape, dt))

        def sem(name):
            return ctx.enter_context(nc.semaphore(name))

        x = sb("x", [P, KT, T])
        xh = sb("xh", [P, KT, T], R)
        xl = sb("xl", [P, KT, T], R)
        raw = sb("raw", [P, RAW, KT, P])
        wh = sb("wh", [P, SPLIT, KT, P], R)
        wl = sb("wl", [P, SPLIT, KT, P], R)
        par = sb("par", [P, NPAR])
        tab = sb("tab", [P, NTAB])
        hh = sb("hh", [P, FT, T], R)
        hl = sb("hl", [P, FT, T], R)
        WORK = 15200
        work = sb("work", [P, WORK])
        lnsq = sb("lnsq", [P, 2, T])
        lnr = sb("lnr", [P, T])
        ps = ctx.enter_context(nc.psum_tensor("ps", [P, 8, 512], F))

        def carve():
            at = [0]

            def take(*shape):
                n = 1
                for s in shape:
                    n *= s
                v = work[:, at[0]:at[0] + n]
                at[0] += n
                assert at[0] <= WORK, at[0]
                if len(shape) == 2:
                    v = v.rearrange("p (a b) -> p a b", b=shape[1])
                if len(shape) == 3:
                    v = v.rearrange("p (a b c) -> p a b c", b=shape[1], c=shape[2])
                return v
            return take

        def pc(name, a=0, b=None):
            lo, hi = PO[name]
            return par[:, lo + a:(hi if b is None else lo + b)]

        def tc(name, a=0, b=None):
            lo, hi = TO[name]
            return tab[:, lo + a:(hi if b is None else lo + b)]

        ident, ones = tc("ident"), tc("ones")

        def pair(i):
            return ps[:, 2 * i:2 * i + 2, 0:HT]

        def two(v):
            return v.rearrange("p (h c) -> p h c", h=2)

        w_in = [sem(f"w_in{j}") for j in range(RAW)]
        w_split = sem("w_split")
        w_used = sem("w_used")
        dve_chain, act_chain = sem("dve_chain"), sem("act_chain")
        pool_hi = sem("pool_hi")
        passed = sem("passed")
        ld_x, ld_par, ld_tab = sem("ld_x"), sem("ld_par"), sem("ld_tab")
        x_split_h, x_split_l = sem("x_split_h"), sem("x_split_l")
        out_done = sem("out_done")
        lw, lru_gw_in = None, sem("lru_gw_in")
        lru_ext, lru_conv = sem("lru_ext"), sem("lru_conv")
        lru_gate_full, lru_gate_ev = sem("lru_gate_full"), sem("lru_gate_ev")
        lru_gelu, lru_act, lru_dve, lru_y, lru_yh = (sem("lru_gelu"), sem("lru_act"), sem("lru_dve"),
                                                     sem("lru_y"), sem("lru_yh"))
        lru_sp, lru_spe, lru_cst = sem("lru_sp"), sem("lru_spe"), sem("lru_cst")
        z_ready = sem("z_ready")
        ln_sum, ln_d, ln_sq, ln_var, ln_std, ln_n, ln_x, ln_xh, ln_xl = (
            sem("ln_sum"), sem("ln_d"), sem("ln_sq"), sem("ln_var"), sem("ln_std"), sem("ln_n"),
            sem("ln_x"), sem("ln_xh"), sem("ln_xl"))
        mem_in, kv_ev = sem("mem_in"), sem("kv_ev")
        ring_free = sem("ring_free")
        q_ev, c_in, c_used = sem("q_ev"), [sem("c_in0"), sem("c_in1")], sem("c_used")
        ss_full, ss_ev, ss_tr, ss_max, ss_exp, ss_p, ss_ptr, ss_pt, ss_o, ss_oh, ss_ol = (
            sem("ss_full"), sem("ss_ev"), sem("ss_tr"), sem("ss_max"), sem("ss_exp"), sem("ss_p"),
            sem("ss_ptr"), sem("ss_pt"), sem("ss_o"), sem("ss_oh"), sem("ss_ol"))
        pa_s, pa_max, pa_exp, pa_p, pa_tr, pa_pt, pa_o, pa_oh, pa_ol = (
            sem("pa_s"), sem("pa_max"), sem("pa_exp"), sem("pa_p"), sem("pa_tr"), sem("pa_pt"),
            sem("pa_o"), sem("pa_oh"), sem("pa_ol"))
        f_silu, f_h, f_hh, f_hl, f_y = sem("f_silu"), sem("f_h"), sem("f_hh"), sem("f_hl"), sem("f_y")
        r_log, r_gate, r_tr, r_row, r_st, r_exp, g_in = (sem("r_log"), sem("r_gate"), sem("r_tr"), sem("r_row"),
                                                         sem("r_st"), sem("r_exp"), sem("g_in"))
        r_d = sem("r_d")
        b_mm, b_beta, b_x, b_e, b_g, b_eg, b_rows, b_st, b_tr, b_col = (
            sem("b_mm"), sem("b_beta"), sem("b_x"), sem("b_e"), sem("b_g"), sem("b_eg"), sem("b_rows"),
            sem("b_st"), sem("b_tr"), sem("b_col"))
        d_row, d_hist, d_s0, d_ext, d_z, d_conv, d_silu, d_cst, d_cso = (
            sem("d_row"), sem("d_hist"), sem("d_s0"), sem("d_ext"), sem("d_z"), sem("d_conv"), sem("d_silu"),
            sem("d_cst"), sem("d_cso"))
        d_sq, d_ss, d_std, d_qk, d_tm, d_tme, d_qg, d_egr = (sem("d_sq"), sem("d_ss"), sem("d_std"), sem("d_qk"),
                                                      sem("d_tm"), sem("d_tme"), sem("d_qg"), sem("d_egr"))
        d_at, d_tt, d_uu = sem("d_at"), sem("d_tt"), sem("d_uu")
        d_kk, d_arg, d_dt, d_b, d_bl, d_pt, d_pte, d_ut, d_ute, d_wt, d_wte = (
            sem("d_kk"), sem("d_arg"), sem("d_dt"), sem("d_b"), sem("d_bl"), sem("d_pt"), sem("d_pte"),
            sem("d_ut"), sem("d_ute"), sem("d_wt"), sem("d_wte"))
        d_vn, d_vne, d_o, d_s, d_oe = sem("d_vn"), sem("d_vne"), sem("d_o"), sem("d_s"), sem("d_oe")
        d_svt, d_svte, d_svn, d_svne, d_so, d_sds, d_ssn, d_kdm = (
            sem("d_svt"), sem("d_svte"), sem("d_svn"), sem("d_svne"), sem("d_so"), sem("d_sds"), sem("d_ssn"),
            sem("d_kdm"))
        d_osq, d_oss, d_ostd, d_on, d_yh, d_yl, d_sout = (
            sem("d_osq"), sem("d_oss"), sem("d_ostd"), sem("d_on"), sem("d_yh"), sem("d_yl"), sem("d_sout"))

        S_LRU = 0
        S_LOUT = S_LRU + 16
        S_KV = [S_LOUT + 8, None]
        S_Q = [S_KV[0] + 16, None]
        S_O = [S_Q[0] + 8, None]
        S_FFN = S_O[0] + 8
        S_GDN = S_FFN + HALVES * 36
        S_GOUT = S_GDN + 4 * GH
        S_KV[1] = S_GOUT + 8
        S_Q[1] = S_KV[1] + 16
        S_O[1] = S_Q[1] + 8
        S_MOE = S_O[1] + 8
        assert S_MOE + NE * 36 == SLOTS

        tk = carve()
        L_ext, L_rec, L_acc = tk(2, EXT), tk(2, T), tk(CONV)
        L_gw = tk(KT, P)
        L_r, L_i, L_gel = tk(2, T), tk(2, T), tk(2, T)
        L_a, L_t, L_b = tk(T), tk(T), tk(T)
        L_par, L_h0, L_hist = tk(2, 6), tk(2, NB), tk(2, NB * HIST)
        L_sp = tk(6, KT)
        L_cst, L_hst = tk(KT, HIST + NB * HIST), tk(KT, 1 + NB)

        tk = carve()
        A_q, A_k, A_v = tk(KT, T), tk(KT, MEM), tk(MT, D)
        A_ring = tk(2, 2048)
        A_mem = tk(KT, MEM)
        A_p = A_mem.rearrange("p a b -> p (a b)")[:, 0:4 * MEM].rearrange("p (a b) -> p a b", b=MEM)
        A_pt = A_mem.rearrange("p a b -> p (a b)")[:, 4 * MEM:].rearrange("p (a b) -> p a b", b=TP)
        A_ss, A_sp = tk(MT * P), tk(MT * P)
        A_spt = A_ss
        A_nm, A_rs = tk(4), tk(4)
        A_snm, A_srs = tk(1), tk(1)

        tk = carve()
        F_s, F_h, F_g = tk(2, T), tk(2, T), tk(T)
        R_l, R_m = tk(NT, 8), tk(NT, 8)
        R_i = tk(NT, 8).bitcast(mybir.dt.uint32)
        R_f, R_w, R_g, R_o, R_row = tk(NT, 8), tk(NT, 2), tk(NT, 8), tk(NT, 8), tk(T)

        tk = carve()
        G_ext, G_acc = tk(3, EXT), tk(EXT)
        G_qkv, G_z = tk(3, T), tk(T)
        G_gc, G_be, G_eg = tk(T), tk(T), tk(T)
        G_sq = G_acc[:, 0:T]
        G_rs = tk(2, T)
        G_vb, G_kb, G_kd = tk(NT, P), tk(NT, P), tk(NT, P)
        G_dt, G_at, G_bl, G_u, G_t = tk(NC, P), tk(NC, P), tk(2, NC, P), tk(NC, P), tk(NC, P)
        G_sdt, G_sat, G_sbl, G_su, G_st, G_spt, G_swt = (tk(NS), tk(NS), tk(NS), tk(NS), tk(NS), tk(NS), tk(NS))
        G_vn, G_s = tk(2, P), tk(2, P)
        G_svt, G_svn = tk(NS), tk(P)
        G_s0 = tk(NB, P)
        G_kdm = G_bl.rearrange("p a b c -> p (a b) c")
        G_hist, G_cst, G_hc, G_cw = tk(3, NB * HIST), tk(3, HIST + NB * HIST), tk(NT, 4), tk(3, CW)
        G_cols = tk(NT, 4, GH)
        G_pt = G_qkv[:, 2, 0:TP].rearrange("p (a b) -> p a b", b=P)
        G_wt = G_qkv[:, 1, 0:TP].rearrange("p (a b) -> p a b", b=P)
        G_ot = G_qkv[:, 0, :]
        tk = carve()
        B_r = [tk(T) for _ in range(10)]

        nc_block = ctx.enter_context(nc.Block())

        @nc_block.sync
        def _(sp):
            sp.dma_start(x[:, :, :], I["xT"]).then_inc(ld_x, 16)

            def load(t, offset):
                for j in range(RAW):
                    if offset is None:
                        ge(sp, w_used, t * RAW + (j + 1 - RAW))
                    else:
                        ge(sp, w_split, t * RAW + (j + 1 - RAW - offset))
                    sp.dma_start(raw[:, j:j + 1, :, :], I["weights"][ds(t * RAW + j, 1)].rearrange(
                        "o p (k c) -> p o k c", k=KT)).then_inc(w_in[j], 16)

            def turns(slot, n, before, own):
                t0 = slot // RAW
                load(t0, before)
                if n > RAW:
                    with sp.Fori(t0 + 1, t0 + n // RAW) as t:
                        load(t, own)

            def cache(l):
                for i in range(2 * NB):
                    b = i % 2
                    if i < 2:
                        sp.wait_ge(ring_free, l + 1)
                    else:
                        sp.wait_ge(c_used, 2 * NB * l + i - 1)
                    sp.dma_start(A_ring[:, b, :], I["cache"][l, i]).then_inc(c_in[b], 16)

            for l in range(NL):
                d0, d1 = 16 * l, 16 * (l + 1)
                if l == 0:
                    turns(0, S_KV[0], 0, 0)
                else:
                    turns(S_FFN, S_KV[1] - S_FFN, d0, d0)
                turns(S_KV[l], 16, d0, None)
                turns(S_Q[l], 8, None, d1)
                turns(S_O[l], RAW, d1, d1)
                cache(l)
                turns(S_O[l] + RAW, RAW, d1, d1)
            turns(S_MOE, NE * 36, 32, 32)
            sp.wait_ge(out_done, 16 * N_OUT)

        @nc_block.gpsimd
        def _(pool):
            pool.wait_ge(ld_tab, 16)
            one_col = tc("ones", 0, 1).to_broadcast((P, KT * P))

            def split(t, first, offset):
                for j in range(RAW):
                    pool.wait_ge(w_in[j], t * 16 + 16)
                    ge(pool, w_used, t * RAW + (j + 1 - SPLIT - (first if j < SPLIT else 0)))
                    h1, l1, r1 = wh[:, j % SPLIT], wl[:, j % SPLIT], raw[:, j]
                    flat = lambda v: v.rearrange("p a b -> p (a b)")
                    nc.gpsimd.tensor_tensor(flat(h1), flat(r1), one_col, MUL).then_inc(pool_hi, 1)
                    pool.wait_ge(pool_hi, t * RAW + (j + 1 - offset))
                    nc.gpsimd.tensor_tensor(flat(l1), flat(r1), flat(h1).bitcast(F), SUB).then_inc(w_split, 1)

            def turns(slot, n, first, offset):
                t0 = slot // RAW
                split(t0, first, offset)
                if n > RAW:
                    with pool.Fori(t0 + 1, t0 + n // RAW) as t:
                        split(t, 0, offset)
            turns(0, S_KV[0], 0, 0)
            turns(S_Q[0], S_KV[1] - S_Q[0], 16, 16)
            turns(S_Q[1], SLOTS - S_Q[1], 16, 32)

        @nc_block.tensor
        def _(pe):
            mm = nc.tensor.matmul

            def lin_steps(slot, direct, par_, i, ah, al, fresh=None, per=6):
                pe.wait_ge(w_split, slot + (1 - direct))
                c = 0
                for n, (w, a) in enumerate(((wh, ah), (wl, ah), (wh, al))):
                    for k in range(KT):
                        if fresh is not None and n != 1:
                            pe.wait_ge(ln_xh if n == 0 else ln_xl, fresh + k + 1)
                        for h in range(2):
                            last = mm(ps[:, 2 * i + h, 0:HT], w[:, par_, k, :], a[:, k, h * HT:(h + 1) * HT],
                                      start=(n == 0 and k == 0), stop=(n == 2 and k == KT - 1))
                            c += 1
                            if c == 6 * KT:
                                last.then_inc(w_used, 1)
                            if c % per == 0:
                                yield

            def lin_tile(*args, **more):
                for _ in lin_steps(*args, **more):
                    pass

            def linear(slot, direct, ah, al, freed, base, fresh=None):
                for s in range(8):
                    if s >= 2:
                        pe.wait_ge(freed, base + s - 1)
                    lin_tile(slot + s, direct, s % 2, s % 2, ah, al, fresh=fresh if s == 0 else None)

            def layer_norm(n, l=None):
                for k in range(KT):
                    pe.wait_ge(z_ready, n * KT + k + 1)
                    for h in range(2):
                        last = mm(ps[:, 4 + h, 0:HT], ones, x[:, k, h * HT:(h + 1) * HT], start=(k == 0), stop=(k == KT - 1))
                last.then_inc(ln_sum, 1)
                if l is not None:
                    kv(l, 0, KV_EARLY)
                for k in range(KT):
                    pe.wait_ge(ln_sq, n * KT + k + 1)
                    for h in range(2):
                        last = mm(ps[:, 6 + h, 0:HT], ones, lnsq[:, k % 2, h * HT:(h + 1) * HT],
                                  start=(k == 0), stop=(k == KT - 1))
                    last.then_inc(ln_var, 1)
                if l is not None:
                    kv(l, KV_EARLY, 16)

            def kv(l, lo, hi):
                if lo == 0:
                    pe.wait_ge(mem_in, 16 * (l + 1))
                for s in range(lo, hi):
                    if s >= 2:
                        pe.wait_ge(kv_ev, 16 * l + s - 1)
                    slot = S_KV[l] + s
                    pe.wait_ge(w_in[slot % RAW], 16 * (slot // RAW + 1))
                    b, q = 2 * (s % 2), slot % RAW
                    if s < 8:
                        for k in range(KT):
                            last = mm(ps[:, b, 0:MEM], raw[:, q, k, :], A_mem[:, k, :], start=(k == 0), stop=(k == KT - 1))
                    else:
                        for mt in range(MT):
                            for k in range(KT):
                                last = mm(ps[:, b, mt * P:(mt + 1) * P], A_mem[:, k, mt * P:(mt + 1) * P], raw[:, q, k, :],
                                          start=(k == 0), stop=(k == KT - 1))
                    last.then_inc(w_used, 1)

            def attention(l):
                pe.wait_ge(kv_ev, 16 * (l + 1))
                linear(S_Q[l], 16 * (l + 1), xh, xl, q_ev, 8 * l, fresh=KT * 3 * l)
                pe.wait_ge(q_ev, 8 * (l + 1))

                def scores(b):
                    n = 2 * NB * l + b
                    pe.wait_ge(c_in[b % 2], (n // 2 + 1) * 16)
                    for mt in range(MT):
                        for h in range(XH):
                            for kk in range(2):
                                o = mt * P + h * NS + b * TS
                                last = mm(ps[:, 2, o:o + TS],
                                          A_ring[:, b % 2, (2 * h + kk) * MEM + mt * P:(2 * h + kk) * MEM + (mt + 1) * P],
                                          A_q[:, 2 * h + kk, TP + b * TS:TP + (b + 1) * TS],
                                          start=(kk == 0), stop=(kk == 1))
                    last.then_inc(c_used, 1)

                def values(b):
                    n = 2 * NB * l + NB + b
                    pe.wait_ge(c_in[b % 2], (n // 2 + 1) * 16)
                    for dt in range(KT):
                        for mt in range(MT):
                            o = mt * P + (dt // 2) * NS + b * TS
                            last = mm(ps[:, 3, dt * NS + b * TS:dt * NS + (b + 1) * TS],
                                      A_ring[:, b % 2, mt * D + dt * P:mt * D + (dt + 1) * P],
                                      A_spt[:, o:o + TS], start=(mt == 0), stop=(mt == MT - 1))
                    last.then_inc(c_used, 1)

                for h in range(XH):
                    n = XH * l + h
                    one_seq = scores if h < 2 else values
                    if h:
                        pe.wait_ge(pa_exp, 4 * n)
                    for tt in range(4):
                        for kk in range(2):
                            last = mm(ps[:, 4 + tt // 2, (tt % 2) * MEM:(tt % 2 + 1) * MEM],
                                      A_q[:, 2 * h + kk, tt * P:(tt + 1) * P], A_k[:, 2 * h + kk, :],
                                      start=(kk == 0), stop=(kk == 1))
                    last.then_inc(pa_s, 1)
                    if h == 2:
                        pe.wait_ge(ss_ev, l + 1)
                        for mt in range(MT):
                            last = nc.tensor.transpose(ps[:, 3, mt * P:(mt + 1) * P], A_ss[:, mt * P:(mt + 1) * P], ident)
                        last.then_inc(ss_tr, 1)
                    else:
                        for b in range(2):
                            one_seq(4 * (h % 2) + b)
                    pe.wait_ge(pa_p, n + 1)
                    for tt in range(4):
                        for mt in range(MT):
                            last = nc.tensor.transpose(ps[:, 6 + mt, tt * P:(tt + 1) * P], A_p[:, tt, mt * P:(mt + 1) * P], ident)
                    last.then_inc(pa_tr, 1)
                    if h == 2:
                        pe.wait_ge(ss_p, l + 1)
                        for mt in range(MT):
                            last = nc.tensor.transpose(ps[:, 2, mt * P:(mt + 1) * P], A_sp[:, mt * P:(mt + 1) * P], ident)
                        last.then_inc(ss_ptr, 1)
                        pe.wait_ge(ss_pt, l + 1)
                        for b in range(4):
                            values(b)
                    else:
                        for b in range(2, 4):
                            one_seq(4 * (h % 2) + b)
                    pe.wait_ge(pa_pt, n + 1)
                    if h:
                        pe.wait_ge(pa_ol, n)
                    for dt in range(2):
                        for mt in range(MT):
                            last = mm(ps[:, dt, :], A_v[:, mt, (2 * h + dt) * P:(2 * h + dt + 1) * P], A_pt[:, mt, :],
                                      start=(mt == 0), stop=(mt == MT - 1))
                    last.then_inc(pa_o, 1)
                pe.wait_ge(ss_ol, l + 1)
                pe.wait_ge(pa_ol, XH * (l + 1))
                linear(S_O[l], 16 * (l + 1), xh, xl, z_ready, KT * (3 * l + 1))

            def experts(n, slot, direct, e0, first_ln):
                def one(e):
                    e36, e12, e8 = e * 36 + slot, (e + e0) * FT, (e + e0) * KT

                    def up(g):
                        for j in range(4):
                            if j % 2 == 0:
                                ge(pe, f_h, e12 + g * 2 + (j // 2 - 1))
                            lin_tile(e36 + g * 4 + j, direct, j % 2, j, xh, xl,
                                     fresh=KT * (first_ln - 1) if j == 0 and isinstance(g, int) and isinstance(e, int) else None)
                    ge(pe, f_y, e8)
                    pe.sem_inc(passed, 1)
                    if isinstance(e, int) and e == 0:
                        up(0)
                        with pe.Fori(1, FT // 2) as g:
                            up(g)
                    else:
                        with pe.Fori(0, FT // 2) as g:
                            up(g)
                    pe.wait_ge(f_hl, e12 + FT)

                    def down(g):
                        for q in range(4 * FT):
                            d, f = divmod(q, FT)
                            s, k = divmod(q, KT)
                            if k == 0:
                                pe.wait_ge(w_split, e36 + g * 6 + (24 + s + 1 - direct))
                            if f == 0:
                                ge(pe, f_y, e8 + g * 4 + (d - 3))
                            w_parts = ((wh, hh), (wh, hl), (wl, hh))
                            for m, (w, a) in enumerate(w_parts):
                                for h in range(2):
                                    last = mm(ps[:, 2 * d + h, 0:HT], w[:, s % 2, k, :], a[:, f, h * HT:(h + 1) * HT],
                                              start=(f == 0 and m == 0), stop=(f == FT - 1 and m == 2))
                            if k == KT - 1:
                                last.then_inc(w_used, 1)
                    pe.sem_inc(passed, 1)
                    if isinstance(e, int) and e + e0 == 0:
                        down(0)
                        down(1)
                    else:
                        with pe.Fori(0, 2) as g:
                            down(g)
                repeat(pe, n, one)

            pe.wait_ge(x_split_l, 1)

            def lru(b):
                for j in range(2):
                    ge(pe, lru_gelu, b * 2 + (j - 1))
                    lin_tile(b * 4 + j, 0, j, j, xh, xl)
                for j in range(2):
                    pe.wait_ge(lru_ext, b * 2 + (j + 1))
                    lin_tile(b * 4 + (2 + j), 0, j, j, xh, xl)
                pe.wait_ge(lru_gw_in, b * 16 + 16)
                pe.wait_ge(lru_conv, b * 2 + 2)
                for g in range(4):
                    ge(pe, lru_gate_ev, b * 4 + (g - 1))
                    for k in range(2):
                        for h in range(2):
                            last = mm(ps[:, 4 + 2 * (g % 2) + h, 0:HT], L_gw[:, 4 * k + g, :],
                                      L_rec[:, k, h * HT:(h + 1) * HT], start=(k == 0), stop=(k == 1))
                    last.then_inc(lru_gate_full, 1)
            repeat(pe, BLK, lru)
            pe.wait_ge(lru_y, 8)
            pe.wait_ge(lru_gelu, 8)
            linear(S_LOUT, 0, hh, hl, z_ready, 0)
            layer_norm(0, 0)
            attention(0)
            layer_norm(1)
            experts(HALVES, S_FFN, 16, 0, 2)
            pe.wait_ge(f_y, KT * HALVES)
            layer_norm(2)
            pe.wait_ge(ln_xl, KT * 3)
            for g in range(2):
                for k in range(KT):
                    for h in range(2):
                        last = mm(ps[0:GH, 4 + 2 * g + h, 0:HT], pc("wba", 16 * k + 8 * g, 16 * k + 8 * g + 8),
                                  x[:, k, h * HT:(h + 1) * HT], start=(k == 0), stop=(k == KT - 1))
            last.then_inc(b_mm, 1)
            pe.wait_ge(b_rows, 1)
            for tt in range(NT):
                n = P if tt < NC else NS
                for r in range(4):
                    last = nc.tensor.transpose(ps[0:n, 4, (tt * 4 + r) * GH:(tt * 4 + r + 1) * GH],
                                               B_r[r][0:GH, tt * P:tt * P + n], ident[0:GH, 0:GH])
            last.then_inc(b_tr, 1)
            pe.wait_ge(b_col, 2)

            def project(h, per=6):
                for j in range(4):
                    if j == 0:
                        ge(pe, d_ext, h * 3)
                    elif j == 1:
                        ge(pe, d_z, h)
                    else:
                        pe.wait_ge(d_ext, h * 3 + (j - 1))
                    yield from lin_steps(h * 4 + (S_GDN + j), 16, j % 2, j % 2, xh, xl, per=per)

            def head(h, ahead=True):
                following = project(h + 1) if ahead else iter(())

                def fill(n):
                    for _ in range(n):
                        next(following, None)

                for j in range(2):
                    pe.wait_ge(d_sq, h * 2 + (j + 1))
                    if j == 0:
                        ge(pe, d_ssn, h)
                        ge(pe, d_ostd, h)
                    for hf in range(2):
                        last = mm(ps[:, 4 + 2 * j + hf, 0:HT], ones, G_rs[:, j, hf * HT:(hf + 1) * HT], start=True, stop=True)
                    last.then_inc(d_ss, 1)
                pe.wait_ge(d_silu, h * 3 + 3)
                pe.wait_ge(d_qk, h * 2 + 2)
                for j in range(2):
                    for c in range(NC):
                        nc.tensor.transpose(ps[:, 4 + 2 * j, c * P:(c + 1) * P], G_qkv[:, 1 + j, c * P:(c + 1) * P], ident)
                    last = nc.tensor.transpose(ps[0:NS, 5 + 2 * j, 0:P], G_qkv[:, 1 + j, TP:T], ident)
                    last.then_inc(d_tm, 1)
                for j in range(2):
                    pe.wait_ge(d_tme, h * 2 + (j + 1))
                    for c in range(NC):
                        mm(ps[:, 4 + 2 * j, c * P:(c + 1) * P], G_qkv[:, 1, c * P:(c + 1) * P],
                           G_qkv[:, 1 - j, c * P:(c + 1) * P], start=True, stop=True)
                    last = mm(ps[0:NS, 5 + 2 * j, 0:NS], G_qkv[:, 1, TP:T], G_qkv[:, 1 - j, TP:T], start=True, stop=True)
                    last.then_inc(d_kk, 1)
                pe.wait_ge(d_bl, h * LEVELS + 1)
                pe.wait_ge(d_at, h + 1)
                for c in range(NC):
                    nc.tensor.transpose(ps[:, 5, c * P:(c + 1) * P], G_bl[:, 0, c, :], ident)
                nc.tensor.transpose(ps[0:NS, 7, 0:NS], G_sbl[0:NS, :], ident[0:NS, 0:NS]).then_inc(d_pt, 1)
                fill(2)
                for v in range(1, LEVELS):
                    small = v < SLEVELS
                    pe.wait_ge(d_bl, h * LEVELS + (v + 1))
                    pe.wait_ge(d_tt, h * (LEVELS - 1) + v)
                    for c in range(NC):
                        last = mm(ps[:, 4, c * P:(c + 1) * P], G_bl[:, v % 2, c, :], G_t[:, c, :], start=True, stop=True)
                    if small:
                        last = mm(ps[0:NS, 7, 0:NS], G_sbl[0:NS, :], G_st[0:NS, :], start=True, stop=True)
                    last.then_inc(d_pt, 1)
                    fill(2)
                    pe.wait_ge(d_pte, h * (LEVELS - 1) + v)
                    pe.wait_ge(d_ute, h * LEVELS + v)
                    if v < LEVELS - 1:
                        for c in range(NC):
                            last = mm(ps[:, 5, c * P:(c + 1) * P], G_u[:, c, :], G_pt[:, c, :], start=True, stop=True)
                        last.then_inc(d_ut, 1)
                    for c in range(NC):
                        last = mm(ps[:, 6, c * P:(c + 1) * P], G_pt[:, c, :], G_u[:, c, :], start=True, stop=True)
                    if small:
                        last = mm(ps[0:NS, 7, 32:32 + NS], G_spt[0:NS, :], G_su[0:NS, :], start=True, stop=True)
                    last.then_inc(d_uu, 1)
                    fill(2)
                pe.wait_ge(d_ute, h * LEVELS + LEVELS)
                for c in range(NC):
                    mm(ps[:, 4, c * P:(c + 1) * P], G_kb[:, c, :], G_u[:, c, :], start=True, stop=True)
                last = mm(ps[:, 5, 0:NS], G_kb[0:NS, NC, :], G_su[0:NS, :], start=True, stop=True)
                last.then_inc(d_wt, 1)
                fill(2)
                pe.wait_ge(d_wte, h + 1)
                pe.wait_ge(d_qg, h + 1)
                for c in range(NC):
                    if c:
                        pe.wait_ge(d_s, h * NC + c)
                    last = mm(ps[:, 6, c * P:(c + 1) * P], G_u[:, c, :], G_vb[:, c, :], start=True, stop=(c == 0))
                    if c:
                        last = mm(ps[:, 6, c * P:(c + 1) * P], G_wt[:, c, :], G_s[:, (c + 1) % 2, :], start=False, stop=True)
                    last.then_inc(d_vn, 1)
                    fill(1)
                    pe.wait_ge(d_vne, h * NC + (c + 1))
                    last = mm(ps[:, 4, c * P:(c + 1) * P], G_kd[:, c, :], G_vn[:, c % 2, :], start=True, stop=True)
                    last.then_inc(d_o, 1)
                    mm(ps[:, 7, c * P:(c + 1) * P], G_vn[:, c % 2, :], G_at[:, c, :], start=True, stop=(c == 0))
                    if c:
                        mm(ps[:, 7, c * P:(c + 1) * P], G_s[:, (c + 1) % 2, :], G_gc[:, c * P:(c + 1) * P], start=False, stop=True)
                fill(100)
                pe.wait_ge(d_s0, h * 16 + 16)
                for b in range(NB):
                    mm(ps[:, 5, 64 + b * TS:64 + (b + 1) * TS], G_s0[:, b, :], G_swt[:, b * TS:(b + 1) * TS],
                       start=(b == 0), stop=False)
                last = mm(ps[:, 5, 64:64 + NS], G_vb[0:NS, NC, :], G_su[0:NS, :], start=False, stop=True)
                last.then_inc(d_svt, 1)
                pe.wait_ge(d_svte, h + 1)
                nc.tensor.transpose(ps[0:NS, 5, 128:256], G_svt, ident).then_inc(d_svn, 1)
                pe.wait_ge(d_svne, h + 1)
                for b in range(NB):
                    mm(ps[:, 5, 256 + b * TS:256 + (b + 1) * TS], G_s0[:, b, :],
                       G_gc[:, TP + b * TS:TP + (b + 1) * TS], start=(b == 0), stop=False)
                last = mm(ps[:, 5, 256:256 + NS], G_svn[0:NS, :], G_sat[0:NS, :], start=False, stop=True)
                last.then_inc(d_so, 1)
                pe.wait_ge(d_kdm, h + 1)
                pe.wait_ge(d_s, h * NC + NC)
                for b in range(NB):
                    last = mm(ps[:, 4 + 2 * (b // 4), (b % 4) * P:(b % 4 + 1) * P], G_kdm[0:NS, b, :], G_svn[0:NS, :],
                              start=True, stop=True)
                last.then_inc(d_sds, 1)
                pe.wait_ge(d_osq, h + 1)
                for hf in range(2):
                    last = mm(ps[:, 5 + 2 * hf, 0:HT], ones, G_sq[:, hf * HT:(hf + 1) * HT], start=True, stop=True)
                last.then_inc(d_oss, 1)
            for _ in project(0):
                pass
            repeat(pe, GH - 1, head)
            head(GH - 1, ahead=False)
            pe.wait_ge(d_yl, GH)
            pe.wait_ge(d_z, GH)
            linear(S_GOUT, 16, hh, hl, z_ready, KT * 3)
            layer_norm(3, 1)
            attention(1)
            layer_norm(4)
            pe.wait_ge(ln_xl, KT * 5)
            for tt in range(NT):
                n = P if tt < NC else NS
                for k in range(KT):
                    last = mm(ps[0:n, 4, tt * 8:tt * 8 + 8], x[:, k, tt * P:tt * P + n], pc("router", 8 * k, 8 * k + 8),
                              start=(k == 0), stop=(k == KT - 1))
            last.then_inc(r_log, 1)
            pe.wait_ge(r_gate, 1)
            for tt in range(NC):
                nc.tensor.transpose(ps[0:NE, 5, tt * P:(tt + 1) * P], R_g[:, tt, :], ident)
            nc.tensor.transpose(ps[0:NE, 6, 0:NS], R_g[0:NS, NC, :], ident[0:NS, 0:NS]).then_inc(r_tr, 1)
            pe.wait_ge(r_row, 2)
            experts(NE, S_MOE, 32, HALVES, 5)
            pe.wait_ge(f_y, KT * (HALVES + NE))
            layer_norm(5)

        @nc_block.scalar
        def _(act):
            A = nc.scalar.activation
            s = Serial(act, act_chain)
            act.dma_start(par[:, :], I["params"]).then_inc(ld_par, 16)
            act.dma_start(tab[:, :], I["tables"]).then_inc(ld_tab, 16)
            act.wait_ge(ld_x, 16)
            for k in range(KT):
                s(A(xh[:, k, :], x[:, k, :], ACT.Copy), *((x_split_h, 1) if k == KT - 1 else ()))
            act.wait_ge(ld_par, 16)
            act.wait_ge(ld_tab, 16)

            def layer_norm(n, l=None):
                for k in range(KT):
                    act.wait_ge(ln_d, n * KT + k + 1)
                    if k >= 2:
                        act.wait_ge(ln_var, n * KT + k - 1)
                    s(A(lnsq[:, k % 2, :], x[:, k, :], ACT.Square), ln_sq, n * KT + k + 1)
                    if l is not None and k < KV_EARLY:
                        kv(l, k)
                act.wait_ge(ln_var, n * KT + KT)
                s(A(two(lnr[:, :]), pair(3), ACT.Ln, bias=pc("eps5"), scale=1.0 / D))
                s(A(lnr[:, :], lnr[:, :], ACT.Exp, scale=-0.5), ln_std, n + 1)
                for k in range(KT):
                    act.wait_ge(ln_n, n * KT + k + 1)
                    if n < NLN - 1:
                        s(A(xh[:, k, :], x[:, k, :], ACT.Identity, bias=pc("lnb", n * 8 + k, n * 8 + k + 1),
                            scale=pc("lng", n * 8 + k, n * 8 + k + 1)), ln_xh, n * KT + k + 1)
                    s(A(x[:, k, :], x[:, k, :], ACT.Identity, bias=pc("lnb", n * 8 + k, n * 8 + k + 1),
                        scale=pc("lng", n * 8 + k, n * 8 + k + 1)), ln_x, n * KT + k + 1)
                    if l is not None:
                        kv(l, KV_EARLY + k)
                    if n == NLN - 1 and k % 4 == 3:
                        act.dma_start(O["y"][:, k - 3:k + 1, :], x[:, k - 3:k + 1, :]).then_inc(out_done, 16)
                if l is not None:
                    for t in range(KV_EARLY + KT, 16):
                        kv(l, t)
                    act.dma_start(O["mem_k"][l], A_k).then_inc(out_done, 16)
                    act.dma_start(O["mem_v"][l], A_v).then_inc(out_done, 16)

            def kv_start(l):
                act.dma_start(A_mem, I["memT"].rearrange("p (a b) -> p a b", b=MEM)).then_inc(mem_in, 16)
                act.sem_inc(ring_free, 1)

            def kv(l, t):
                act.wait_ge(w_used, S_KV[l] + t + 1)
                if t < 8:
                    s(A(A_k[:, t, :], ps[:, 2 * (t % 2), 0:MEM], ACT.Copy), kv_ev, 16 * l + t + 1)
                else:
                    s(A(A_v[:, :, (t - 8) * P:(t - 7) * P], ps[:, 2 * (t % 2), 0:MEM].rearrange("p (a b) -> p a b", b=P),
                        ACT.Copy), kv_ev, 16 * l + t + 1)

            def attention(l):
                for t in range(8):
                    act.wait_ge(w_used, S_Q[l] + t + 1)
                    s(A(two(A_q[:, t, :]), pair(t % 2), ACT.Copy, scale=XD ** -0.5), q_ev, 8 * l + t + 1)
                for h in range(XH):
                    n = XH * l + h
                    act.wait_ge(pa_max, n + 1)
                    for tt in range(4):
                        s(A(A_p[:, tt, :], ps[:, 4 + tt // 2, (tt % 2) * MEM:(tt % 2 + 1) * MEM], ACT.Exp,
                            bias=A_nm[:, tt:tt + 1], accum_out=A_rs[:, tt:tt + 1]), pa_exp, 4 * n + tt + 1)
                    if h == 2:
                        act.wait_ge(ss_max, l + 1)
                        s(A(A_sp, ps[:, 3, 0:MEM], ACT.Exp, bias=A_snm, accum_out=A_srs), ss_exp, l + 1)
                    act.wait_ge(pa_tr, n + 1)
                    s(A(A_pt, ps[:, 6:8, :], ACT.Copy), pa_pt, n + 1)
                    if h == 1:
                        act.wait_ge(c_used, 2 * NB * l + NB)
                        s(A(A_ss, ps[:, 2, 0:MT * P], ACT.Copy), ss_ev, l + 1)
                    if h == 2:
                        act.wait_ge(ss_ptr, l + 1)
                        s(A(A_spt, ps[:, 2, 0:MT * P], ACT.Copy), ss_pt, l + 1)
                    act.wait_ge(pa_o, n + 1)
                    s(A(xh[:, 2 * h:2 * h + 2, 0:TP], ps[:, 0:2, :], ACT.Copy), pa_oh, n + 1)
                act.wait_ge(c_used, 2 * NB * (l + 1))
                s(A(xh[:, :, TP:T], ps[:, 3, 0:KT * NS].rearrange("p (a b) -> p a b", b=NS), ACT.Copy), ss_oh, l + 1)

            def experts(n, slot, e0, gated):
                def one(e):
                    e36, e12 = e * 36 + slot, (e + e0) * FT

                    def up(g):
                        for j in range(2):
                            act.wait_ge(w_used, e36 + g * 4 + (2 * j + 1))
                            ge(act, f_h, e12 + g * 2 + (j - 1))
                            s(A(two(F_s[:, j, :]), pair(2 * j), ACT.Silu), f_silu, e12 + g * 2 + (j + 1))
                            act.wait_ge(f_h, e12 + g * 2 + (j + 1))
                            s(A(hh[:, ds(g * 2 + j, 1), :], F_h[:, j:j + 1, :], ACT.Copy), f_hh, e12 + g * 2 + (j + 1))
                    repeat(act, FT // 2, up, s, passed)
                repeat(act, n, one, s)

            lgw = I["lru_gate"]

            act.wait_ge(lru_sp, 1)
            s(A(L_sp[:, 1, :], L_sp[:, 0, :], ACT.Exp, scale=-1.0), lru_spe, 1)

            def lru(b):
                ge(act, lru_gate_full, b * 4)
                act.dma_start(L_gw.rearrange("p (o a) b -> p o a b", o=1),
                              lgw[ds(b, 1)].rearrange("o p (a b) -> p o a b", a=KT)).then_inc(lru_gw_in, 16)
                for j in range(2):
                    act.wait_ge(w_used, b * 4 + (j + 1))
                    ge(act, lru_cst, b * 2 + (j - 1))
                    s(A(L_ext[:, j, HIST:HIST + HT], ps[:, 2 * j, 0:HT], ACT.Copy))
                    s(A(L_ext[:, j, HIST + HT:HIST + TP], ps[:, 2 * j + 1, 0:TP - HT], ACT.Copy))
                    s(A(L_ext[:, j, EXTP:EXT].rearrange("p (a b) -> p a b", b=SEG)[:, :, HIST:SEG],
                        ps[:, 2 * j + 1, TP - HT:HT].rearrange("p (a b) -> p a b", b=TS), ACT.Copy),
                      lru_ext, b * 2 + (j + 1))
                for j in range(2):
                    act.wait_ge(w_used, b * 4 + (2 + j + 1))
                    ge(act, lru_y, b * 2 + (j - 1))
                    s(A(two(L_gel[:, j, :]), pair(j), ACT.Gelu_apprx_tanh), lru_gelu, b * 2 + (j + 1))
                ge(act, lru_dve, b * 10)
                for g in range(4):
                    act.wait_ge(lru_gate_full, b * 4 + (g + 1))
                    dst = (L_r, L_i)[g // 2]
                    s(A(two(dst[:, g % 2, :]), pair(2 + g % 2), ACT.Sigmoid, bias=L_par[:, g % 2, 4 + g // 2:5 + g // 2]),
                      lru_gate_ev, b * 4 + (g + 1))
                for j in range(2):
                    act.wait_ge(lru_dve, b * 10 + (5 * j + 1))
                    s(A(L_a, L_r[:, j, :], ACT.Exp, scale=-1.0))
                    s(A(L_t, L_r[:, j, :], ACT.Tanh), lru_act, b * 4 + (2 * j + 1))
                    act.wait_ge(lru_dve, b * 10 + (5 * j + 3))
                    s(A(L_t, L_t, ACT.Sqrt), lru_act, b * 4 + (2 * j + 2))
                    act.wait_ge(lru_dve, b * 10 + (5 * j + 5))
                    s(A(hh[:, ds(b * 2 + j, 1), :], L_b.rearrange("p (o c) -> p o c", o=1), ACT.Copy), lru_yh, b * 2 + (j + 1))
            repeat(act, BLK, lru, s)
            act.wait_ge(lru_y, 8)
            act.dma_start(O["lru_conv"], L_cst).then_inc(out_done, 16)
            act.dma_start(O["lru_h"], L_hst).then_inc(out_done, 16)
            act.wait_ge(out_done, 32)
            kv_start(0)
            layer_norm(0, 0)
            attention(0)
            layer_norm(1)
            act.wait_ge(out_done, 64)
            experts(HALVES, S_FFN, 0, False)
            layer_norm(2)

            act.wait_ge(b_mm, 1)
            s(A(two(B_r[1])[0:GH], pair(2)[0:GH], ACT.Sigmoid), b_beta, 1)
            act.wait_ge(b_x, 1)
            s(A(B_r[5][0:GH, :], B_r[5][0:GH, :], ACT.Exp, scale=-1.0))
            s(A(B_r[9][0:GH, 0:1], pc("alog")[0:GH, :], ACT.Exp), b_e, 1)
            act.wait_ge(b_g, 1)
            s(A(B_r[2][0:GH, :], B_r[0][0:GH, :], ACT.Exp))
            s(A(B_r[3][0:GH, :], B_r[3][0:GH, :], ACT.Exp), b_eg, 1)
            act.wait_ge(b_rows, 1)
            for r in range(2):
                act.dma_start(I["scratch"][r], B_r[r][0:GH, :]).then_inc(b_st, 16)
            act.wait_ge(b_st, 32)

            def ext(h, j):
                act.wait_ge(w_used, h * 4 + (S_GDN + j + 1))
                bk = 2 * (j % 2)
                s(A(G_ext[:, j, HIST:HIST + HT], ps[:, bk, 0:HT], ACT.Copy))
                s(A(G_ext[:, j, HIST + HT:HIST + TP], ps[:, bk + 1, 0:TP - HT], ACT.Copy))
                s(A(G_ext[:, j, EXTP:EXT].rearrange("p (a b) -> p a b", b=SEG)[:, :, HIST:SEG],
                    ps[:, bk + 1, TP - HT:HT].rearrange("p (a b) -> p a b", b=TS), ACT.Copy), d_ext, h * 3 + (j + 1))

            def gate_z(h):
                act.wait_ge(w_used, h * 4 + (S_GDN + 4))
                s(A(two(G_z), pair(1), ACT.Silu), d_z, h + 1)

            def rows(h):
                for r, dst in enumerate((G_gc, G_be)):
                    act.dma_start(dst, I["scratch"][r, ds(h, 1), :].to_broadcast((P, T))).then_inc(d_row, 16)
                act.dma_start(G_hist, I["gdn_hist"][ds(h, 1)].rearrange("o p (a b) -> p (o a) b", a=3)).then_inc(d_hist, 16)

            act.wait_ge(b_col, 2)
            rows(0)
            for j in range(3):
                ext(0, j)
            gate_z(0)

            def head(h, ahead=True):
                for j in range(3):
                    act.wait_ge(d_conv, h * 3 + (j + 1))
                    s(A(G_qkv[:, j, :], G_qkv[:, j, :], ACT.Silu), d_silu, h * 3 + (j + 1))
                    if j < 2:
                        s(A(G_rs[:, j, :], G_qkv[:, j, :], ACT.Square), d_sq, h * 2 + (j + 1))
                ge(act, d_sout, h * 32)
                act.dma_start(G_s0, I["gdn_s0"][ds(h, 1)].rearrange("o p (a b) -> p (o a) b", a=NB)).then_inc(d_s0, 16)
                for j in range(2):
                    act.wait_ge(d_ss, h * 2 + (j + 1))
                    s(A(two(G_rs[:, j, :]), pair(2 + j), ACT.Ln, bias=pc("eps6")))
                    s(A(G_rs[:, j, :], G_rs[:, j, :], ACT.Exp, scale=-0.5), d_std, h * 2 + (j + 1))
                act.wait_ge(d_row, h * 32 + 32)
                s(A(G_eg, G_gc, ACT.Exp), d_egr, h + 1)
                act.wait_ge(d_arg, h + 1)
                s(A(G_dt, G_dt, ACT.Exp))
                s(A(G_sdt[0:NS, :], G_sdt[0:NS, :], ACT.Exp), d_dt, h + 1)
                ge(act, d_cso, h * 16)
                s(A(G_cst[:, :, 0:HIST], G_ext[:, :, TP:EXTP], ACT.Copy))
                for j in range(3):
                    s(A(G_cst[:, j, HIST:].rearrange("p (a b) -> p a b", b=HIST),
                        G_ext[:, j, EXTP:EXT].rearrange("p (a b) -> p a b", b=SEG)[:, :, TS:SEG], ACT.Copy),
                      *((d_cst, h + 1) if j == 2 else ()))
                act.dma_start(O["gdn_conv"][ds(h, 1)].rearrange("o p (a b) -> p (o a) b", a=3), G_cst).then_inc(d_cso, 16)
                for v in range(1, LEVELS):
                    act.wait_ge(d_pt, h * LEVELS + (v + 1))
                    if v < SLEVELS:
                        s(A(G_spt[0:NS, :], ps[0:NS, 7, 0:NS], ACT.Copy))
                    s(A(G_pt, ps[:, 4, :].rearrange("p (a b) -> p a b", b=P), ACT.Copy), d_pte, h * (LEVELS - 1) + v)
                    if ahead and v in (3, 5):
                        ext(h + 1, v // 2 - 1)
                act.wait_ge(d_wt, h + 1)
                s(A(G_swt, ps[:, 5, 0:NS], ACT.Copy, scale=-1.0))
                s(A(G_wt, ps[:, 4, :].rearrange("p (a b) -> p a b", b=P), ACT.Copy, scale=-1.0), d_wte, h + 1)
                for c in range(NC):
                    act.wait_ge(d_vn, h * NC + (c + 1))
                    s(A(G_vn[:, c % 2, :], ps[:, 6, c * P:(c + 1) * P], ACT.Copy), d_vne, h * NC + (c + 1))
                    if ahead and c == 1:
                        ext(h + 1, 2)
                act.wait_ge(d_s, h * NC + NC)
                act.dma_start(O["gdn_sp"][ds(h, 1)].rearrange("o p b -> p (o b)"), G_s[:, (NC - 1) % 2, :]).then_inc(d_sout, 16)
                act.wait_ge(d_svt, h + 1)
                s(A(G_svt, ps[:, 5, 64:64 + NS], ACT.Copy), d_svte, h + 1)
                act.wait_ge(d_svn, h + 1)
                s(A(G_svn[0:NS, :], ps[0:NS, 5, 128:256], ACT.Copy), d_svne, h + 1)
                act.wait_ge(d_oe, h + 1)
                s(A(G_sq, G_ot, ACT.Square), d_osq, h + 1)
                if ahead:
                    act.wait_ge(d_so, h + 1)
                    rows(h + 1)
                act.wait_ge(d_oss, h + 1)
                s(A(G_rs[:, 0, 0:HT], ps[:, 5, 0:HT], ACT.Ln, bias=pc("eps6"), scale=1.0 / P))
                s(A(G_rs[:, 0, HT:T], ps[:, 7, 0:HT], ACT.Ln, bias=pc("eps6"), scale=1.0 / P))
                s(A(G_rs[:, 0, :], G_rs[:, 0, :], ACT.Exp, scale=-0.5), d_ostd, h + 1)
                act.wait_ge(d_ssn, h + 1)
                act.dma_start(O["gdn_ss"][ds(h, 1)].rearrange("o p (a b) -> p (o a) b", a=NB), G_s0).then_inc(d_sout, 16)
                act.wait_ge(d_on, h + 1)
                s(A(hh[:, ds(h, 1), :], G_ot.rearrange("p (o c) -> p o c", o=1), ACT.Copy), d_yh, h + 1)
                if ahead:
                    gate_z(h + 1)
            repeat(act, GH - 1, head, s)
            head(GH - 1, ahead=False)
            act.wait_ge(d_cso, 16 * GH)
            act.wait_ge(d_sout, 32 * GH)
            kv_start(1)
            layer_norm(3, 1)
            attention(1)
            layer_norm(4)
            act.wait_ge(r_d, 1)
            s(A(R_w[:, :, 0:1], R_w[:, :, 0:1], ACT.Exp), r_exp, 1)
            act.wait_ge(r_row, 2)
            act.dma_start(I["scratch"][0], R_row[0:NE, :]).then_inc(r_st, 16)
            act.wait_ge(r_st, 16)
            act.wait_ge(out_done, 96)

            def gate_row(e, first):
                if not first:
                    act.wait_ge(f_h, (e + HALVES) * FT)
                act.dma_start(F_g, I["scratch"][0, ds(e, 1), :].to_broadcast((P, T))).then_inc(g_in, 16)

            def one(e):
                gate_row(e, isinstance(e, int))
                e36, e12 = e * 36 + S_MOE, (e + HALVES) * FT

                def up(g):
                    for j in range(2):
                        act.wait_ge(w_used, e36 + g * 4 + (2 * j + 1))
                        ge(act, f_h, e12 + g * 2 + (j - 1))
                        s(A(two(F_s[:, j, :]), pair(2 * j), ACT.Silu), f_silu, e12 + g * 2 + (j + 1))
                        act.wait_ge(f_h, e12 + g * 2 + (j + 1))
                        s(A(hh[:, ds(g * 2 + j, 1), :], F_h[:, j:j + 1, :], ACT.Copy), f_hh, e12 + g * 2 + (j + 1))
                repeat(act, FT // 2, up, s, passed)
            repeat(act, NE, one, s)
            layer_norm(5)

        @nc_block.vector
        def _(dve):
            V = nc.vector
            s = Serial(dve, dve_chain)

            def split_low(dst, src, hi, sm, val):
                s(V.tensor_tensor(dst, src, hi.bitcast(F), SUB), sm, val)

            dve.wait_ge(x_split_h, 1)
            for k in range(KT):
                s(V.tensor_tensor(xl[:, k, :], x[:, k, :], xh[:, k, :].bitcast(F), SUB), *((x_split_l, 1) if k == KT - 1 else ()))
            dve.wait_ge(ld_par, 16)
            dve.wait_ge(ld_tab, 16)

            def layer_norm(n):
                dve.wait_ge(ln_sum, n + 1)
                for k in range(KT):
                    s(V.scalar_tensor_tensor(two(x[:, k, :]), pair(2), -1.0 / D, two(x[:, k, :]), MUL, ADD), ln_d, n * KT + k + 1)
                dve.wait_ge(ln_std, n + 1)
                for k in range(KT):
                    s(V.tensor_tensor(x[:, k, :], x[:, k, :], lnr[:, :], MUL), ln_n, n * KT + k + 1)
                if n < NLN - 1:
                    for k in range(KT):
                        dve.wait_ge(ln_x, n * KT + k + 1)
                        split_low(xl[:, k, :], x[:, k, :], xh[:, k, :], ln_xl, n * KT + k + 1)

            def residual(slot, n):
                for t in range(8):
                    dve.wait_ge(w_used, slot + t + 1)
                    s(V.scalar_tensor_tensor(two(x[:, t, :]), two(x[:, t, :]), ALPHA, pair(t % 2), MUL, ADD),
                      z_ready, n * KT + t + 1)

            def attention(l):
                for h in range(XH):
                    n = XH * l + h
                    dve.wait_ge(pa_s, n + 1)
                    if h:
                        dve.wait_ge(pa_exp, 4 * n)
                    s(V.tensor_reduce(A_nm, ps[:, 4:6, :].rearrange("p a (b c) -> p (a b) c", c=MEM), AX.X, ALU.max, negate=True),
                      pa_max, n + 1)
                    if h == 2:
                        dve.wait_ge(ss_tr, l + 1)
                        s(V.tensor_reduce(A_snm, ps[:, 3, 0:MEM], AX.X, ALU.max, negate=True), ss_max, l + 1)
                    dve.wait_ge(pa_exp, 4 * n + 4)
                    s(V.reciprocal(A_rs, A_rs))
                    s(V.tensor_tensor(A_p, A_p, A_rs.unsqueeze(2).to_broadcast((P, 4, MEM)), MUL), pa_p, n + 1)
                    if h == 2:
                        dve.wait_ge(ss_exp, l + 1)
                        s(V.reciprocal(A_srs, A_srs))
                        s(V.tensor_scalar(A_sp, A_sp, A_srs, None, MUL), ss_p, l + 1)
                    dve.wait_ge(pa_oh, n + 1)
                    s(V.tensor_tensor(xl[:, 2 * h:2 * h + 2, 0:TP], ps[:, 0:2, :], xh[:, 2 * h:2 * h + 2, 0:TP].bitcast(F), SUB),
                      pa_ol, n + 1)
                dve.wait_ge(ss_oh, l + 1)
                s(V.tensor_tensor(xl[:, :, TP:T], ps[:, 3, 0:KT * NS].rearrange("p (a b) -> p a b", b=NS),
                                  xh[:, :, TP:T].bitcast(F), SUB), ss_ol, l + 1)

            def experts(n, slot, e0, gated, n_ln):
                def one(e):
                    e36, e12, e8 = e * 36 + slot, (e + e0) * FT, (e + e0) * KT
                    if gated:
                        dve.wait_ge(g_in, e * 16 + 16)

                    def up(g):
                        for j in range(2):
                            dve.wait_ge(w_used, e36 + g * 4 + (2 * j + 2))
                            dve.wait_ge(f_silu, e12 + g * 2 + (j + 1))
                            if gated:
                                s(V.tensor_tensor(F_s[:, j, :], F_s[:, j, :], F_g, MUL))
                            s(V.tensor_tensor(two(F_h[:, j, :]), two(F_s[:, j, :]), pair(2 * j + 1), MUL), f_h, e12 + g * 2 + (j + 1))
                            dve.wait_ge(f_hh, e12 + g * 2 + (j + 1))
                            split_low(hl[:, ds(g * 2 + j, 1), :], F_h[:, j:j + 1, :], hh[:, ds(g * 2 + j, 1), :],
                                      f_hl, e12 + g * 2 + (j + 1))
                    repeat(dve, FT // 2, up, s, passed)
                    first = isinstance(e, int) and e == 0
                    final = False
                    for d in range(KT):
                        dve.wait_ge(w_used, e36 + (24 + ((d + 1) * FT + KT - 1) // KT))
                        s(V.scalar_tensor_tensor(two(x[:, d, :]), two(x[:, d, :]), ALPHA if first else 1.0, pair(d % 4), MUL, ADD),
                          f_y, e8 + (d + 1))
                repeat(dve, n, one, s)
                for k in range(KT):
                    s(V.tensor_copy(lnr[0:1, 0:1], lnr[0:1, 0:1]), z_ready, n_ln * KT + k + 1)

            def log1p_half(e, t0, t1, t2):
                s(V.tensor_scalar(t0, e, 2.0, None, ADD))
                s(V.reciprocal(t0, t0))
                s(V.tensor_tensor(t0, t0, e, MUL))
                s(V.tensor_tensor(t1, t0, t0, MUL))
                s(V.tensor_scalar(t2, t1, 1.0 / 17, None, MUL))
                for m in range(7, 0, -1):
                    s(V.scalar_tensor_tensor(t2, t2, 1.0 / (2 * m + 1), t1, ADD, MUL))
                s(V.scalar_tensor_tensor(t2, t2, 1.0, t0, ADD, MUL))
                s(V.tensor_scalar(t2, t2, 2.0, None, MUL))

            sp0 = [L_sp[:, i, :] for i in range(6)]
            s(V.scalar_tensor_tensor(sp0[0], pc("lam"), -1.0, pc("lam"), MUL, ALU.max), lru_sp, 1)
            dve.wait_ge(lru_spe, 1)
            log1p_half(sp0[1], sp0[2], sp0[3], sp0[4])
            s(V.tensor_scalar(sp0[0], pc("lam"), -1.0, 0.0, MUL, ALU.max))
            s(V.tensor_tensor(sp0[0], sp0[0], sp0[4], ADD))
            s(V.tensor_scalar(sp0[0], sp0[0], LRU_C, None, MUL))
            s(V.memset(L_ext[:, :, 0:HIST], 0.0))

            lgb = pc("lgb").rearrange("p (a b) -> p a b", b=2)
            lcw = pc("lcw").rearrange("p (a b) -> p a b", b=CW)
            lcb = pc("lcb").rearrange("p (a b) -> p a b", b=1)
            h0v = pc("h0").rearrange("p (a b) -> p a b", b=NB)
            lhv = pc("lhist").rearrange("p (a b) -> p a b", b=NB * HIST)

            def conv(ext, acc, out, w, bias):
                if bias is None:
                    s(V.tensor_scalar(acc, ext[:, 0:CONV], w(0), None, MUL))
                else:
                    s(V.tensor_scalar(acc, ext[:, 0:CONV], w(0), bias, MUL, ADD))
                for j in (1, 2):
                    s(V.scalar_tensor_tensor(acc, ext[:, j:j + CONV], w(j), acc, MUL, ADD))
                s(V.scalar_tensor_tensor(out[:, 0:TP], ext[:, 3:3 + TP], w(3), acc[:, 0:TP], MUL, ADD))
                seg = ext[:, EXTP:EXT].rearrange("p (a b) -> p a b", b=SEG)[:, :, HIST:SEG]
                a7 = acc[:, EXTP:EXTP + (NB - 1) * SEG].rearrange("p (a b) -> p a b", b=SEG)[:, :, 0:TS]
                o7 = out[:, TP:TP + (NB - 1) * TS].rearrange("p (a b) -> p a b", b=TS)
                s(V.scalar_tensor_tensor(o7, seg[:, 0:NB - 1, :], w(3), a7, MUL, ADD))
                return V.scalar_tensor_tensor(out[:, T - TS:T], ext[:, EXT - TS:EXT], w(3), acc[:, CONV - TS:CONV], MUL, ADD)

            def lru(b):
                s(V.tensor_copy(L_par[:, :, 0:4], lcw[:, ds(b * 2, 2), :]))
                s(V.tensor_copy(L_par[:, :, 4:6], lgb[:, ds(b * 2, 2), :]))
                s(V.tensor_copy(L_h0, h0v[:, ds(b * 2, 2), :]))
                s(V.tensor_copy(L_sp[:, 5, 0:2], L_sp[:, 0, ds(b * 2, 2)]))
                s(V.tensor_copy(L_sp[:, 5, 2:4], pc("lcb")[:, ds(b * 2, 2)]))
                hv = lhv[:, ds(b * 2, 2), :]
                for j in range(2):
                    s(V.tensor_copy(L_ext[:, j, EXTP:EXT].rearrange("p (a b) -> p a b", b=SEG)[:, :, 0:HIST],
                                    lhv[:, ds(b * 2 + j, 1), :].rearrange("p o (a b) -> p (o a) b", b=HIST)))
                for j in range(2):
                    dve.wait_ge(lru_ext, b * 2 + (j + 1))
                    ge(dve, lru_gate_full, b * 4)
                    s(conv(L_ext[:, j, :], L_acc, L_rec[:, j, :], lambda t: L_par[:, j, t:t + 1], L_sp[:, 5, 2 + j:3 + j]),
                      lru_conv, b * 2 + (j + 1))
                    s(V.tensor_copy(L_cst[:, ds(b * 2 + j, 1), 0:HIST], L_ext[:, j:j + 1, TP:EXTP]))
                    s(V.tensor_copy(L_cst[:, ds(b * 2 + j, 1), HIST:].rearrange("p o (a b) -> p (o a) b", b=HIST),
                                    L_ext[:, j, EXTP:EXT].rearrange("p (a b) -> p a b", b=SEG)[:, :, TS:SEG]),
                      lru_cst, b * 2 + (j + 1))
                dve.wait_ge(lru_gate_ev, b * 4 + 4)
                for j in range(2):
                    s(V.tensor_scalar(L_r[:, j, :], L_r[:, j, :], L_sp[:, 5, j:j + 1], None, MUL), lru_dve, b * 10 + (5 * j + 1))
                    s(V.tensor_tensor(L_i[:, j, :], L_i[:, j, :], L_rec[:, j, :], MUL), lru_dve, b * 10 + (5 * j + 2))
                    dve.wait_ge(lru_act, b * 4 + (2 * j + 1))
                    s(V.tensor_scalar(L_b, L_t, 1.0, None, ADD))
                    s(V.reciprocal(L_b, L_b))
                    s(V.scalar_tensor_tensor(L_t, L_t, 2.0, L_b, MUL, MUL), lru_dve, b * 10 + (5 * j + 3))
                    dve.wait_ge(lru_act, b * 4 + (2 * j + 2))
                    s(V.tensor_tensor(L_b, L_t, L_i[:, j, :], MUL))
                    a0 = L_a[:, TP:T].rearrange("p (a b) -> p a b", b=TS)[:, :, 0:1]
                    b0 = L_b[:, TP:T].rearrange("p (a b) -> p a b", b=TS)[:, :, 0:1]
                    s(V.tensor_tensor(L_h0[:, j, :].unsqueeze(2), a0, L_h0[:, j, :].unsqueeze(2), MUL))
                    s(V.tensor_tensor(b0, b0, L_h0[:, j, :].unsqueeze(2), ADD))
                    s(V.memset(a0, 0.0))
                    s(V.tensor_tensor_scan(L_t, L_a, L_b, 0.0, MUL, ADD))
                    s(V.tensor_copy(L_hst[:, ds(b * 2 + j, 1), 0:1], L_t[:, TP - 1:TP].unsqueeze(1)))
                    s(V.tensor_copy(L_hst[:, ds(b * 2 + j, 1), 1:], L_t[:, TP:T].rearrange("p (o a b) -> p o a b", o=1, b=TS)[:, :, :, TS - 1]),
                      lru_dve, b * 10 + (5 * j + 4))
                    dve.wait_ge(lru_gelu, b * 2 + (j + 1))
                    s(V.tensor_tensor(L_b, L_t, L_gel[:, j, :], MUL), lru_dve, b * 10 + (5 * j + 5))
                    dve.wait_ge(lru_yh, b * 2 + (j + 1))
                    split_low(hl[:, ds(b * 2 + j, 1), :], L_b.rearrange("p (o c) -> p o c", o=1), hh[:, ds(b * 2 + j, 1), :],
                              lru_y, b * 2 + (j + 1))
            repeat(dve, BLK, lru, s)
            residual(S_LOUT, 0)
            layer_norm(0)
            attention(0)
            residual(S_O[0], 1)
            layer_norm(1)
            experts(HALVES, S_FFN, 0, False, 2)
            layer_norm(2)

            g8 = lambda i: B_r[i][0:GH, :]
            dve.wait_ge(ln_x, KT * 3)
            dve.wait_ge(b_beta, 1)
            s(V.tensor_scalar(two(g8(4)), pair(3)[0:GH], pc("dtb")[0:GH, :], None, ADD))
            s(V.scalar_tensor_tensor(g8(5), g8(4), -1.0, g8(4), MUL, ALU.max), b_x, 1)
            dve.wait_ge(b_e, 1)
            log1p_half(g8(5), g8(6), g8(7), g8(8))
            s(V.scalar_tensor_tensor(g8(4), g8(4), 0.0, g8(8), ALU.max, ADD))
            s(V.tensor_scalar(g8(4), g8(4), B_r[9][0:GH, 0:1], -1.0, MUL, MUL))
            s(V.memset(g8(6), 1.0))
            s(V.memset(B_r[6][0:GH, 0:TP].rearrange("p (a b) -> p a b", b=C)[:, :, 0:1], 0.0))
            s(V.memset(B_r[6][0:GH, TP:T].rearrange("p (a b) -> p a b", b=TS)[:, :, 0:1], 0.0))
            s(V.tensor_tensor_scan(g8(0), g8(6), g8(4), 0.0, MUL, ADD))
            for lo, hi, w in ((0, TP, C), (TP, T, TS)):
                v0 = B_r[0][0:GH, lo:hi].rearrange("p (a b) -> p a b", b=w)
                v3 = B_r[3][0:GH, lo:hi].rearrange("p (a b) -> p a b", b=w)
                n = (hi - lo) // w
                s(V.tensor_tensor(v3, v0[:, :, w - 1:w].to_broadcast((GH, n, w)), v0, SUB), *((b_g, 1) if lo else ()))
            dve.wait_ge(b_eg, 1)
            s(V.tensor_tensor(g8(2), g8(2), g8(1), MUL), b_rows, 1)
            dve.wait_ge(b_tr, 1)
            s(V.tensor_copy(G_cols[:, 0:NC, :, :], ps[:, 4, 0:NC * 32].rearrange("p (a b c) -> p a b c", b=4, c=GH)), b_col, 1)
            s(V.tensor_copy(G_cols[0:NS, NC, :, :], ps[0:NS, 4, NC * 32:NT * 32].rearrange("p (b c) -> p b c", c=GH)), b_col, 2)
            dve.wait_ge(b_st, 32)
            s(V.memset(G_ext[:, :, 0:HIST], 0.0))

            gcw = pc("gcw").rearrange("p (h a) -> p h a", h=GH)
            mincl = tc("mincl")
            levels = tc("levels").rearrange("p (a b) -> p a b", b=P)

            def head(h):
                s(V.tensor_copy(G_cw.rearrange("p (o a) b -> p o (a b)", o=1), gcw[:, ds(h, 1), :]))
                s(V.tensor_copy(G_hc[:, 0:NC, :], G_cols[:, 0:NC, :, ds(h, 1)].rearrange("p a b o -> p a (b o)")))
                s(V.tensor_copy(G_hc[0:NS, NC, :], G_cols[0:NS, NC, :, ds(h, 1)].rearrange("p b o -> p (b o)")))
                dve.wait_ge(d_hist, h * 16 + 16)
                ge(dve, d_cst, h)
                for j in range(3):
                    s(V.tensor_copy(G_ext[:, j, EXTP:EXT].rearrange("p (a b) -> p a b", b=SEG)[:, :, 0:HIST],
                                    G_hist[:, j, :].rearrange("p (a b) -> p a b", b=HIST)))
                ge(dve, d_yh, h)
                for j in range(3):
                    dve.wait_ge(d_ext, h * 3 + (j + 1))
                    s(conv(G_ext[:, j, :], G_acc[:, 0:CONV], G_qkv[:, j, :], lambda t: G_cw[:, j, t:t + 1], None),
                      d_conv, h * 3 + (j + 1))
                dve.wait_ge(d_row, h * 32 + 32)
                for c in range(NC):
                    s(V.scalar_tensor_tensor(G_dt[:, c, :], G_gc[:, c * P:(c + 1) * P], G_hc[:, c, 0:1], mincl, SUB, ALU.min))
                s(V.scalar_tensor_tensor(G_sdt[0:NS, :], G_gc[0:NS, TP:T], G_hc[0:NS, NC, 0:1], tc("smincl")[0:NS, :], SUB, ALU.min),
                  d_arg, h + 1)
                for j in range(2):
                    dve.wait_ge(d_std, h * 2 + (j + 1))
                    s(V.scalar_tensor_tensor(G_qkv[:, j, :], G_qkv[:, j, :], P ** -0.5 if j == 0 else 1.0, G_rs[:, j, :], MUL, MUL),
                      d_qk, h * 2 + (j + 1))
                dve.wait_ge(d_dt, h + 1)
                s(V.tensor_tensor(G_bl[:, 1], G_dt, G_be[:, 0:TP].rearrange("p (a b) -> p a b", b=P), MUL))
                s(V.tensor_tensor(G_sbl[0:NS, :], G_sdt[0:NS, :], G_be[0:NS, TP:T], MUL))
                col = lambda c: G_hc[:, 0:NC, c:c + 1].to_broadcast((P, NC, P))
                b4 = lambda bank: ps[:, bank, :].rearrange("p (a b) -> p a b", b=P)
                dve.wait_ge(d_tm, h * 2 + 1)
                s(V.tensor_tensor(G_kb[:, 0:NC, :], b4(4), col(2), MUL))
                s(V.tensor_tensor(G_kd[:, 0:NC, :], b4(4), col(3), MUL))
                s(V.tensor_scalar(G_kb[0:NS, NC, :], ps[0:NS, 5, 0:P], G_hc[0:NS, NC, 2:3], None, MUL))
                s(V.tensor_scalar(G_kd[0:NS, NC, :], ps[0:NS, 5, 0:P], G_hc[0:NS, NC, 3:4], None, MUL), d_tme, h * 2 + 1)
                dve.wait_ge(d_tm, h * 2 + 2)
                s(V.tensor_tensor(G_vb[:, 0:NC, :], b4(6), col(1), MUL))
                s(V.tensor_scalar(G_vb[0:NS, NC, :], ps[0:NS, 7, 0:P], G_hc[0:NS, NC, 1:2], None, MUL), d_tme, h * 2 + 2)
                dve.wait_ge(d_kk, h * 2 + 2)
                s(V.tensor_tensor(G_at, b4(6), G_dt, MUL))
                s(V.tensor_tensor(G_sat[0:NS, :], ps[0:NS, 7, 0:NS], G_sdt[0:NS, :], MUL))
                s(V.tensor_tensor(G_dt, b4(4), G_bl[:, 1], MUL))
                s(V.tensor_tensor(G_sdt[0:NS, :], ps[0:NS, 5, 0:NS], G_sbl[0:NS, :], MUL), d_at, h + 1)
                idb = ident.unsqueeze(1).to_broadcast((P, NC, P))

                def block(v):
                    if v < SLEVELS:
                        s(V.tensor_tensor(G_sbl[0:NS, :], G_sdt[0:NS, :], levels[0:NS, v, 0:NS], MUL))
                    s(V.tensor_tensor(G_bl[:, v % 2], G_dt, levels[:, v, :].unsqueeze(1).to_broadcast((P, NC, P)), MUL),
                      d_bl, h * LEVELS + (v + 1))

                block(0)
                s(V.tensor_tensor(G_u, idb, G_bl[:, 0], SUB))
                s(V.tensor_tensor(G_su[0:NS, :], ident[0:NS, 0:NS], G_sbl[0:NS, :], SUB), d_ute, h * LEVELS + 1)
                dve.wait_ge(d_pt, h * LEVELS + 1)
                block(1)
                s(V.tensor_tensor(G_st[0:NS, :], ident[0:NS, 0:NS], ps[0:NS, 7, 0:NS], SUB))
                s(V.tensor_tensor(G_t, idb, b4(5), SUB), d_tt, h * (LEVELS - 1) + 1)
                dve.wait_ge(d_egr, h + 1)
                s(V.tensor_tensor(G_gc, G_eg, G_qkv[:, 0, :], MUL), d_qg, h + 1)
                for v in range(1, LEVELS):
                    small = v < SLEVELS
                    if v + 1 < LEVELS:
                        block(v + 1)
                    if v < LEVELS - 1:
                        dve.wait_ge(d_ut, h * (LEVELS - 2) + v)
                        s(V.tensor_tensor(G_t, G_t, b4(5), SUB), d_tt, h * (LEVELS - 1) + (v + 1))
                    dve.wait_ge(d_uu, h * (LEVELS - 1) + v)
                    if small:
                        s(V.tensor_tensor(G_su[0:NS, :], G_su[0:NS, :], ps[0:NS, 7, 32:32 + NS], SUB))
                    s(V.tensor_tensor(G_u, G_u, b4(6), SUB), d_ute, h * LEVELS + (v + 1))
                ge(dve, d_sout, h * 32)
                for c in range(NC):
                    dve.wait_ge(d_o, h * NC + (c + 1))
                    if c:
                        s(V.scalar_tensor_tensor(G_s[:, c % 2, :], G_s[:, (c + 1) % 2, :], G_eg[:, c * P + P - 1:c * P + P],
                                                 ps[:, 4, c * P:(c + 1) * P], MUL, ADD), d_s, h * NC + (c + 1))
                    else:
                        s(V.tensor_copy(G_s[:, 0, :], ps[:, 4, 0:P]), d_s, h * NC + 1)
                s(V.tensor_tensor(G_kdm[0:NS, :, :], G_kd[0:NS, NC:NT, :].to_broadcast((NS, NB, P)),
                                  tc("smask")[0:NS, :].unsqueeze(2).to_broadcast((NS, NB, P)), MUL), d_kdm, h + 1)
                dve.wait_ge(d_so, h + 1)
                s(V.tensor_copy(G_ot[:, 0:TP], ps[:, 7, :]))
                s(V.tensor_copy(G_ot[:, TP:T], ps[:, 5, 256:256 + NS]), d_oe, h + 1)
                egl = G_eg[:, TP:T].rearrange("p (a b) -> p a b", b=TS)[:, :, TS - 1:TS].to_broadcast((P, NB, P))
                s(V.tensor_tensor(G_s0, G_s0, egl, MUL))
                dve.wait_ge(d_sds, h + 1)
                s(V.tensor_tensor(G_s0[:, 0:4, :], G_s0[:, 0:4, :], b4(4), ADD))
                s(V.tensor_tensor(G_s0[:, 4:8, :], G_s0[:, 4:8, :], b4(6), ADD), d_ssn, h + 1)
                dve.wait_ge(d_ostd, h + 1)
                s(V.tensor_tensor(G_ot, G_ot, G_rs[:, 0, :], MUL))
                s(V.scalar_tensor_tensor(G_ot, G_ot, pc("ng"), G_z, MUL, MUL), d_on, h + 1)
                dve.wait_ge(d_yh, h + 1)
                split_low(hl[:, ds(h, 1), :], G_ot.rearrange("p (o c) -> p o c", o=1), hh[:, ds(h, 1), :], d_yl, h + 1)
            repeat(dve, GH, head, s)
            residual(S_GOUT, 3)
            layer_norm(3)
            attention(1)
            residual(S_O[1], 4)
            layer_norm(4)

            dve.wait_ge(r_log, 1)
            s(V.memset(R_l, 0.0))
            s(V.tensor_copy(R_l[:, 0:NC, :], ps[:, 4, 0:NC * 8].rearrange("p (a b) -> p a b", b=8)))
            s(V.tensor_copy(R_l[0:NS, NC, :], ps[0:NS, 4, NC * 8:NT * 8]))
            for tt in range(NT):
                s(V.max(R_m[:, tt, :], R_l[:, tt, :]))
                s(V.max_index(R_i[:, tt, :], R_m[:, tt, :], R_l[:, tt, :]))
            s(V.tensor_copy(R_f, R_i))
            s(V.tensor_tensor(R_w[:, :, 0:1], R_m[:, :, 1:2], R_m[:, :, 0:1], SUB), r_d, 1)
            dve.wait_ge(r_exp, 1)
            s(V.tensor_scalar(R_w[:, :, 1:2], R_w[:, :, 0:1], 1.0, None, ADD))
            s(V.reciprocal(R_w[:, :, 1:2], R_w[:, :, 1:2]))
            s(V.tensor_tensor(R_w[:, :, 0:1], R_w[:, :, 0:1], R_w[:, :, 1:2], MUL))
            iob = pc("iota").unsqueeze(1).to_broadcast((P, NT, 8))
            for m, dst in ((0, R_g), (1, R_o)):
                s(V.tensor_tensor(dst, iob, R_f[:, :, m:m + 1].to_broadcast((P, NT, 8)), ALU.is_equal))
                s(V.tensor_tensor(dst, dst, R_w[:, :, 1 - m:2 - m].to_broadcast((P, NT, 8)), MUL))
            s(V.tensor_tensor(R_g, R_g, R_o, ADD), r_gate, 1)
            dve.wait_ge(r_tr, 1)
            s(V.tensor_copy(R_row[0:NE, 0:TP], ps[0:NE, 5, :]), r_row, 1)
            s(V.tensor_copy(R_row[0:NE, TP:T], ps[0:NE, 6, 0:NS]), r_row, 2)
            experts(NE, S_MOE, HALVES, True, 5)
            layer_norm(5)


N_OUT = 2 + 2 * NL + 2


def kernel(**inputs):
    import numpy as np
    import concourse.bacc as bacc
    from concourse.bass_utils import run_bass_kernel_spmd as run

    g = {k: np.asarray(v) for k, v in inputs.items()}

    def feat(a):
        a = a.reshape(-1, a.shape[-1])
        return np.ascontiguousarray(a.reshape(a.shape[0], -1, P).transpose(2, 1, 0))

    def slots(w):
        n = w.shape[1] // P
        return w.reshape(KT, P, n, P).transpose(2, 1, 0, 3).reshape(n, P, KT * P)

    def hidden(gu, down):
        f = gu.shape[1] // 2
        a = np.stack([slots(gu[:, :f]), slots(gu[:, f:])], 1).reshape(-1, P, KT * P)
        t = down.reshape(FT, P, KT, P).transpose(2, 0, 1, 3).reshape(12, KT, P, P)
        return [a, t.transpose(0, 2, 1, 3).reshape(12, P, KT * P)]

    win = slots(g["lru_w_in"][0])
    order = [win[[8 + 2 * b, 9 + 2 * b, 2 * b, 2 * b + 1]] for b in range(BLK)]
    order.append(slots(g["lru_w_out"][0]))
    order += [slots(g[n][0]) for n in ("xa_wk", "xa_wv", "xa_wq", "xa_wo")]
    gu, dn = g["ffn_w_gu"][0], g["ffn_w_down"][0]
    for i in range(HALVES):
        c = slice(i * FF, (i + 1) * FF)
        order += hidden(np.concatenate([gu[:, :2 * FF][:, c], gu[:, 2 * FF:][:, c]], 1), dn[c])
    gin = g["gdn_w_in"][0]
    gs = slots(gin[:, :4096])
    order.append(gs.reshape(4, GH, P, KT * P).transpose(1, 0, 2, 3).reshape(4 * GH, P, KT * P))
    order.append(slots(g["gdn_w_out"][0]))
    order += [slots(g[n][1]) for n in ("xa_wk", "xa_wv", "xa_wq", "xa_wo")]
    for e in range(NE):
        order += hidden(g["moe_w_gu"][0, e], g["moe_w_down"][0, e])
    weights = np.concatenate(order, 0)

    par = np.zeros((P, NPAR), np.float32)

    def put(name, a):
        a = a.reshape(a.shape[0], -1)
        par[:a.shape[0], PO[name][0]:PO[name][0] + a.shape[1]] = a

    put("lcw", g["lru_conv_w"][0].reshape(CW, KT, P).transpose(2, 1, 0))
    put("lcb", feat(g["lru_conv_b"][0][None]))
    put("lgb", g["lru_gate_b"][0].reshape(BLK, 2, 2, P).transpose(3, 0, 2, 1))
    put("lam", feat(g["lru_lambda"][0][None]))
    put("h0", feat(g["state_lru_h"][0]))
    put("lhist", feat(g["state_lru_conv"][0]))
    put("lng", g["ln_g"].reshape(NLN, KT, P).transpose(2, 0, 1))
    put("lnb", g["ln_b"].reshape(NLN, KT, P).transpose(2, 0, 1))
    put("gcw", g["gdn_conv_w"][0].reshape(CW, 3, GH, P).transpose(3, 2, 1, 0))
    put("ng", g["gdn_norm_g"][0][:, None])
    put("router", g["moe_router"][0].reshape(KT, P, NE).transpose(1, 0, 2))
    put("wba", gin[:, 4096:].reshape(KT, P, 2 * GH).transpose(1, 0, 2))
    put("dtb", g["gdn_dt_bias"][0][:, None])
    put("alog", g["gdn_a_log"][0][:, None])
    put("eps5", np.full((P, 1), 1e-5, np.float32))
    put("eps6", np.full((P, 1), 1e-6, np.float32))
    put("iota", np.broadcast_to(np.arange(8, dtype=np.float32), (P, 8)))

    tab = np.zeros((P, NTAB), np.float32)
    i, j = np.arange(P)[None, :], np.arange(P)[:, None]
    tab[:, TO["ident"][0]:TO["ident"][1]] = i == j
    tab[:, TO["ones"][0]:TO["ones"][1]] = 1.0
    tab[:, TO["mincl"][0]:TO["mincl"][1]] = np.where(i >= j, 0.0, NEG)
    for v in range(LEVELS):
        w = 1 << v
        tab[:, TO["levels"][0] + v * P:TO["levels"][0] + (v + 1) * P] = \
            (i // (2 * w) == j // (2 * w)) & (i // w % 2 == 1) & (j // w % 2 == 0)
    si, sj = i[:, :NS], j[:NS]
    tab[:NS, TO["smincl"][0]:TO["smincl"][1]] = np.where((si // TS == sj // TS) & (si >= sj), 0.0, NEG)
    tab[:NS, TO["smask"][0]:TO["smask"][1]] = sj // TS == np.arange(NB)[None, :]

    gw = g["lru_gate_w"][0].reshape(BLK, 2, P, 4, P).transpose(0, 2, 1, 3, 4).reshape(BLK, P, KT * P)
    ck = g["cache_mem_k"].reshape(NL, NB, MEM, KT, P).transpose(0, 1, 4, 3, 2).reshape(NL, NB, P, 2048)
    cv = g["cache_mem_v"].reshape(NL, NB, MT, P, D).transpose(0, 1, 3, 2, 4).reshape(NL, NB, P, 2048)
    ins = {
        "xT": feat(np.concatenate([g["x_prompt"].reshape(TP, D), g["x_sample"].reshape(NS, D)], 0)),
        "weights": weights, "params": par, "tables": tab, "lru_gate": gw,
        "memT": feat(g["mem_prompt"][0]).reshape(P, -1),
        "cache": np.concatenate([ck, cv], 1),
        "gdn_hist": g["state_gdn_conv"][0].reshape(NB * HIST, 3, GH, P).transpose(2, 3, 1, 0).reshape(GH, P, -1),
        "gdn_s0": g["state_gdn_s"][0].transpose(1, 2, 0, 3).reshape(GH, P, NB * P),
    }
    outs = {"y": (P, KT, T), "lru_conv": (P, KT, HIST + NB * HIST), "lru_h": (P, KT, 1 + NB),
            "mem_k": (NL, P, KT, MEM), "mem_v": (NL, P, MT, D), "gdn_conv": (GH, P, 3 * (HIST + NB * HIST)),
            "gdn_sp": (GH, P, P), "gdn_ss": (GH, P, NB * P)}
    nc = bacc.Bacc("TRN2", target_bir_lowering=False, num_devices=1)
    f32 = mybir.dt.float32
    ins = {k: np.ascontiguousarray(v) for k, v in ins.items()}
    I = {k: nc.dram_tensor(k, v.shape, f32, kind="ExternalInput").ap() for k, v in ins.items()}
    O = {k: nc.dram_tensor("out_" + k, v, f32, kind="ExternalOutput").ap() for k, v in outs.items()}
    I["scratch"] = nc.dram_tensor("scratch", (2, GH, T), f32, kind="Internal").ap()
    trunk(nc, I, O)
    r = run(nc, [ins], core_ids=[0]).results[0]
    r = {k: r["out_" + k] for k in outs}

    y = r["y"].transpose(2, 1, 0).reshape(T, D)
    lc = r["lru_conv"].transpose(2, 1, 0).reshape(-1, D)
    lh = r["lru_h"].transpose(2, 1, 0).reshape(-1, D)
    gc = r["gdn_conv"].reshape(GH, P, 3, -1).transpose(3, 2, 0, 1).reshape(-1, 3 * D)
    mk = r["mem_k"].transpose(0, 3, 2, 1).reshape(NL, 1, MEM, XH, XD)
    mv = r["mem_v"].transpose(0, 2, 1, 3).reshape(NL, 1, MEM, XH, XD)
    ss = r["gdn_ss"].reshape(GH, P, NB, P).transpose(2, 0, 1, 3)
    c = np.ascontiguousarray
    return (c(y[:TP][None]), c(y[TP:].reshape(NB, TS, D)), c(lh[:1][None]), c(lc[:HIST].reshape(1, 1, HIST, D)),
            c(r["gdn_sp"][None, None]), c(gc[:HIST].reshape(1, 1, HIST, 3 * D)), c(mk), c(mv),
            c(lh[1:][None]), c(lc[HIST:].reshape(1, NB, HIST, D)), c(ss[None]), c(gc[HIST:].reshape(1, NB, HIST, 3 * D)))
```

```python
import concourse.bass as bass
from concourse import mybir
from contextlib import ExitStack

P = 128
D, KT = 1024, 8
TP, NB, TS = 512, 8, 4
NS = NB * TS
T = TP + NS
HT = T // 2
CW, HIST = 4, 3
EXTP = HIST + TP
SEG = HIST + TS
EXT = EXTP + NB * SEG
CONV = EXT - HIST
NL, NLN = 2, 6
XH, XD, MEM, MT = 4, 256, 256, 2
GH, C, NC = 8, 128, 4
NT = NC + 1
NE, FF, FT = 8, 1536, 12
HALVES = 2
KV_EARLY = 3
LEVELS = 7
SLEVELS = 2
CAP = 192
CT = ((0, P), (P, CAP - P))
TBANK = (0, 1, 2, 3, 6, 7, 4, 5, 0, 1)
EARLY = 6
BLK = 4
ALPHA = float((2 * NL) ** 0.25)
LRU_C = 8.0
RAW, SPLIT = 4, 2
SLOTS = 16 + 8 + 4 * 8 + HALVES * 36 + GH * 4 + 8 + 4 * 8 + NE * 36
NEG = -1.0e30

_COLS = [("lcw", 8 * 4), ("lcb", 8), ("lgb", 16), ("lam", 8), ("h0", 64), ("lhist", 192),
         ("lng", 48), ("lnb", 48), ("gcw", 96), ("ng", 1), ("router", 64), ("wba", 128),
         ("dtb", 1), ("alog", 1), ("eps5", 1), ("eps6", 1), ("iota", 8)]
PO, _n = {}, 0
for _name, _w in _COLS:
    PO[_name] = (_n, _n + _w)
    _n += _w
NPAR = _n
_TABS = [("ident", 128), ("ones", 128), ("mincl", 128), ("levels", LEVELS * 128), ("smincl", 32), ("smask", NB)]
TO, _n = {}, 0
for _name, _w in _TABS:
    TO[_name] = (_n, _n + _w)
    _n += _w
NTAB = _n


class Serial:

    def __init__(self, eng, sem):
        self.eng, self.sem, self.base, self.k, self.total = eng, sem, 0, 0, 0

    def __call__(self, ins, sem=None, val=None):
        if sem is None:
            self.k += 1
            self.total += 1
            ins.then_inc(self.sem, 1)
            self.eng.wait_ge(self.sem, self.base + self.k)
        else:
            ins.then_inc(sem, 1)
            self.eng.wait_ge(sem, val)


def repeat(eng, n, body, chain=None, inner=None):
    if chain is None:
        body(0)
        if n > 1:
            with eng.Fori(1, n) as i:
                body(i)
        return
    start, before = chain.base + chain.k, chain.total
    chain.base, chain.k = start, 0
    body(0)
    length = chain.total - before
    if inner is not None:
        eng.sem_inc(inner, 1)
    if n > 1:
        with eng.Fori(1, n) as i:
            chain.base, chain.k = start + i * length, 0
            body(i)
    chain.base, chain.k, chain.total = start + n * length, 0, before + n * length


def ge(eng, sem, val):
    if isinstance(val, int) and val <= 0:
        return
    eng.wait_ge(sem, val)


def trunk(nc, I, O):
    F, R = mybir.dt.float32, mybir.dt.float32r
    ALU, ACT, AX = mybir.AluOpType, mybir.ActivationFunctionType, mybir.AxisListType
    MUL, ADD, SUB = ALU.mult, ALU.add, ALU.subtract
    ds = bass.ds

    with ExitStack() as ctx:
        def sb(name, shape, dt=F):
            return ctx.enter_context(nc.sbuf_tensor(name, shape, dt))

        def sem(name):
            return ctx.enter_context(nc.semaphore(name))

        x = sb("x", [P, KT, T])
        xh = sb("xh", [P, KT, T], R)
        xl = sb("xl", [P, KT, T], R)
        raw = sb("raw", [P, RAW, KT, P])
        wh = sb("wh", [P, SPLIT, KT, P], R)
        wl = sb("wl", [P, SPLIT, KT, P], R)
        par = sb("par", [P, NPAR])
        tab = sb("tab", [P, NTAB])
        hh = sb("hh", [P, FT, T], R)
        hl = sb("hl", [P, FT, T], R)
        WORK = 15200
        work = sb("work", [P, WORK])
        lnsq = sb("lnsq", [P, 2, T])
        lnr = sb("lnr", [P, T])
        ps = ctx.enter_context(nc.psum_tensor("ps", [P, 8, 512], F))

        def carve():
            at = [0]

            def take(*shape):
                n = 1
                for s in shape:
                    n *= s
                v = work[:, at[0]:at[0] + n]
                at[0] += n
                assert at[0] <= WORK, at[0]
                if len(shape) == 2:
                    v = v.rearrange("p (a b) -> p a b", b=shape[1])
                if len(shape) == 3:
                    v = v.rearrange("p (a b c) -> p a b c", b=shape[1], c=shape[2])
                return v
            return take

        def pc(name, a=0, b=None):
            lo, hi = PO[name]
            return par[:, lo + a:(hi if b is None else lo + b)]

        def tc(name, a=0, b=None):
            lo, hi = TO[name]
            return tab[:, lo + a:(hi if b is None else lo + b)]

        ident, ones = tc("ident"), tc("ones")

        def pair(i):
            return ps[:, 2 * i:2 * i + 2, 0:HT]

        def two(v):
            return v.rearrange("p (h c) -> p h c", h=2)

        w_in = [sem(f"w_in{j}") for j in range(RAW)]
        w_split = sem("w_split")
        w_used = sem("w_used")
        dve_chain, act_chain = sem("dve_chain"), sem("act_chain")
        pool_hi = sem("pool_hi")
        passed = sem("passed")
        ld_x, ld_par, ld_tab = sem("ld_x"), sem("ld_par"), sem("ld_tab")
        x_split_h, x_split_l = sem("x_split_h"), sem("x_split_l")
        out_done = sem("out_done")
        lru_gw_in = sem("lru_gw_in")
        lru_ext, lru_conv = sem("lru_ext"), sem("lru_conv")
        lru_gate_full, lru_gate_ev = sem("lru_gate_full"), sem("lru_gate_ev")
        lru_gelu, lru_act, lru_dve, lru_y, lru_yh = (sem("lru_gelu"), sem("lru_act"), sem("lru_dve"),
                                                     sem("lru_y"), sem("lru_yh"))
        lru_sp, lru_spe, lru_cst = sem("lru_sp"), sem("lru_spe"), sem("lru_cst")
        z_ready = sem("z_ready")
        z_sum = sem("z_sum")
        ln_sum, ln_d, ln_sq, ln_var, ln_std, ln_n, ln_x, ln_xh, ln_xl = (
            sem("ln_sum"), sem("ln_d"), sem("ln_sq"), sem("ln_var"), sem("ln_std"), sem("ln_n"),
            sem("ln_x"), sem("ln_xh"), sem("ln_xl"))
        mem_in, kv_ev = sem("mem_in"), sem("kv_ev")
        ring_free = sem("ring_free")
        q_ev, c_in, c_used = sem("q_ev"), [sem("c_in0"), sem("c_in1")], sem("c_used")
        ss_ev, ss_tr, ss_max, ss_exp, ss_p, ss_ptr, ss_pt, ss_oh, ss_ol = (
            sem("ss_ev"), sem("ss_tr"), sem("ss_max"), sem("ss_exp"), sem("ss_p"),
            sem("ss_ptr"), sem("ss_pt"), sem("ss_oh"), sem("ss_ol"))
        pa_s, pa_max, pa_exp, pa_p, pa_tr, pa_pt, pa_o, pa_oh, pa_ol = (
            sem("pa_s"), sem("pa_max"), sem("pa_exp"), sem("pa_p"), sem("pa_tr"), sem("pa_pt"),
            sem("pa_o"), sem("pa_oh"), sem("pa_ol"))
        f_silu, f_h, f_hh, f_hl, f_y = sem("f_silu"), sem("f_h"), sem("f_hh"), sem("f_hl"), sem("f_y")
        r_pe, r_act, r_dve = sem("r_pe"), sem("r_act"), sem("r_dve")
        LOGITS, RANKS, TURNED = 1, 2, 3
        TRIANGLE, EXPONENT = 1, 2
        DIFFERENCE, CHOSEN, GATES, COUNTED = 1, 2, 3, 4
        r_row, g_in = sem("r_row"), sem("g_in")
        row_st = sem("row_st")
        r_iota = sem("r_iota")
        t_tr, t_h, t_l = sem("t_tr"), sem("t_h"), sem("t_l")
        m_p, m_x, m_xe, m_pt, m_pte = (sem("m_p"), sem("m_x"), sem("m_xe"), sem("m_pt"), sem("m_pte"))
        m_silu, m_h, m_yh, m_yl, m_z, m_add = (sem("m_silu"), sem("m_h"), sem("m_yh"),
                                                    sem("m_yl"), sem("m_z"), sem("m_add"))
        m_yt, m_tr = sem("m_yt"), sem("m_tr")
        act_chain2, dve_chain2 = sem("act_chain2"), sem("dve_chain2")
        act_chain3, dve_chain3 = sem("act_chain3"), sem("dve_chain3")
        b_pe = sem("b_pe")
        b_beta, b_x, b_e, b_g, b_eg, b_rows, b_col = (
            sem("b_beta"), sem("b_x"), sem("b_e"), sem("b_g"), sem("b_eg"), sem("b_rows"),
            sem("b_col"))
        d_row, d_hist, d_s0, d_ext, d_z, d_conv, d_silu, d_cst, d_cso = (
            sem("d_row"), sem("d_hist"), sem("d_s0"), sem("d_ext"), sem("d_z"), sem("d_conv"), sem("d_silu"),
            sem("d_cst"), sem("d_cso"))
        d_sq, d_ss, d_std, d_qk, d_tm, d_tme, d_qg, d_egr = (sem("d_sq"), sem("d_ss"), sem("d_std"), sem("d_qk"),
                                                      sem("d_tm"), sem("d_tme"), sem("d_qg"), sem("d_egr"))
        d_at, d_tt, d_uu, d_log = sem("d_at"), sem("d_tt"), sem("d_uu"), sem("d_log")
        d_kk, d_arg, d_dt, d_bl, d_pt, d_pte, d_ut, d_ute, d_wt, d_wte = (
            sem("d_kk"), sem("d_arg"), sem("d_dt"), sem("d_bl"), sem("d_pt"), sem("d_pte"),
            sem("d_ut"), sem("d_ute"), sem("d_wt"), sem("d_wte"))
        d_vn, d_vne, d_o, d_s, d_oe = sem("d_vn"), sem("d_vne"), sem("d_o"), sem("d_s"), sem("d_oe")
        d_svt, d_svte, d_svn, d_svne, d_so, d_sds, d_ssn, d_kdm = (
            sem("d_svt"), sem("d_svte"), sem("d_svn"), sem("d_svne"), sem("d_so"), sem("d_sds"), sem("d_ssn"),
            sem("d_kdm"))
        d_osq, d_oss, d_ostd, d_on, d_yh, d_yl, d_sout = (
            sem("d_osq"), sem("d_oss"), sem("d_ostd"), sem("d_on"), sem("d_yh"), sem("d_yl"), sem("d_sout"))

        S_LRU = 0
        S_LOUT = S_LRU + 16
        S_KV = [S_LOUT + 8, None]
        S_Q = [S_KV[0] + 16, None]
        S_O = [S_Q[0] + 8, None]
        S_FFN = S_O[0] + 8
        S_GDN = S_FFN + HALVES * 36
        S_GOUT = S_GDN + 4 * GH
        S_KV[1] = S_GOUT + 8
        S_Q[1] = S_KV[1] + 16
        S_O[1] = S_Q[1] + 8
        S_MOE = S_O[1] + 8
        assert S_MOE + NE * 36 == SLOTS

        flat = lambda v: v.rearrange("p a b -> p (a b)")
        tk = carve()
        L_ext, L_rec, L_acc = tk(2, EXT), tk(2, T), tk(CONV)
        L_gw = tk(KT, P)
        L_r, L_i, L_gel = tk(2, T), tk(2, T), tk(2, T)
        L_a, L_t, L_b = tk(T), tk(T), tk(T)
        L_par, L_h0, L_hist = tk(2, 6), tk(2, NB), tk(2, NB * HIST)
        L_sp = tk(6, KT)
        L_cst, L_hst = tk(KT, HIST + NB * HIST), tk(KT, 1 + NB)

        tk = carve()
        A_q, A_k, A_v = tk(KT, T), tk(KT, MEM), tk(MT, D)
        A_ring = tk(2, 2048)
        A_mem = tk(KT, MEM)
        A_p = A_mem.rearrange("p a b -> p (a b)")[:, 0:4 * MEM].rearrange("p (a b) -> p a b", b=MEM)
        A_pt = A_mem.rearrange("p a b -> p (a b)")[:, 4 * MEM:].rearrange("p (a b) -> p a b", b=TP)
        A_ss, A_sp = tk(MT * P), tk(MT * P)
        A_spt = A_ss
        A_nm, A_rs = tk(4), tk(4)
        A_snm, A_srs = tk(1), tk(1)

        tk = carve()
        F_s, F_h, F_g = tk(2, T), tk(2, T), tk(T)
        R_l, R_m = tk(NT, 8), tk(NT, 8)
        R_i = tk(NT, 8).bitcast(mybir.dt.uint32)
        R_f, R_w, R_g, R_o, R_row = tk(NT, 8), tk(NT, 2), tk(NT, NE + 1), tk(NT, 8), tk(T)
        R_sel, R_pos, R_most = tk(NT, 8), tk(NT, NE + 1), tk(1)
        R_over = tk(1).bitcast(mybir.dt.int32)
        M_tri, M_iota = tk(P), tk(CAP)
        M_x, M_h, M_s, M_gcol, M_gate = tk(KT, CAP), tk(FT, CAP), tk(2, CAP), tk(NT, 1), tk(2)
        M_yt = F_s[:, :, 0:CAP]
        T_h = flat(hh)[:, 0:NT * D].rearrange("p (a b) -> p a b", b=D)
        T_l = flat(hl)[:, 0:NT * D].rearrange("p (a b) -> p a b", b=D)
        M_yh = flat(xh)[:, 0:2 * D].rearrange("p (a b) -> p a b", b=D)
        M_yl = flat(xl)[:, 0:2 * D].rearrange("p (a b) -> p a b", b=D)
        M_p = flat(xh)[:, 2 * D:2 * D + NT * CAP].rearrange("p (a b) -> p a b", b=CAP)
        M_pt = flat(xl)[:, 2 * D:2 * D + 2 * T].rearrange("p (a b) -> p a b", b=T)

        tk = carve()
        G_ext, G_acc = tk(3, EXT), tk(EXT)
        G_qkv, G_z = tk(3, T), tk(T)
        G_gc, G_be, G_eg = tk(T), tk(T), tk(T)
        G_rs = tk(2, T)
        G_vb, G_kb, G_kd = tk(NT, P), tk(NT, P), tk(NT, P)
        G_dt, G_at, G_bl, G_u, G_t = tk(NC, P), tk(NC, P), tk(2, NC, P), tk(NC, P), tk(NC, P)
        G_sdt, G_sat, G_sbl, G_su, G_st, G_spt, G_swt = (tk(NS), tk(NS), tk(NS), tk(NS), tk(NS), tk(NS), tk(NS))
        G_vn, G_s = tk(2, P), tk(2, P)
        G_svt, G_svn = tk(NS), tk(P)
        G_s0 = tk(NB, P)
        G_kdm = G_bl.rearrange("p a b c -> p (a b) c")
        G_hist, G_cst, G_hc, G_cw = tk(3, NB * HIST), tk(3, HIST + NB * HIST), tk(NT, 4), tk(3, CW)
        G_cols = tk(NT, 4, GH)
        G_wt = G_pt = tk(NC, P)
        G_ot = G_acc[:, 0:T]
        G_sq, G_qg = lnsq[:, 0, :], lnsq[:, 1, :]
        G_ors = lnr
        tk = carve()
        B_r = [tk(T) for _ in range(10)]

        nc_block = ctx.enter_context(nc.Block())

        @nc_block.sync
        def _(sp):
            sp.dma_start(x[:, :, :], I["xT"]).then_inc(ld_x, 16)

            def load(t, offset):
                for j in range(RAW):
                    if offset is None:
                        ge(sp, w_used, t * RAW + (j + 1 - RAW))
                    else:
                        ge(sp, w_split, t * RAW + (j + 1 - RAW - offset))
                    sp.dma_start(raw[:, j:j + 1, :, :], I["weights"][ds(t * RAW + j, 1)].rearrange(
                        "o p (k c) -> p o k c", k=KT)).then_inc(w_in[j], 16)

            def turns(slot, n, before, own):
                t0 = slot // RAW
                load(t0, before)
                if n > RAW:
                    with sp.Fori(t0 + 1, t0 + n // RAW) as t:
                        load(t, own)

            def cache(l):
                for i in range(2 * NB):
                    b = i % 2
                    if i < 2:
                        sp.wait_ge(ring_free, l + 1)
                    else:
                        sp.wait_ge(c_used, 2 * NB * l + i - 1)
                    sp.dma_start(A_ring[:, b, :], I["cache"][l, i]).then_inc(c_in[b], 16)

            for l in range(NL):
                d0, d1 = 16 * l, 16 * (l + 1)
                if l == 0:
                    turns(0, S_KV[0], 0, 0)
                else:
                    turns(S_FFN, S_KV[1] - S_FFN, d0, d0)
                turns(S_KV[l], 16, d0, None)
                turns(S_Q[l], 8, None, d1)
                turns(S_O[l], RAW, d1, d1)
                cache(l)
                turns(S_O[l] + RAW, RAW, d1, d1)
            turns(S_MOE, NE * 36, None, None)
            sp.wait_ge(out_done, 16 * N_OUT)

        @nc_block.gpsimd
        def _(pool):
            pool.wait_ge(ld_tab, 16)
            one_col = tc("ones", 0, 1).to_broadcast((P, KT * P))

            def split(t, first, offset):
                for j in range(RAW):
                    pool.wait_ge(w_in[j], t * 16 + 16)
                    ge(pool, w_used, t * RAW + (j + 1 - SPLIT - (first if j < SPLIT else 0)))
                    h1, l1, r1 = wh[:, j % SPLIT], wl[:, j % SPLIT], raw[:, j]
                    nc.gpsimd.tensor_tensor(flat(h1), flat(r1), one_col, MUL).then_inc(pool_hi, 1)
                    pool.wait_ge(pool_hi, t * RAW + (j + 1 - offset))
                    nc.gpsimd.tensor_tensor(flat(l1), flat(r1), flat(h1).bitcast(F), SUB).then_inc(w_split, 1)

            def turns(slot, n, first, offset):
                t0 = slot // RAW
                split(t0, first, offset)
                if n > RAW:
                    with pool.Fori(t0 + 1, t0 + n // RAW) as t:
                        split(t, 0, offset)
            turns(0, S_KV[0], 0, 0)
            turns(S_Q[0], S_KV[1] - S_Q[0], 16, 16)
            turns(S_Q[1], S_MOE - S_Q[1], 16, 32)
            pool.wait_ge(r_dve, COUNTED)
            over = pool.value_load(R_over[0:1, 0:1], min_val=0, max_val=1)
            with pool.If(over > 0):
                turns(S_MOE, NE * 36, 0, 32)
            pool.end_ifs()

        @nc_block.tensor
        def _(pe):
            mm = nc.tensor.matmul

            def lin_steps(slot, direct, par_, i, ah, al, fresh=None, per=6):
                pe.wait_ge(w_split, slot + (1 - direct))
                c = 0
                for n, (w, a) in enumerate(((wh, ah), (wl, ah), (wh, al))):
                    for k in range(KT):
                        if fresh is not None and n != 1:
                            pe.wait_ge(ln_xh if n == 0 else ln_xl, fresh + k + 1)
                        for h in range(2):
                            last = mm(ps[:, 2 * i + h, 0:HT], w[:, par_, k, :], a[:, k, h * HT:(h + 1) * HT],
                                      start=(n == 0 and k == 0), stop=(n == 2 and k == KT - 1))
                            c += 1
                            if c == 6 * KT:
                                last.then_inc(w_used, 1)
                            if c % per == 0:
                                yield

            def lin_tile(*args, **more):
                for _ in lin_steps(*args, **more):
                    pass

            def linear(slot, direct, ah, al, freed, base, fresh=None):
                for s in range(8):
                    if s >= 2:
                        pe.wait_ge(freed, base + s - 1)
                    lin_tile(slot + s, direct, s % 2, s % 2, ah, al, fresh=fresh if s == 0 else None)

            def layer_norm(n, l=None):
                pe.wait_ge(z_sum, n + 1)
                for h in range(2):
                    last = mm(ps[:, 4 + h, 0:HT], ones, lnsq[:, 0, h * HT:(h + 1) * HT], start=True, stop=True)
                last.then_inc(ln_sum, 1)
                if l is not None:
                    kv(l, 0, KV_EARLY)
                for k in range(KT):
                    pe.wait_ge(ln_sq, n * KT + k + 1)
                    for h in range(2):
                        last = mm(ps[:, 6 + h, 0:HT], ones, lnsq[:, k % 2, h * HT:(h + 1) * HT],
                                  start=(k == 0), stop=(k == KT - 1))
                    last.then_inc(ln_var, 1)
                if l is not None:
                    kv(l, KV_EARLY, 16)

            def kv(l, lo, hi):
                if lo == 0:
                    pe.wait_ge(mem_in, 16 * (l + 1))
                for s in range(lo, hi):
                    if s >= 2:
                        pe.wait_ge(kv_ev, 16 * l + s - 1)
                    slot = S_KV[l] + s
                    pe.wait_ge(w_in[slot % RAW], 16 * (slot // RAW + 1))
                    b, q = 2 * (s % 2), slot % RAW
                    if s < 8:
                        for k in range(KT):
                            last = mm(ps[:, b, 0:MEM], raw[:, q, k, :], A_mem[:, k, :], start=(k == 0), stop=(k == KT - 1))
                    else:
                        for mt in range(MT):
                            for k in range(KT):
                                last = mm(ps[:, b, mt * P:(mt + 1) * P], A_mem[:, k, mt * P:(mt + 1) * P], raw[:, q, k, :],
                                          start=(k == 0), stop=(k == KT - 1))
                    last.then_inc(w_used, 1)

            def attention(l):
                pe.wait_ge(kv_ev, 16 * (l + 1))
                linear(S_Q[l], 16 * (l + 1), xh, xl, q_ev, 8 * l, fresh=KT * 3 * l)
                pe.wait_ge(q_ev, 8 * (l + 1))

                def scores(b):
                    n = 2 * NB * l + b
                    pe.wait_ge(c_in[b % 2], (n // 2 + 1) * 16)
                    for mt in range(MT):
                        for h in range(XH):
                            for kk in range(2):
                                o = mt * P + h * NS + b * TS
                                last = mm(ps[:, 2, o:o + TS],
                                          A_ring[:, b % 2, (2 * h + kk) * MEM + mt * P:(2 * h + kk) * MEM + (mt + 1) * P],
                                          A_q[:, 2 * h + kk, TP + b * TS:TP + (b + 1) * TS],
                                          start=(kk == 0), stop=(kk == 1))
                    last.then_inc(c_used, 1)

                def values(b):
                    n = 2 * NB * l + NB + b
                    pe.wait_ge(c_in[b % 2], (n // 2 + 1) * 16)
                    for dt in range(KT):
                        for mt in range(MT):
                            o = mt * P + (dt // 2) * NS + b * TS
                            last = mm(ps[:, 3, dt * NS + b * TS:dt * NS + (b + 1) * TS],
                                      A_ring[:, b % 2, mt * D + dt * P:mt * D + (dt + 1) * P],
                                      A_spt[:, o:o + TS], start=(mt == 0), stop=(mt == MT - 1))
                    last.then_inc(c_used, 1)

                for h in range(XH):
                    n = XH * l + h
                    one_seq = scores if h < 2 else values
                    if h:
                        pe.wait_ge(pa_exp, 4 * n)
                    for tt in range(4):
                        for kk in range(2):
                            last = mm(ps[:, 4 + tt // 2, (tt % 2) * MEM:(tt % 2 + 1) * MEM],
                                      A_q[:, 2 * h + kk, tt * P:(tt + 1) * P], A_k[:, 2 * h + kk, :],
                                      start=(kk == 0), stop=(kk == 1))
                    last.then_inc(pa_s, 1)
                    if h == 2:
                        pe.wait_ge(ss_ev, l + 1)
                        for mt in range(MT):
                            last = nc.tensor.transpose(ps[:, 3, mt * P:(mt + 1) * P], A_ss[:, mt * P:(mt + 1) * P], ident)
                        last.then_inc(ss_tr, 1)
                    else:
                        for b in range(2):
                            one_seq(4 * (h % 2) + b)
                    pe.wait_ge(pa_p, n + 1)
                    for tt in range(4):
                        for mt in range(MT):
                            last = nc.tensor.transpose(ps[:, 6 + mt, tt * P:(tt + 1) * P], A_p[:, tt, mt * P:(mt + 1) * P], ident)
                    last.then_inc(pa_tr, 1)
                    if h == 2:
                        pe.wait_ge(ss_p, l + 1)
                        for mt in range(MT):
                            last = nc.tensor.transpose(ps[:, 2, mt * P:(mt + 1) * P], A_sp[:, mt * P:(mt + 1) * P], ident)
                        last.then_inc(ss_ptr, 1)
                        pe.wait_ge(ss_pt, l + 1)
                        for b in range(4):
                            values(b)
                    else:
                        for b in range(2, 4):
                            one_seq(4 * (h % 2) + b)
                    pe.wait_ge(pa_pt, n + 1)
                    if h:
                        pe.wait_ge(pa_ol, n)
                    for dt in range(2):
                        for mt in range(MT):
                            last = mm(ps[:, dt, :], A_v[:, mt, (2 * h + dt) * P:(2 * h + dt + 1) * P], A_pt[:, mt, :],
                                      start=(mt == 0), stop=(mt == MT - 1))
                    last.then_inc(pa_o, 1)
                pe.wait_ge(ss_ol, l + 1)
                pe.wait_ge(pa_ol, XH * (l + 1))
                linear(S_O[l], 16 * (l + 1), xh, xl, z_ready, KT * (2 * l + 1))

            def experts(n, slot, direct, e0, first_ln):
                def one(e):
                    e36, e12, e8 = e * 36 + slot, (e + e0) * FT, (e + e0) * KT

                    def up(g):
                        for j in range(4):
                            if j % 2 == 0:
                                ge(pe, f_h, e12 + g * 2 + (j // 2 - 1))
                            lin_tile(e36 + g * 4 + j, direct, j % 2, j, xh, xl,
                                     fresh=KT * (first_ln - 1) if j == 0 and isinstance(g, int) and isinstance(e, int) else None)
                    ge(pe, f_y, e8)
                    pe.sem_inc(passed, 1)
                    if isinstance(e, int) and e == 0:
                        up(0)
                        with pe.Fori(1, FT // 2) as g:
                            up(g)
                    else:
                        with pe.Fori(0, FT // 2) as g:
                            up(g)
                    pe.wait_ge(f_hl, e12 + FT)

                    def down(g):
                        for q in range(4 * FT):
                            d, f = divmod(q, FT)
                            s, k = divmod(q, KT)
                            if k == 0:
                                pe.wait_ge(w_split, e36 + g * 6 + (24 + s + 1 - direct))
                            if f == 0:
                                ge(pe, f_y, e8 + g * 4 + (d - 3))
                            w_parts = ((wh, hh), (wh, hl), (wl, hh))
                            for m, (w, a) in enumerate(w_parts):
                                for h in range(2):
                                    last = mm(ps[:, 2 * d + h, 0:HT], w[:, s % 2, k, :], a[:, f, h * HT:(h + 1) * HT],
                                              start=(f == 0 and m == 0), stop=(f == FT - 1 and m == 2))
                            if k == KT - 1:
                                last.then_inc(w_used, 1)
                    pe.sem_inc(passed, 1)
                    if isinstance(e, int) and e + e0 == 0:
                        down(0)
                        down(1)
                    else:
                        with pe.Fori(0, 2) as g:
                            down(g)
                repeat(pe, n, one)

            pe.wait_ge(x_split_l, KT)

            def lru(b):
                for j in range(2):
                    ge(pe, lru_gelu, b * 2 + (j - 1))
                    lin_tile(b * 4 + j, 0, j, j, xh, xl)
                for j in range(2):
                    pe.wait_ge(lru_ext, b * 2 + (j + 1))
                    lin_tile(b * 4 + (2 + j), 0, j, j, xh, xl)
                pe.wait_ge(lru_gw_in, b * 16 + 16)
                pe.wait_ge(lru_conv, b * 2 + 2)
                for g in range(4):
                    ge(pe, lru_gate_ev, b * 4 + (g - 1))
                    for k in range(2):
                        for h in range(2):
                            last = mm(ps[:, 4 + 2 * (g % 2) + h, 0:HT], L_gw[:, 4 * k + g, :],
                                      L_rec[:, k, h * HT:(h + 1) * HT], start=(k == 0), stop=(k == 1))
                    last.then_inc(lru_gate_full, 1)
            repeat(pe, BLK, lru)
            pe.wait_ge(lru_y, 8)
            pe.wait_ge(lru_gelu, 8)
            linear(S_LOUT, 0, hh, hl, z_ready, 0)
            layer_norm(0, 0)
            attention(0)
            layer_norm(1)
            experts(HALVES, S_FFN, 16, 0, 2)
            pe.wait_ge(f_y, KT * HALVES)
            layer_norm(2)
            pe.wait_ge(ln_xl, KT * 3)
            for g in range(2):
                for k in range(KT):
                    for h in range(2):
                        last = mm(ps[0:GH, 4 + 2 * g + h, 0:HT], pc("wba", 16 * k + 8 * g, 16 * k + 8 * g + 8),
                                  x[:, k, h * HT:(h + 1) * HT], start=(k == 0), stop=(k == KT - 1))
            last.then_inc(b_pe, 1)
            pe.wait_ge(b_rows, 1)
            for tt in range(NT):
                n = P if tt < NC else NS
                for r in range(4):
                    last = nc.tensor.transpose(ps[0:n, 4, (tt * 4 + r) * GH:(tt * 4 + r + 1) * GH],
                                               B_r[r][0:GH, tt * P:tt * P + n], ident[0:GH, 0:GH])
            last.then_inc(b_pe, 1)
            pe.wait_ge(b_col, 2)

            def project(h, per=6):
                for j in range(4):
                    if j == 0:
                        ge(pe, d_ext, h * 3)
                        ge(pe, d_std, h * 2)
                        ge(pe, d_ostd, h - 1)
                    elif j == 1:
                        ge(pe, d_z, h)
                    else:
                        pe.wait_ge(d_ext, h * 3 + (j - 1))
                    yield from lin_steps(h * 4 + (S_GDN + j), 16, j % 2, j % 2, xh, xl, per=per)

            def lengths(h, j):
                pe.wait_ge(d_sq, h * 2 + (j + 1))
                if j == 0:
                    pe.wait_ge(d_ext, h * 3 + 3)
                else:
                    pe.wait_ge(d_log, h * 2 + 1)
                for hf in range(2):
                    last = mm(ps[:, hf, 0:HT], ones, G_rs[:, j, hf * HT:(hf + 1) * HT], start=True, stop=True)
                last.then_inc(d_ss, 1)

            def head(h, ahead=True):
                following = project(h + 1) if ahead else iter(())

                def fill(n):
                    for _ in range(n):
                        next(following, None)

                ge(pe, d_ssn, h)
                pe.wait_ge(d_silu, h * 3 + 3)
                pe.wait_ge(d_qk, h * 2 + 2)
                for j in range(2):
                    for c in range(NC):
                        nc.tensor.transpose(ps[:, 4 + 2 * j, c * P:(c + 1) * P], G_qkv[:, 1 + j, c * P:(c + 1) * P], ident)
                    last = nc.tensor.transpose(ps[0:NS, 5 + 2 * j, 0:P], G_qkv[:, 1 + j, TP:T], ident)
                    last.then_inc(d_tm, 1)
                for j in range(2):
                    pe.wait_ge(d_tme, h * 2 + (j + 1))
                    for c in range(NC):
                        mm(ps[:, 4 + 2 * j, c * P:(c + 1) * P], G_qkv[:, 1, c * P:(c + 1) * P],
                           G_qkv[:, 1 - j, c * P:(c + 1) * P], start=True, stop=True)
                    last = mm(ps[0:NS, 5 + 2 * j, 0:NS], G_qkv[:, 1, TP:T], G_qkv[:, 1 - j, TP:T], start=True, stop=True)
                    last.then_inc(d_kk, 1)
                pe.wait_ge(d_bl, h * LEVELS + 1)
                pe.wait_ge(d_at, h + 1)
                for c in range(NC):
                    nc.tensor.transpose(ps[:, 5, c * P:(c + 1) * P], G_bl[:, 0, c, :], ident)
                nc.tensor.transpose(ps[0:NS, 7, 0:NS], G_sbl[0:NS, :], ident[0:NS, 0:NS]).then_inc(d_pt, 1)
                fill(2)
                for v in range(1, LEVELS):
                    small = v < SLEVELS
                    pe.wait_ge(d_bl, h * LEVELS + (v + 1))
                    pe.wait_ge(d_tt, h * (LEVELS - 1) + v)
                    for c in range(NC):
                        last = mm(ps[:, 4, c * P:(c + 1) * P], G_bl[:, v % 2, c, :], G_t[:, c, :], start=True, stop=True)
                    if small:
                        last = mm(ps[0:NS, 7, 0:NS], G_sbl[0:NS, :], G_st[0:NS, :], start=True, stop=True)
                    last.then_inc(d_pt, 1)
                    fill(2)
                    pe.wait_ge(d_pte, h * (LEVELS - 1) + v)
                    pe.wait_ge(d_ute, h * LEVELS + v)
                    if v < LEVELS - 1:
                        for c in range(NC):
                            last = mm(ps[:, 5, c * P:(c + 1) * P], G_u[:, c, :], G_pt[:, c, :], start=True, stop=True)
                        last.then_inc(d_ut, 1)
                    for c in range(NC):
                        last = mm(ps[:, 6, c * P:(c + 1) * P], G_pt[:, c, :], G_u[:, c, :], start=True, stop=True)
                    if small:
                        last = mm(ps[0:NS, 7, 32:32 + NS], G_spt[0:NS, :], G_su[0:NS, :], start=True, stop=True)
                    last.then_inc(d_uu, 1)
                    fill(2)
                pe.wait_ge(d_ute, h * LEVELS + LEVELS)
                for c in range(NC):
                    mm(ps[:, 4, c * P:(c + 1) * P], G_kb[:, c, :], G_u[:, c, :], start=True, stop=True)
                last = mm(ps[:, 5, 0:NS], G_kb[0:NS, NC, :], G_su[0:NS, :], start=True, stop=True)
                last.then_inc(d_wt, 1)
                fill(2)
                pe.wait_ge(d_wte, h + 1)
                pe.wait_ge(d_qg, h + 1)
                for c in range(NC):
                    if c:
                        pe.wait_ge(d_s, h * NC + c)
                    last = mm(ps[:, 6, c * P:(c + 1) * P], G_u[:, c, :], G_vb[:, c, :], start=True, stop=(c == 0))
                    if c:
                        last = mm(ps[:, 6, c * P:(c + 1) * P], G_wt[:, c, :], G_s[:, (c + 1) % 2, :], start=False, stop=True)
                    last.then_inc(d_vn, 1)
                    fill(1)
                    pe.wait_ge(d_vne, h * NC + (c + 1))
                    last = mm(ps[:, 4, c * P:(c + 1) * P], G_kd[:, c, :], G_vn[:, c % 2, :], start=True, stop=True)
                    last.then_inc(d_o, 1)
                    mm(ps[:, 7, c * P:(c + 1) * P], G_vn[:, c % 2, :], G_at[:, c, :], start=True, stop=(c == 0))
                    if c:
                        mm(ps[:, 7, c * P:(c + 1) * P], G_s[:, (c + 1) % 2, :], G_qg[:, c * P:(c + 1) * P], start=False, stop=True)
                fill(100)
                if ahead:
                    lengths(h + 1, 0)
                pe.wait_ge(d_s0, h * 16 + 16)
                for b in range(NB):
                    mm(ps[:, 5, 64 + b * TS:64 + (b + 1) * TS], G_s0[:, b, :], G_swt[:, b * TS:(b + 1) * TS],
                       start=(b == 0), stop=False)
                last = mm(ps[:, 5, 64:64 + NS], G_vb[0:NS, NC, :], G_su[0:NS, :], start=False, stop=True)
                last.then_inc(d_svt, 1)
                pe.wait_ge(d_svte, h + 1)
                nc.tensor.transpose(ps[0:NS, 5, 128:256], G_svt, ident).then_inc(d_svn, 1)
                pe.wait_ge(d_svne, h + 1)
                for b in range(NB):
                    mm(ps[:, 5, 256 + b * TS:256 + (b + 1) * TS], G_s0[:, b, :],
                       G_qg[:, TP + b * TS:TP + (b + 1) * TS], start=(b == 0), stop=False)
                last = mm(ps[:, 5, 256:256 + NS], G_svn[0:NS, :], G_sat[0:NS, :], start=False, stop=True)
                last.then_inc(d_so, 1)
                if ahead:
                    lengths(h + 1, 1)
                pe.wait_ge(d_kdm, h + 1)
                pe.wait_ge(d_s, h * NC + NC)
                for b in range(NB):
                    last = mm(ps[:, 4 + 2 * (b // 4), (b % 4) * P:(b % 4 + 1) * P], G_kdm[0:NS, b, :], G_svn[0:NS, :],
                              start=True, stop=True)
                last.then_inc(d_sds, 1)
                pe.wait_ge(d_osq, h + 1)
                if ahead:
                    pe.wait_ge(d_log, h * 2 + 4)
                for hf in range(2):
                    last = mm(ps[:, hf, 0:HT], ones, G_sq[:, hf * HT:(hf + 1) * HT], start=True, stop=True)
                last.then_inc(d_oss, 1)
            for _ in project(0):
                pass
            for j in range(2):
                lengths(0, j)
            repeat(pe, GH - 1, head)
            head(GH - 1, ahead=False)
            pe.wait_ge(d_yl, GH)
            pe.wait_ge(d_z, GH)
            linear(S_GOUT, 16, hh, hl, z_ready, KT * 2)
            layer_norm(3, 1)
            attention(1)
            layer_norm(4)
            def turn_tokens(lo, hi):
                for n in range(lo, hi):
                    tt, hf = divmod(n, 2)
                    w = P if tt < NC else NS
                    if n >= 8:
                        pe.wait_ge(t_l, n - 7)
                    for k in range(4):
                        last = nc.tensor.transpose(ps[0:w, TBANK[n], k * P:(k + 1) * P], x[:, 4 * hf + k, tt * P:tt * P + w], ident)
                    last.then_inc(t_tr, 1)

            pe.wait_ge(ln_xl, KT * 5)
            for tt in range(NT):
                n = P if tt < NC else NS
                for k in range(KT):
                    last = mm(ps[0:n, 4, tt * 8:tt * 8 + 8], x[:, k, tt * P:tt * P + n], pc("router", 8 * k, 8 * k + 8),
                              start=(k == 0), stop=(k == KT - 1))
            last.then_inc(r_pe, 1)
            turn_tokens(0, EARLY)
            pe.wait_ge(r_act, TRIANGLE)
            pe.wait_ge(r_dve, CHOSEN)
            for tt in range(NT):
                n = P if tt < NC else NS
                for u in range(tt):
                    mm(ps[0:n, 5, tt * 8:tt * 8 + 8], ones[:, 0:n], R_sel[:, u, :], start=(u == 0), stop=False)
                mm(ps[0:n, 5, tt * 8:tt * 8 + 8], M_tri[0:n, 0:n], R_sel[0:n, tt, :], start=(tt == 0), stop=True)
            for tt in range(NT):
                n = P if tt < NC else NS
                last = mm(ps[:, 5, 64:72], ones[0:n, :], R_sel[0:n, tt, :], start=(tt == 0), stop=(tt == NT - 1))
            last.then_inc(r_pe, 1)

            def gathered(e):
                t9, e12, e8 = e * 9 + S_MOE // RAW, e * FT, e * KT
                pe.wait_ge(m_p, e + 1)
                for k in range(KT):
                    if k >= 2:
                        pe.wait_ge(m_xe, e8 + (k - 1))
                    for tt in range(NT):
                        n = P if tt < NC else NS
                        for u in (T_h, T_l):
                            last = mm(ps[:, 2 + k % 2, 0:CAP], u[0:n, tt, k * P:(k + 1) * P], M_p[0:n, tt, :],
                                      start=(tt == 0 and u is T_h), stop=(tt == NT - 1 and u is T_l))
                    last.then_inc(m_x, 1)
                ge(pe, m_add, e8)
                for i, (c, w) in enumerate(CT):
                    b = 4 + 2 * i
                    for tt in range(NT):
                        n = P if tt < NC else NS
                        nc.tensor.transpose(ps[0:w, b + tt // NC, (tt % NC) * P:(tt % NC) * P + n],
                                            M_p[0:n, tt, c:c + w].bitcast(F), ident[0:n, 0:n])
                    for tt in range(NT):
                        n = P if tt < NC else NS
                        last = mm(ps[0:w, b + 1, NS:NS + 1], M_p[0:n, tt, c:c + w].bitcast(F), M_gcol[0:n, tt, :],
                                  start=(tt == 0), stop=(tt == NT - 1))
                last.then_inc(m_pt, 1)
                pe.wait_ge(m_xe, e8 + KT)
                pe.sem_inc(passed, 1)

                def up(g):
                    for j in range(RAW):
                        if j % 2 == 0:
                            ge(pe, m_h, e12 + g * 2 + (j // 2 - 1))
                        pe.wait_ge(w_in[j], t9 * 16 + g * 16 + 16)
                        for k in range(KT):
                            last = mm(ps[:, j // 2, (j % 2) * CAP:(j % 2 + 1) * CAP], raw[:, j, k, :], M_x[:, k, :],
                                      start=(k == 0), stop=(k == KT - 1))
                        last.then_inc(w_used, 1)
                if isinstance(e, int):
                    up(0)
                    with pe.Fori(1, FT // 2) as g:
                        up(g)
                else:
                    with pe.Fori(0, FT // 2) as g:
                        up(g)
                pe.wait_ge(m_h, e12 + FT)

                def turn(d):
                    pe.wait_ge(m_yt, e8 + (d + 1))
                    if d >= 2:
                        pe.wait_ge(m_yl, e8 + (d - 1))
                    for i, (c, w) in enumerate(CT):
                        last = nc.tensor.transpose(ps[0:w, d % 2, i * P:(i + 1) * P], M_yt[:, d % 2, c:c + w], ident)
                    last.then_inc(m_tr, 1)

                for q in range(KT * FT):
                    d, f = divmod(q, FT)
                    sl, k = divmod(q, KT)
                    if k == 0:
                        pe.wait_ge(w_in[sl % RAW], t9 * 16 + (16 * (6 + sl // RAW) + 16))
                    if f == 0 and d >= 2:
                        pe.wait_ge(m_yt, e8 + (d - 1))
                    last = mm(ps[:, 2 + d % 2, 0:CAP], raw[:, sl % RAW, k, :], M_h[:, f, :],
                              start=(f == 0), stop=(f == FT - 1))
                    if k == KT - 1:
                        last.then_inc(w_used, 1)
                    if f == FT // 2 and d:
                        turn(d - 1)
                turn(KT - 1)
                pe.wait_ge(m_pte, e + 1)
                for d in range(KT):
                    pe.wait_ge(m_yl, e8 + (d + 1))
                    if d >= 2:
                        pe.wait_ge(m_add, e8 + (d - 1))
                    for h in range(2):
                        for i, (c, w) in enumerate(CT):
                            for u in (M_yh, M_yl):
                                last = mm(ps[:, 4 + 2 * (d % 2) + h, 0:HT], u[0:w, i, d * P:(d + 1) * P],
                                          M_pt[0:w, i, h * HT:(h + 1) * HT],
                                          start=(i == 0 and u is M_yh), stop=(i == 1 and u is M_yl))
                    last.then_inc(m_z, 1)

            pe.wait_ge(r_dve, COUNTED)
            over = pe.value_load(R_over[0:1, 0:1], min_val=0, max_val=1)
            with pe.If(over > 0):
                pe.wait_ge(r_dve, GATES)
                for tt in range(NC):
                    nc.tensor.transpose(ps[0:NE, 5, tt * P:(tt + 1) * P], R_g[:, tt, 0:NE], ident)
                nc.tensor.transpose(ps[0:NE, 6, 0:NS], R_g[0:NS, NC, 0:NE], ident[0:NS, 0:NS]).then_inc(r_pe, 1)
                pe.wait_ge(r_row, 2)
                experts(NE, S_MOE, 32, HALVES, 5)
                pe.wait_ge(f_y, KT * (HALVES + NE))
            with pe.Else():
                turn_tokens(EARLY, 2 * NT)
                pe.wait_ge(t_l, 2 * NT)
                repeat(pe, NE, gathered)
            pe.end_ifs()
            layer_norm(5)

        @nc_block.scalar
        def _(act):
            A = nc.scalar.activation
            s = Serial(act, act_chain)
            act.dma_start(tab[:, :], I["tables"]).then_inc(ld_tab, 16)
            act.dma_start(par[:, :], I["params"]).then_inc(ld_par, 16)
            act.wait_ge(ld_x, 16)
            for k in range(KT):
                s(A(xh[:, k, :], x[:, k, :], ACT.Copy), x_split_h, k + 1)
            act.wait_ge(ld_par, 16)
            act.wait_ge(ld_tab, 16)

            def layer_norm(n, l=None):
                act.preload_act_table_set("natural_log_exp_and_others")
                for k in range(KT):
                    act.wait_ge(ln_d, n * KT + k + 1)
                    if k >= 2:
                        act.wait_ge(ln_var, n * KT + k - 1)
                    s(A(lnsq[:, k % 2, :], x[:, k, :], ACT.Square), ln_sq, n * KT + k + 1)
                    if l is not None and k < KV_EARLY:
                        kv(l, k)
                act.wait_ge(ln_var, n * KT + KT)
                s(A(two(lnr[:, :]), pair(3), ACT.Ln, bias=pc("eps5"), scale=1.0 / D))
                s(A(lnr[:, :], lnr[:, :], ACT.Exp, scale=-0.5), ln_std, n + 1)
                for k in range(KT):
                    act.wait_ge(ln_n, n * KT + k + 1)
                    if n < NLN - 1:
                        s(A(xh[:, k, :], x[:, k, :], ACT.Identity, bias=pc("lnb", n * 8 + k, n * 8 + k + 1),
                            scale=pc("lng", n * 8 + k, n * 8 + k + 1)), ln_xh, n * KT + k + 1)
                    s(A(x[:, k, :], x[:, k, :], ACT.Identity, bias=pc("lnb", n * 8 + k, n * 8 + k + 1),
                        scale=pc("lng", n * 8 + k, n * 8 + k + 1)), ln_x, n * KT + k + 1)
                    if l is not None:
                        kv(l, KV_EARLY + k)
                    if n == NLN - 1 and k % 4 == 3:
                        act.dma_start(O["y"][:, k - 3:k + 1, :], x[:, k - 3:k + 1, :]).then_inc(out_done, 16)
                if l is not None:
                    for t in range(KV_EARLY + KT, 16):
                        kv(l, t)
                    act.dma_start(O["mem_k"][l], A_k).then_inc(out_done, 16)
                    act.dma_start(O["mem_v"][l], A_v).then_inc(out_done, 16)

            def kv_start(l):
                act.dma_start(A_mem, I["memT"].rearrange("p (a b) -> p a b", b=MEM)).then_inc(mem_in, 16)
                act.sem_inc(ring_free, 1)

            def kv(l, t):
                act.wait_ge(w_used, S_KV[l] + t + 1)
                if t < 8:
                    s(A(A_k[:, t, :], ps[:, 2 * (t % 2), 0:MEM], ACT.Copy), kv_ev, 16 * l + t + 1)
                else:
                    s(A(A_v[:, :, (t - 8) * P:(t - 7) * P], ps[:, 2 * (t % 2), 0:MEM].rearrange("p (a b) -> p a b", b=P),
                        ACT.Copy), kv_ev, 16 * l + t + 1)

            def attention(l):
                for t in range(8):
                    act.wait_ge(w_used, S_Q[l] + t + 1)
                    s(A(two(A_q[:, t, :]), pair(t % 2), ACT.Copy, scale=XD ** -0.5), q_ev, 8 * l + t + 1)
                for h in range(XH):
                    n = XH * l + h
                    act.wait_ge(pa_max, n + 1)
                    for tt in range(4):
                        s(A(A_p[:, tt, :], ps[:, 4 + tt // 2, (tt % 2) * MEM:(tt % 2 + 1) * MEM], ACT.Exp,
                            bias=A_nm[:, tt:tt + 1], accum_out=A_rs[:, tt:tt + 1]), pa_exp, 4 * n + tt + 1)
                    if h == 2:
                        act.wait_ge(ss_max, l + 1)
                        s(A(A_sp, ps[:, 3, 0:MEM], ACT.Exp, bias=A_snm, accum_out=A_srs), ss_exp, l + 1)
                    act.wait_ge(pa_tr, n + 1)
                    s(A(A_pt, ps[:, 6:8, :], ACT.Copy), pa_pt, n + 1)
                    if h == 1:
                        act.wait_ge(c_used, 2 * NB * l + NB)
                        s(A(A_ss, ps[:, 2, 0:MT * P], ACT.Copy), ss_ev, l + 1)
                    if h == 2:
                        act.wait_ge(ss_ptr, l + 1)
                        s(A(A_spt, ps[:, 2, 0:MT * P], ACT.Copy), ss_pt, l + 1)
                    act.wait_ge(pa_o, n + 1)
                    s(A(xh[:, 2 * h:2 * h + 2, 0:TP], ps[:, 0:2, :], ACT.Copy), pa_oh, n + 1)
                act.wait_ge(c_used, 2 * NB * (l + 1))
                s(A(xh[:, :, TP:T], ps[:, 3, 0:KT * NS].rearrange("p (a b) -> p a b", b=NS), ACT.Copy), ss_oh, l + 1)

            def experts(n, slot, e0, gated):
                def one(e):
                    e36, e12 = e * 36 + slot, (e + e0) * FT

                    def up(g):
                        for j in range(2):
                            act.wait_ge(w_used, e36 + g * 4 + (2 * j + 1))
                            ge(act, f_h, e12 + g * 2 + (j - 1))
                            s(A(two(F_s[:, j, :]), pair(2 * j), ACT.Silu), f_silu, e12 + g * 2 + (j + 1))
                            act.wait_ge(f_h, e12 + g * 2 + (j + 1))
                            s(A(hh[:, ds(g * 2 + j, 1), :], F_h[:, j:j + 1, :], ACT.Copy), f_hh, e12 + g * 2 + (j + 1))
                    repeat(act, FT // 2, up, s, passed)
                repeat(act, n, one, s)

            lgw = I["lru_gate"]

            act.wait_ge(lru_sp, 1)
            s(A(L_sp[:, 1, :], L_sp[:, 0, :], ACT.Exp, scale=-1.0), lru_spe, 1)

            def lru_row(b, j):
                act.wait_ge(w_used, b * 4 + (j + 1))
                ge(act, lru_cst, b * 2 + (j - 1))
                s(A(L_ext[:, j, HIST:HIST + HT], ps[:, 2 * j, 0:HT], ACT.Copy))
                s(A(L_ext[:, j, HIST + HT:HIST + TP], ps[:, 2 * j + 1, 0:TP - HT], ACT.Copy))
                s(A(L_ext[:, j, EXTP:EXT].rearrange("p (a b) -> p a b", b=SEG)[:, :, HIST:SEG],
                    ps[:, 2 * j + 1, TP - HT:HT].rearrange("p (a b) -> p a b", b=TS), ACT.Copy),
                  lru_ext, b * 2 + (j + 1))

            for j in range(2):
                lru_row(0, j)

            def lru(b, ahead=True):
                ge(act, lru_gate_full, b * 4)
                act.dma_start(L_gw.rearrange("p (o a) b -> p o a b", o=1),
                              lgw[ds(b, 1)].rearrange("o p (a b) -> p o a b", a=KT)).then_inc(lru_gw_in, 16)
                for j in range(2):
                    act.wait_ge(w_used, b * 4 + (2 + j + 1))
                    ge(act, lru_y, b * 2 + (j - 1))
                    s(A(two(L_gel[:, j, :]), pair(j), ACT.Gelu_apprx_tanh), lru_gelu, b * 2 + (j + 1))
                ge(act, lru_dve, b * 10)
                for g in range(4):
                    act.wait_ge(lru_gate_full, b * 4 + (g + 1))
                    dst = (L_r, L_i)[g // 2]
                    s(A(two(dst[:, g % 2, :]), pair(2 + g % 2), ACT.Sigmoid, bias=L_par[:, g % 2, 4 + g // 2:5 + g // 2]),
                      lru_gate_ev, b * 4 + (g + 1))
                for j in range(2):
                    act.wait_ge(lru_dve, b * 10 + (6 * j + 1))
                    s(A(L_a, L_r[:, j, :], ACT.Exp, scale=-1.0))
                    s(A(L_t, L_r[:, j, :], ACT.Tanh), lru_act, b * 4 + (2 * j + 1))
                    if ahead:
                        lru_row(b + 1, j)
                    act.wait_ge(lru_dve, b * 10 + (3 * j + 5))
                    s(A(L_t, L_t, ACT.Sqrt), lru_act, b * 4 + (2 * j + 2))
                    act.wait_ge(lru_dve, b * 10 + (3 * j + 7))
                    s(A(hh[:, ds(b * 2 + j, 1), :], L_b.rearrange("p (o c) -> p o c", o=1), ACT.Copy), lru_yh, b * 2 + (j + 1))
            repeat(act, BLK - 1, lru, s)
            lru(BLK - 1, ahead=False)
            act.wait_ge(lru_y, 8)
            act.dma_start(O["lru_conv"], L_cst).then_inc(out_done, 16)
            act.dma_start(O["lru_h"], L_hst).then_inc(out_done, 16)
            act.wait_ge(out_done, 32)
            kv_start(0)
            layer_norm(0, 0)
            attention(0)
            layer_norm(1)
            act.wait_ge(out_done, 64)
            experts(HALVES, S_FFN, 0, False)
            layer_norm(2)

            act.wait_ge(b_pe, 1)
            s(A(two(B_r[1])[0:GH], pair(2)[0:GH], ACT.Sigmoid), b_beta, 1)
            act.wait_ge(b_x, 1)
            s(A(B_r[5][0:GH, :], B_r[5][0:GH, :], ACT.Exp, scale=-1.0))
            s(A(B_r[9][0:GH, 0:1], pc("alog")[0:GH, :], ACT.Exp), b_e, 1)
            act.wait_ge(b_g, 1)
            s(A(B_r[2][0:GH, :], B_r[0][0:GH, :], ACT.Exp))
            s(A(B_r[3][0:GH, :], B_r[3][0:GH, :], ACT.Exp), b_eg, 1)
            act.wait_ge(b_rows, 1)
            for r in range(2):
                act.dma_start(I["scratch"][r], B_r[r][0:GH, :]).then_inc(row_st, 16)
            act.wait_ge(row_st, 32)

            def ext(h, j):
                act.wait_ge(w_used, h * 4 + (S_GDN + j + 1))
                bk = 2 * (j % 2)
                s(A(G_ext[:, j, HIST:HIST + HT], ps[:, bk, 0:HT], ACT.Copy))
                s(A(G_ext[:, j, HIST + HT:HIST + TP], ps[:, bk + 1, 0:TP - HT], ACT.Copy))
                s(A(G_ext[:, j, EXTP:EXT].rearrange("p (a b) -> p a b", b=SEG)[:, :, HIST:SEG],
                    ps[:, bk + 1, TP - HT:HT].rearrange("p (a b) -> p a b", b=TS), ACT.Copy), d_ext, h * 3 + (j + 1))

            def gate_z(h):
                act.wait_ge(w_used, h * 4 + (S_GDN + 4))
                s(A(two(G_z), pair(1), ACT.Silu), d_z, h + 1)

            def rows(h):
                for r, dst in enumerate((G_gc, G_be)):
                    act.dma_start(dst, I["scratch"][r, ds(h, 1), :].to_broadcast((P, T))).then_inc(d_row, 16)
                act.dma_start(G_hist, I["gdn_hist"][ds(h, 1)].rearrange("o p (a b) -> p (o a) b", a=3)).then_inc(d_hist, 16)

            act.wait_ge(b_col, 2)
            rows(0)
            for j in range(3):
                ext(0, j)
            gate_z(0)

            def silu(h, j):
                act.wait_ge(d_conv, h * 3 + (j + 1))
                s(A(G_qkv[:, j, :], G_qkv[:, j, :], ACT.Silu), d_silu, h * 3 + (j + 1))
                if j < 2:
                    s(A(G_rs[:, j, :], G_qkv[:, j, :], ACT.Square), d_sq, h * 2 + (j + 1))

            def log_length(h, j):
                act.wait_ge(d_ss, h * 2 + (j + 1))
                s(A(two(G_rs[:, j, :]), pair(0), ACT.Ln, bias=pc("eps6")), d_log, h * 2 + (j + 1))

            def unit(h):
                for j in range(2):
                    s(A(G_rs[:, j, :], G_rs[:, j, :], ACT.Exp, scale=-0.5), d_std, h * 2 + (j + 1))

            def grow(h):
                act.wait_ge(d_row, h * 32 + 32)
                s(A(G_eg, G_gc, ACT.Exp), d_egr, h + 1)

            def decay(h):
                act.wait_ge(d_arg, h + 1)
                s(A(G_dt, G_dt, ACT.Exp))
                s(A(G_sdt[0:NS, :], G_sdt[0:NS, :], ACT.Exp), d_dt, h + 1)

            for j in range(3):
                silu(0, j)
            for j in range(2):
                log_length(0, j)
            unit(0)
            decay(0)
            grow(0)

            def head(h, ahead=True):
                ge(act, d_sout, h * 32)
                act.dma_start(G_s0, I["gdn_s0"][ds(h, 1)].rearrange("o p (a b) -> p (o a) b", a=NB)).then_inc(d_s0, 16)
                ge(act, d_cso, h * 16)
                s(A(G_cst[:, :, 0:HIST], G_ext[:, :, TP:EXTP], ACT.Copy))
                for j in range(3):
                    s(A(G_cst[:, j, HIST:].rearrange("p (a b) -> p a b", b=HIST),
                        G_ext[:, j, EXTP:EXT].rearrange("p (a b) -> p a b", b=SEG)[:, :, TS:SEG], ACT.Copy),
                      *((d_cst, h + 1) if j == 2 else ()))
                act.dma_start(O["gdn_conv"][ds(h, 1)].rearrange("o p (a b) -> p (o a) b", a=3), G_cst).then_inc(d_cso, 16)
                for v in range(1, LEVELS):
                    act.wait_ge(d_pt, h * LEVELS + (v + 1))
                    if v < SLEVELS:
                        s(A(G_spt[0:NS, :], ps[0:NS, 7, 0:NS], ACT.Copy))
                    s(A(G_pt, ps[:, 4, :].rearrange("p (a b) -> p a b", b=P), ACT.Copy), d_pte, h * (LEVELS - 1) + v)
                    if ahead and v == 2:
                        act.wait_ge(d_qg, h + 1)
                        rows(h + 1)
                    if ahead and v == 5:
                        silu(h + 1, 0)
                    if ahead and v in (3, 5):
                        ext(h + 1, v // 2 - 1)
                act.wait_ge(d_wt, h + 1)
                s(A(G_swt, ps[:, 5, 0:NS], ACT.Copy, scale=-1.0))
                s(A(G_wt, ps[:, 4, :].rearrange("p (a b) -> p a b", b=P), ACT.Copy, scale=-1.0), d_wte, h + 1)
                for c in range(NC):
                    act.wait_ge(d_vn, h * NC + (c + 1))
                    s(A(G_vn[:, c % 2, :], ps[:, 6, c * P:(c + 1) * P], ACT.Copy), d_vne, h * NC + (c + 1))
                    if ahead and c == 0:
                        silu(h + 1, 1)
                    if ahead and c == 1:
                        ext(h + 1, 2)
                act.wait_ge(d_s, h * NC + NC)
                act.dma_start(O["gdn_sp"][ds(h, 1)].rearrange("o p b -> p (o b)"), G_s[:, (NC - 1) % 2, :]).then_inc(d_sout, 16)
                act.wait_ge(d_svt, h + 1)
                s(A(G_svt, ps[:, 5, 64:64 + NS], ACT.Copy), d_svte, h + 1)
                act.wait_ge(d_svn, h + 1)
                s(A(G_svn[0:NS, :], ps[0:NS, 5, 128:256], ACT.Copy), d_svne, h + 1)
                if ahead:
                    silu(h + 1, 2)
                if ahead:
                    log_length(h + 1, 0)
                act.wait_ge(d_oe, h + 1)
                s(A(G_sq, G_ot, ACT.Square), d_osq, h + 1)
                if ahead:
                    log_length(h + 1, 1)
                act.wait_ge(d_oss, h + 1)
                s(A(two(G_ors[:, :]), pair(0), ACT.Ln, bias=pc("eps6"), scale=1.0 / P))
                if ahead:
                    unit(h + 1)
                s(A(G_ors[:, :], G_ors[:, :], ACT.Exp, scale=-0.5), d_ostd, h + 1)
                act.wait_ge(d_ssn, h + 1)
                act.dma_start(O["gdn_ss"][ds(h, 1)].rearrange("o p (a b) -> p (o a) b", a=NB), G_s0).then_inc(d_sout, 16)
                if ahead:
                    decay(h + 1)
                    grow(h + 1)
                act.wait_ge(d_on, h + 1)
                s(A(hh[:, ds(h, 1), :], G_ot.rearrange("p (o c) -> p o c", o=1), ACT.Copy), d_yh, h + 1)
                if ahead:
                    gate_z(h + 1)
            repeat(act, GH - 1, head, s)
            head(GH - 1, ahead=False)
            act.wait_ge(d_cso, 16 * GH)
            act.wait_ge(d_sout, 32 * GH)
            kv_start(1)
            layer_norm(3, 1)
            attention(1)
            layer_norm(4)
            act.wait_ge(out_done, 96)
            act.dma_start(M_iota, I["places"]).then_inc(r_iota, 16)
            s(A(M_tri, tc("mincl"), ACT.Exp), r_act, TRIANGLE)
            act.wait_ge(r_dve, DIFFERENCE)
            s(A(R_w[:, :, 0:1], R_w[:, :, 0:1], ACT.Exp), r_act, EXPONENT)

            def upper_tokens(lo, hi):
                for n in range(lo, hi):
                    tt, hf = divmod(n, 2)
                    w = P if tt < NC else NS
                    act.wait_ge(t_tr, n + 1)
                    s(A(T_h[0:w, tt, 512 * hf:512 * hf + 512], ps[0:w, TBANK[n], :], ACT.Copy), t_h, n + 1)

            upper_tokens(0, EARLY)

            def gathered(e):
                e12, e8 = e * FT, e * KT
                for k in range(KT):
                    act.wait_ge(m_x, e8 + (k + 1))
                    s(A(M_x[:, k, :], ps[:, 2 + k % 2, 0:CAP], ACT.Copy), m_xe, e8 + (k + 1))
                act.wait_ge(m_pt, e + 1)
                for i, (c, w) in enumerate(CT):
                    s(A(M_gate[0:w, i:i + 1], ps[0:w, 5 + 2 * i, NS:NS + 1], ACT.Copy))
                    s(A(M_pt[0:w, i, 0:TP], ps[0:w, 4 + 2 * i, :], ACT.Copy))
                    s(A(M_pt[0:w, i, TP:T], ps[0:w, 5 + 2 * i, 0:NS], ACT.Copy), *((m_pte, e + 1) if i else ()))

                def up(g):
                    for j in range(2):
                        act.wait_ge(w_used, e * 36 + g * 4 + (S_MOE + 2 * j + 2))
                        ge(act, m_h, e12 + g * 2 + (j - 1))
                        s(A(M_s[:, j, :], ps[:, j, 0:CAP], ACT.Silu), m_silu, e12 + g * 2 + (j + 1))
                repeat(act, FT // 2, up, s, passed)
                for d in range(KT + 1):
                    if d < KT:
                        act.wait_ge(w_used, e * 36 + (S_MOE + 24 + ((d + 1) * FT + KT - 1) // KT))
                        if d >= 2:
                            act.wait_ge(m_tr, e8 + (d - 1))
                        s(A(M_yt[:, d % 2, :], ps[:, 2 + d % 2, 0:CAP], ACT.Copy), m_yt, e8 + (d + 1))
                    if d:
                        act.wait_ge(m_tr, e8 + d)
                        for i, (c, w) in enumerate(CT):
                            s(A(M_yh[0:w, i, (d - 1) * P:d * P], ps[0:w, (d - 1) % 2, i * P:(i + 1) * P], ACT.Copy,
                                scale=M_gate[0:w, i:i + 1]), *((m_yh, e8 + d) if i else ()))
            act.wait_ge(r_dve, COUNTED)
            over = act.value_load(R_over[0:1, 0:1], min_val=0, max_val=1)
            with act.If(over > 0):
                act.wait_ge(r_row, 2)
                act.dma_start(I["scratch"][0], R_row[0:NE, :]).then_inc(row_st, 16)
                act.wait_ge(row_st, 48)

                def gate_row(e, first):
                    if not first:
                        act.wait_ge(f_h, (e + HALVES) * FT)
                    act.dma_start(F_g, I["scratch"][0, ds(e, 1), :].to_broadcast((P, T))).then_inc(g_in, 16)

                def one(e):
                    gate_row(e, isinstance(e, int))
                    e36, e12 = e * 36 + S_MOE, (e + HALVES) * FT

                    def up(g):
                        for j in range(2):
                            act.wait_ge(w_used, e36 + g * 4 + (2 * j + 1))
                            ge(act, f_h, e12 + g * 2 + (j - 1))
                            s(A(two(F_s[:, j, :]), pair(2 * j), ACT.Silu), f_silu, e12 + g * 2 + (j + 1))
                            act.wait_ge(f_h, e12 + g * 2 + (j + 1))
                            s(A(hh[:, ds(g * 2 + j, 1), :], F_h[:, j:j + 1, :], ACT.Copy), f_hh, e12 + g * 2 + (j + 1))
                    repeat(act, FT // 2, up, s, passed)
                repeat(act, NE, one, s)
            with act.Else():
                s = Serial(act, act_chain2)
                upper_tokens(EARLY, 2 * NT)
                repeat(act, NE, gathered, s)
            act.end_ifs()
            s = Serial(act, act_chain3)
            layer_norm(5)

        @nc_block.vector
        def _(dve):
            V = nc.vector
            s = Serial(dve, dve_chain)

            def split_low(dst, src, hi, sm, val):
                s(V.tensor_tensor(dst, src, hi.bitcast(F), SUB), sm, val)

            for k in range(KT):
                dve.wait_ge(x_split_h, k + 1)
                split_low(xl[:, k, :], x[:, k, :], xh[:, k, :], x_split_l, k + 1)
            dve.wait_ge(ld_par, 16)
            dve.wait_ge(ld_tab, 16)

            def layer_norm(n):
                dve.wait_ge(ln_sum, n + 1)
                for k in range(KT):
                    s(V.scalar_tensor_tensor(two(x[:, k, :]), pair(2), -1.0 / D, two(x[:, k, :]), MUL, ADD), ln_d, n * KT + k + 1)
                dve.wait_ge(ln_std, n + 1)
                for k in range(KT):
                    s(V.tensor_tensor(x[:, k, :], x[:, k, :], lnr[:, :], MUL), ln_n, n * KT + k + 1)
                if n < NLN - 1:
                    for k in range(KT):
                        dve.wait_ge(ln_x, n * KT + k + 1)
                        split_low(xl[:, k, :], x[:, k, :], xh[:, k, :], ln_xl, n * KT + k + 1)

            def add_tile(t, n):
                if t:
                    s(V.tensor_tensor(lnsq[:, 0, :], x[:, 0, :] if t == 1 else lnsq[:, 0, :], x[:, t, :], ADD),
                      *((z_sum, n + 1) if t == KT - 1 else ()))

            def residual(slot, n):
                done = (0, 1, 1, 2, 3)[n]
                for t in range(8):
                    dve.wait_ge(w_used, slot + t + 1)
                    s(V.scalar_tensor_tensor(two(x[:, t, :]), two(x[:, t, :]), ALPHA, pair(t % 2), MUL, ADD),
                      z_ready, done * KT + t + 1)
                    add_tile(t, n)

            def attention(l):
                for h in range(XH):
                    n = XH * l + h
                    dve.wait_ge(pa_s, n + 1)
                    if h:
                        dve.wait_ge(pa_exp, 4 * n)
                    s(V.tensor_reduce(A_nm, ps[:, 4:6, :].rearrange("p a (b c) -> p (a b) c", c=MEM), AX.X, ALU.max, negate=True),
                      pa_max, n + 1)
                    if h == 2:
                        dve.wait_ge(ss_tr, l + 1)
                        s(V.tensor_reduce(A_snm, ps[:, 3, 0:MEM], AX.X, ALU.max, negate=True), ss_max, l + 1)
                    dve.wait_ge(pa_exp, 4 * n + 4)
                    s(V.reciprocal(A_rs, A_rs))
                    s(V.tensor_tensor(A_p, A_p, A_rs.unsqueeze(2).to_broadcast((P, 4, MEM)), MUL), pa_p, n + 1)
                    if h == 2:
                        dve.wait_ge(ss_exp, l + 1)
                        s(V.reciprocal(A_srs, A_srs))
                        s(V.tensor_scalar(A_sp, A_sp, A_srs, None, MUL), ss_p, l + 1)
                    dve.wait_ge(pa_oh, n + 1)
                    s(V.tensor_tensor(xl[:, 2 * h:2 * h + 2, 0:TP], ps[:, 0:2, :], xh[:, 2 * h:2 * h + 2, 0:TP].bitcast(F), SUB),
                      pa_ol, n + 1)
                dve.wait_ge(ss_oh, l + 1)
                s(V.tensor_tensor(xl[:, :, TP:T], ps[:, 3, 0:KT * NS].rearrange("p (a b) -> p a b", b=NS),
                                  xh[:, :, TP:T].bitcast(F), SUB), ss_ol, l + 1)

            def experts(n, slot, e0, gated, n_ln):
                def one(e):
                    e36, e12, e8 = e * 36 + slot, (e + e0) * FT, (e + e0) * KT
                    if gated:
                        dve.wait_ge(g_in, e * 16 + 16)

                    def up(g):
                        for j in range(2):
                            dve.wait_ge(w_used, e36 + g * 4 + (2 * j + 2))
                            dve.wait_ge(f_silu, e12 + g * 2 + (j + 1))
                            if gated:
                                s(V.tensor_tensor(F_s[:, j, :], F_s[:, j, :], F_g, MUL))
                            s(V.tensor_tensor(two(F_h[:, j, :]), two(F_s[:, j, :]), pair(2 * j + 1), MUL), f_h, e12 + g * 2 + (j + 1))
                            dve.wait_ge(f_hh, e12 + g * 2 + (j + 1))
                            split_low(hl[:, ds(g * 2 + j, 1), :], F_h[:, j:j + 1, :], hh[:, ds(g * 2 + j, 1), :],
                                      f_hl, e12 + g * 2 + (j + 1))
                    repeat(dve, FT // 2, up, s, passed)
                    first = isinstance(e, int) and e == 0
                    for d in range(KT):
                        dve.wait_ge(w_used, e36 + (24 + ((d + 1) * FT + KT - 1) // KT))
                        s(V.scalar_tensor_tensor(two(x[:, d, :]), two(x[:, d, :]), ALPHA if first else 1.0, pair(d % 4), MUL, ADD),
                          f_y, e8 + (d + 1))
                repeat(dve, n, one, s)
                for k in range(KT):
                    add_tile(k, n_ln)

            def log1p_half(e, t0, t1, t2):
                s(V.tensor_scalar(t0, e, 2.0, None, ADD))
                s(V.reciprocal(t0, t0))
                s(V.tensor_tensor(t0, t0, e, MUL))
                s(V.tensor_tensor(t1, t0, t0, MUL))
                s(V.tensor_scalar(t2, t1, 1.0 / 17, None, MUL))
                for m in range(7, 0, -1):
                    s(V.scalar_tensor_tensor(t2, t2, 1.0 / (2 * m + 1), t1, ADD, MUL))
                s(V.scalar_tensor_tensor(t2, t2, 1.0, t0, ADD, MUL))
                s(V.tensor_scalar(t2, t2, 2.0, None, MUL))

            sp0 = [L_sp[:, i, :] for i in range(6)]
            s(V.scalar_tensor_tensor(sp0[0], pc("lam"), -1.0, pc("lam"), MUL, ALU.max), lru_sp, 1)
            dve.wait_ge(lru_spe, 1)
            log1p_half(sp0[1], sp0[2], sp0[3], sp0[4])
            s(V.tensor_scalar(sp0[0], pc("lam"), -1.0, 0.0, MUL, ALU.max))
            s(V.tensor_tensor(sp0[0], sp0[0], sp0[4], ADD))
            s(V.tensor_scalar(sp0[0], sp0[0], LRU_C, None, MUL))
            s(V.memset(L_ext[:, :, 0:HIST], 0.0))

            lgb = pc("lgb").rearrange("p (a b) -> p a b", b=2)
            lcw = pc("lcw").rearrange("p (a b) -> p a b", b=CW)
            lcb = pc("lcb").rearrange("p (a b) -> p a b", b=1)
            h0v = pc("h0").rearrange("p (a b) -> p a b", b=NB)
            lhv = pc("lhist").rearrange("p (a b) -> p a b", b=NB * HIST)

            def conv(ext, acc, out, w, bias, taps=range(CW), done=()):
                if 0 in taps and bias is None:
                    s(V.tensor_scalar(acc, ext[:, 0:CONV], w(0), None, MUL))
                elif 0 in taps:
                    s(V.tensor_scalar(acc, ext[:, 0:CONV], w(0), bias, MUL, ADD))
                for j in (1, 2):
                    if j in taps:
                        s(V.scalar_tensor_tensor(acc, ext[:, j:j + CONV], w(j), acc, MUL, ADD))
                if 3 in taps:
                    s(V.scalar_tensor_tensor(out[:, 0:TP], ext[:, 3:3 + TP], w(3), acc[:, 0:TP], MUL, ADD))
                    seg = ext[:, EXTP:EXT].rearrange("p (a b) -> p a b", b=SEG)[:, :, HIST:SEG]
                    a7 = acc[:, EXTP:EXTP + (NB - 1) * SEG].rearrange("p (a b) -> p a b", b=SEG)[:, :, 0:TS]
                    o7 = out[:, TP:TP + (NB - 1) * TS].rearrange("p (a b) -> p a b", b=TS)
                    s(V.scalar_tensor_tensor(o7, seg[:, 0:NB - 1, :], w(3), a7, MUL, ADD))
                    s(V.scalar_tensor_tensor(out[:, T - TS:T], ext[:, EXT - TS:EXT], w(3), acc[:, CONV - TS:CONV], MUL, ADD),
                      *done)

            def lru_params(b):
                s(V.tensor_copy(L_par[:, :, 0:4], lcw[:, ds(b * 2, 2), :]))
                s(V.tensor_copy(L_par[:, :, 4:6], lgb[:, ds(b * 2, 2), :]))
                s(V.tensor_copy(L_sp[:, 5, 0:2], L_sp[:, 0, ds(b * 2, 2)]))
                s(V.tensor_copy(L_sp[:, 5, 2:4], pc("lcb")[:, ds(b * 2, 2)]))
                for j in range(2):
                    s(V.tensor_copy(L_ext[:, j, EXTP:EXT].rearrange("p (a b) -> p a b", b=SEG)[:, :, 0:HIST],
                                    lhv[:, ds(b * 2 + j, 1), :].rearrange("p o (a b) -> p (o a) b", b=HIST)))

            def lru_convolve(b, j, lo, hi):
                if lo == 0:
                    dve.wait_ge(lru_ext, b * 2 + (j + 1))
                    ge(dve, lru_gate_full, b * 4)
                conv(L_ext[:, j, :], L_acc, L_rec[:, j, :], lambda t: L_par[:, j, t:t + 1], L_sp[:, 5, 2 + j:3 + j],
                     taps=range(lo, hi), done=(lru_conv, b * 2 + (j + 1)))
                if hi == CW:
                    s(V.tensor_copy(L_cst[:, ds(b * 2 + j, 1), 0:HIST], L_ext[:, j:j + 1, TP:EXTP]))
                    s(V.tensor_copy(L_cst[:, ds(b * 2 + j, 1), HIST:].rearrange("p o (a b) -> p (o a) b", b=HIST),
                                    L_ext[:, j, EXTP:EXT].rearrange("p (a b) -> p a b", b=SEG)[:, :, TS:SEG]),
                      lru_cst, b * 2 + (j + 1))

            lru_params(0)
            for j in range(2):
                lru_convolve(0, j, 0, CW)

            def lru(b, ahead=True):
                s(V.tensor_copy(L_h0, h0v[:, ds(b * 2, 2), :]))
                dve.wait_ge(lru_gate_ev, b * 4 + 4)
                for j in range(2):
                    s(V.tensor_scalar(L_r[:, j, :], L_r[:, j, :], L_sp[:, 5, j:j + 1], None, MUL), lru_dve, b * 10 + (j + 1))
                for j in range(2):
                    s(V.tensor_tensor(L_i[:, j, :], L_i[:, j, :], L_rec[:, j, :], MUL), lru_dve, b * 10 + (j + 3))
                if ahead:
                    lru_params(b + 1)
                for j in range(2):
                    dve.wait_ge(lru_act, b * 4 + (2 * j + 1))
                    s(V.tensor_scalar(L_b, L_t, 1.0, None, ADD))
                    s(V.reciprocal(L_b, L_b))
                    s(V.scalar_tensor_tensor(L_t, L_t, 2.0, L_b, MUL, MUL), lru_dve, b * 10 + (3 * j + 5))
                    if ahead:
                        lru_convolve(b + 1, j, 0, 2)
                    dve.wait_ge(lru_act, b * 4 + (2 * j + 2))
                    s(V.tensor_tensor(L_b, L_t, L_i[:, j, :], MUL))
                    a0 = L_a[:, TP:T].rearrange("p (a b) -> p a b", b=TS)[:, :, 0:1]
                    b0 = L_b[:, TP:T].rearrange("p (a b) -> p a b", b=TS)[:, :, 0:1]
                    s(V.tensor_tensor(L_h0[:, j, :].unsqueeze(2), a0, L_h0[:, j, :].unsqueeze(2), MUL))
                    s(V.tensor_tensor(b0, b0, L_h0[:, j, :].unsqueeze(2), ADD))
                    s(V.memset(a0, 0.0))
                    s(V.tensor_tensor_scan(L_t, L_a, L_b, 0.0, MUL, ADD))
                    s(V.tensor_copy(L_hst[:, ds(b * 2 + j, 1), 0:1], L_t[:, TP - 1:TP].unsqueeze(1)))
                    s(V.tensor_copy(L_hst[:, ds(b * 2 + j, 1), 1:], L_t[:, TP:T].rearrange("p (o a b) -> p o a b", o=1, b=TS)[:, :, :, TS - 1]),
                      lru_dve, b * 10 + (3 * j + 6))
                    dve.wait_ge(lru_gelu, b * 2 + (j + 1))
                    s(V.tensor_tensor(L_b, L_t, L_gel[:, j, :], MUL), lru_dve, b * 10 + (3 * j + 7))
                    dve.wait_ge(lru_yh, b * 2 + (j + 1))
                    split_low(hl[:, ds(b * 2 + j, 1), :], L_b.rearrange("p (o c) -> p o c", o=1), hh[:, ds(b * 2 + j, 1), :],
                              lru_y, b * 2 + (j + 1))
                    if ahead:
                        lru_convolve(b + 1, j, 2, CW)
            repeat(dve, BLK - 1, lru, s)
            lru(BLK - 1, ahead=False)
            residual(S_LOUT, 0)
            layer_norm(0)
            attention(0)
            residual(S_O[0], 1)
            layer_norm(1)
            experts(HALVES, S_FFN, 0, False, 2)
            layer_norm(2)

            g8 = lambda i: B_r[i][0:GH, :]
            dve.wait_ge(ln_x, KT * 3)
            dve.wait_ge(b_beta, 1)
            s(V.tensor_scalar(two(g8(4)), pair(3)[0:GH], pc("dtb")[0:GH, :], None, ADD))
            s(V.scalar_tensor_tensor(g8(5), g8(4), -1.0, g8(4), MUL, ALU.max), b_x, 1)
            dve.wait_ge(b_e, 1)
            log1p_half(g8(5), g8(6), g8(7), g8(8))
            s(V.scalar_tensor_tensor(g8(4), g8(4), 0.0, g8(8), ALU.max, ADD))
            s(V.tensor_scalar(g8(4), g8(4), B_r[9][0:GH, 0:1], -1.0, MUL, MUL))
            s(V.memset(g8(6), 1.0))
            s(V.memset(B_r[6][0:GH, 0:TP].rearrange("p (a b) -> p a b", b=C)[:, :, 0:1], 0.0))
            s(V.memset(B_r[6][0:GH, TP:T].rearrange("p (a b) -> p a b", b=TS)[:, :, 0:1], 0.0))
            s(V.tensor_tensor_scan(g8(0), g8(6), g8(4), 0.0, MUL, ADD))
            for lo, hi, w in ((0, TP, C), (TP, T, TS)):
                v0 = B_r[0][0:GH, lo:hi].rearrange("p (a b) -> p a b", b=w)
                v3 = B_r[3][0:GH, lo:hi].rearrange("p (a b) -> p a b", b=w)
                n = (hi - lo) // w
                s(V.tensor_tensor(v3, v0[:, :, w - 1:w].to_broadcast((GH, n, w)), v0, SUB), *((b_g, 1) if lo else ()))
            dve.wait_ge(b_eg, 1)
            s(V.tensor_tensor(g8(2), g8(2), g8(1), MUL), b_rows, 1)
            dve.wait_ge(b_pe, 2)
            s(V.tensor_copy(G_cols[:, 0:NC, :, :], ps[:, 4, 0:NC * 32].rearrange("p (a b c) -> p a b c", b=4, c=GH)), b_col, 1)
            s(V.tensor_copy(G_cols[0:NS, NC, :, :], ps[0:NS, 4, NC * 32:NT * 32].rearrange("p (b c) -> p b c", c=GH)), b_col, 2)
            dve.wait_ge(row_st, 32)
            s(V.memset(G_ext[:, :, 0:HIST], 0.0))

            gcw = pc("gcw").rearrange("p (h a) -> p h a", h=GH)
            mincl = tc("mincl")
            levels = tc("levels").rearrange("p (a b) -> p a b", b=P)

            def columns(h):
                s(V.tensor_copy(G_cw.rearrange("p (o a) b -> p o (a b)", o=1), gcw[:, ds(h, 1), :]))
                s(V.tensor_copy(G_hc[:, 0:NC, :], G_cols[:, 0:NC, :, ds(h, 1)].rearrange("p a b o -> p a (b o)")))
                s(V.tensor_copy(G_hc[0:NS, NC, :], G_cols[0:NS, NC, :, ds(h, 1)].rearrange("p b o -> p (b o)")))
                dve.wait_ge(d_hist, h * 16 + 16)
                ge(dve, d_cst, h)
                for j in range(3):
                    s(V.tensor_copy(G_ext[:, j, EXTP:EXT].rearrange("p (a b) -> p a b", b=SEG)[:, :, 0:HIST],
                                    G_hist[:, j, :].rearrange("p (a b) -> p a b", b=HIST)))

            def convolve(h, j, lo, hi):
                if lo == 0:
                    dve.wait_ge(d_ext, h * 3 + (j + 1))
                conv(G_ext[:, j, :], G_acc[:, 0:CONV], G_qkv[:, j, :], lambda t: G_cw[:, j, t:t + 1], None,
                     taps=range(lo, hi), done=(d_conv, h * 3 + (j + 1)))

            def argument(h):
                dve.wait_ge(d_row, h * 32 + 32)
                for c in range(NC):
                    s(V.scalar_tensor_tensor(G_dt[:, c, :], G_gc[:, c * P:(c + 1) * P], G_hc[:, c, 0:1], mincl, SUB, ALU.min))
                s(V.scalar_tensor_tensor(G_sdt[0:NS, :], G_gc[0:NS, TP:T], G_hc[0:NS, NC, 0:1], tc("smincl")[0:NS, :], SUB, ALU.min),
                  d_arg, h + 1)

            def unit(h, j):
                dve.wait_ge(d_std, h * 2 + (j + 1))
                s(V.scalar_tensor_tensor(G_qkv[:, j, :], G_qkv[:, j, :], P ** -0.5 if j == 0 else 1.0, G_rs[:, j, :], MUL, MUL),
                  d_qk, h * 2 + (j + 1))

            columns(0)
            for j in range(3):
                convolve(0, j, 0, CW)
            argument(0)
            for j in range(2):
                unit(0, j)

            def head(h, ahead=True):
                dve.wait_ge(d_dt, h + 1)
                s(V.tensor_tensor(G_bl[:, 1], G_dt, G_be[:, 0:TP].rearrange("p (a b) -> p a b", b=P), MUL))
                s(V.tensor_tensor(G_sbl[0:NS, :], G_sdt[0:NS, :], G_be[0:NS, TP:T], MUL))
                col = lambda c: G_hc[:, 0:NC, c:c + 1].to_broadcast((P, NC, P))
                b4 = lambda bank: ps[:, bank, :].rearrange("p (a b) -> p a b", b=P)
                dve.wait_ge(d_tm, h * 2 + 1)
                s(V.tensor_tensor(G_kb[:, 0:NC, :], b4(4), col(2), MUL))
                s(V.tensor_tensor(G_kd[:, 0:NC, :], b4(4), col(3), MUL))
                s(V.tensor_scalar(G_kb[0:NS, NC, :], ps[0:NS, 5, 0:P], G_hc[0:NS, NC, 2:3], None, MUL))
                s(V.tensor_scalar(G_kd[0:NS, NC, :], ps[0:NS, 5, 0:P], G_hc[0:NS, NC, 3:4], None, MUL), d_tme, h * 2 + 1)
                dve.wait_ge(d_tm, h * 2 + 2)
                s(V.tensor_tensor(G_vb[:, 0:NC, :], b4(6), col(1), MUL))
                s(V.tensor_scalar(G_vb[0:NS, NC, :], ps[0:NS, 7, 0:P], G_hc[0:NS, NC, 1:2], None, MUL), d_tme, h * 2 + 2)
                dve.wait_ge(d_kk, h * 2 + 2)
                s(V.tensor_tensor(G_at, b4(6), G_dt, MUL))
                s(V.tensor_tensor(G_sat[0:NS, :], ps[0:NS, 7, 0:NS], G_sdt[0:NS, :], MUL))
                s(V.tensor_tensor(G_dt, b4(4), G_bl[:, 1], MUL))
                s(V.tensor_tensor(G_sdt[0:NS, :], ps[0:NS, 5, 0:NS], G_sbl[0:NS, :], MUL), d_at, h + 1)
                idb = ident.unsqueeze(1).to_broadcast((P, NC, P))

                def block(v):
                    if v < SLEVELS:
                        s(V.tensor_tensor(G_sbl[0:NS, :], G_sdt[0:NS, :], levels[0:NS, v, 0:NS], MUL))
                    s(V.tensor_tensor(G_bl[:, v % 2], G_dt, levels[:, v, :].unsqueeze(1).to_broadcast((P, NC, P)), MUL),
                      d_bl, h * LEVELS + (v + 1))

                block(0)
                s(V.tensor_tensor(G_u, idb, G_bl[:, 0], SUB))
                s(V.tensor_tensor(G_su[0:NS, :], ident[0:NS, 0:NS], G_sbl[0:NS, :], SUB), d_ute, h * LEVELS + 1)
                dve.wait_ge(d_pt, h * LEVELS + 1)
                block(1)
                s(V.tensor_tensor(G_st[0:NS, :], ident[0:NS, 0:NS], ps[0:NS, 7, 0:NS], SUB))
                s(V.tensor_tensor(G_t, idb, b4(5), SUB), d_tt, h * (LEVELS - 1) + 1)
                dve.wait_ge(d_egr, h + 1)
                s(V.tensor_tensor(G_qg, G_eg, G_qkv[:, 0, :], MUL), d_qg, h + 1)
                for v in range(1, LEVELS):
                    small = v < SLEVELS
                    if v + 1 < LEVELS:
                        block(v + 1)
                    if v < LEVELS - 1:
                        dve.wait_ge(d_ut, h * (LEVELS - 2) + v)
                        s(V.tensor_tensor(G_t, G_t, b4(5), SUB), d_tt, h * (LEVELS - 1) + (v + 1))
                    dve.wait_ge(d_uu, h * (LEVELS - 1) + v)
                    if small:
                        s(V.tensor_tensor(G_su[0:NS, :], G_su[0:NS, :], ps[0:NS, 7, 32:32 + NS], SUB))
                    s(V.tensor_tensor(G_u, G_u, b4(6), SUB), d_ute, h * LEVELS + (v + 1))
                    if ahead and v == 3:
                        columns(h + 1)
                        convolve(h + 1, 0, 0, 2)
                    if ahead and v == 4:
                        convolve(h + 1, 0, 2, CW)
                    if ahead and v == 5:
                        convolve(h + 1, 1, 0, 2)
                    if ahead and v == 6:
                        convolve(h + 1, 1, 2, CW)
                        argument(h + 1)
                ge(dve, d_sout, h * 32)
                for c in range(NC):
                    dve.wait_ge(d_o, h * NC + (c + 1))
                    if c:
                        s(V.scalar_tensor_tensor(G_s[:, c % 2, :], G_s[:, (c + 1) % 2, :], G_eg[:, c * P + P - 1:c * P + P],
                                                 ps[:, 4, c * P:(c + 1) * P], MUL, ADD), d_s, h * NC + (c + 1))
                    else:
                        s(V.tensor_copy(G_s[:, 0, :], ps[:, 4, 0:P]), d_s, h * NC + 1)
                    if ahead and c == 2:
                        convolve(h + 1, 2, 0, 1)
                    if ahead and c == 3:
                        convolve(h + 1, 2, 1, CW)
                s(V.tensor_tensor(G_kdm[0:NS, :, :], G_kd[0:NS, NC:NT, :].to_broadcast((NS, NB, P)),
                                  tc("smask")[0:NS, :].unsqueeze(2).to_broadcast((NS, NB, P)), MUL), d_kdm, h + 1)
                dve.wait_ge(d_so, h + 1)
                s(V.tensor_copy(G_ot[:, 0:TP], ps[:, 7, :]))
                s(V.tensor_copy(G_ot[:, TP:T], ps[:, 5, 256:256 + NS]), d_oe, h + 1)
                egl = G_eg[:, TP:T].rearrange("p (a b) -> p a b", b=TS)[:, :, TS - 1:TS].to_broadcast((P, NB, P))
                s(V.tensor_tensor(G_s0, G_s0, egl, MUL))
                dve.wait_ge(d_sds, h + 1)
                s(V.tensor_tensor(G_s0[:, 0:4, :], G_s0[:, 0:4, :], b4(4), ADD))
                s(V.tensor_tensor(G_s0[:, 4:8, :], G_s0[:, 4:8, :], b4(6), ADD), d_ssn, h + 1)
                if ahead:
                    for j in range(2):
                        unit(h + 1, j)
                dve.wait_ge(d_ostd, h + 1)
                s(V.tensor_tensor(G_ot, G_ot, G_ors[:, :], MUL))
                s(V.scalar_tensor_tensor(G_ot, G_ot, pc("ng"), G_z, MUL, MUL), d_on, h + 1)
                dve.wait_ge(d_yh, h + 1)
                split_low(hl[:, ds(h, 1), :], G_ot.rearrange("p (o c) -> p o c", o=1), hh[:, ds(h, 1), :], d_yl, h + 1)
            repeat(dve, GH - 1, head, s)
            head(GH - 1, ahead=False)
            residual(S_GOUT, 3)
            layer_norm(3)
            attention(1)
            residual(S_O[1], 4)
            layer_norm(4)

            dve.wait_ge(r_pe, LOGITS)
            s(V.memset(R_l, 0.0))
            s(V.tensor_copy(R_l[:, 0:NC, :], ps[:, 4, 0:NC * 8].rearrange("p (a b) -> p a b", b=8)))
            s(V.tensor_copy(R_l[0:NS, NC, :], ps[0:NS, 4, NC * 8:NT * 8]))
            for tt in range(NT):
                s(V.max(R_m[:, tt, :], R_l[:, tt, :]))
                s(V.max_index(R_i[:, tt, :], R_m[:, tt, :], R_l[:, tt, :]))
            s(V.tensor_copy(R_f, R_i))
            s(V.memset(R_g, 0.0))
            s(V.tensor_tensor(R_w[:, :, 0:1], R_m[:, :, 1:2], R_m[:, :, 0:1], SUB), r_dve, DIFFERENCE)
            dve.wait_ge(r_act, EXPONENT)
            s(V.tensor_scalar(R_w[:, :, 1:2], R_w[:, :, 0:1], 1.0, None, ADD))
            s(V.reciprocal(R_w[:, :, 1:2], R_w[:, :, 1:2]))
            s(V.tensor_tensor(R_w[:, :, 0:1], R_w[:, :, 0:1], R_w[:, :, 1:2], MUL))
            iob = pc("iota").unsqueeze(1).to_broadcast((P, NT, 8))
            for m, dst in ((0, R_g[:, :, 0:NE]), (1, R_o)):
                s(V.tensor_tensor(dst, iob, R_f[:, :, m:m + 1].to_broadcast((P, NT, 8)), ALU.is_equal))
                if m:
                    s(V.tensor_tensor(R_sel, R_g[:, :, 0:NE], R_o, ADD), r_dve, CHOSEN)
            for m, dst in ((0, R_g[:, :, 0:NE]), (1, R_o)):
                s(V.tensor_tensor(dst, dst, R_w[:, :, 1 - m:2 - m].to_broadcast((P, NT, 8)), MUL))
            s(V.tensor_tensor(R_g[:, :, 0:NE], R_g[:, :, 0:NE], R_o, ADD), r_dve, GATES)

            def lower_tokens(lo, hi):
                for n in range(lo, hi):
                    tt, hf = divmod(n, 2)
                    w = P if tt < NC else NS
                    dve.wait_ge(t_h, n + 1)
                    split_low(T_l[0:w, tt, 512 * hf:512 * hf + 512], ps[0:w, TBANK[n], :], T_h[0:w, tt, 512 * hf:512 * hf + 512],
                              t_l, n + 1)

            lower_tokens(0, EARLY)
            s(V.memset(R_pos, -1.0))
            dve.wait_ge(r_pe, RANKS)
            for w, t0, t1 in ((P, 0, NC), (NS, NC, NT)):
                s(V.tensor_tensor(R_pos[0:w, t0:t1, 0:NE], ps[0:w, 5, t0 * 8:t1 * 8].rearrange("p (a b) -> p a b", b=8),
                                  R_sel[0:w, t0:t1, :], MUL))
                s(V.tensor_scalar(R_pos[0:w, t0:t1, 0:NE], R_pos[0:w, t0:t1, 0:NE], -1.0, None, ADD))
            s(V.tensor_reduce(R_most[0:1, :], ps[0:1, 5, 64:72], AX.X, ALU.max))
            s(V.tensor_scalar(R_over[0:1, :], R_most[0:1, :], float(CAP), None, ALU.is_gt), r_dve, COUNTED)

            def one_hot(e):
                s(V.tensor_copy(M_gcol, R_g[:, :, ds(e, 1)]))
                s(V.tensor_tensor(M_p, M_iota.unsqueeze(1).to_broadcast((P, NT, CAP)),
                                  R_pos[:, :, ds(e, 1)].to_broadcast((P, NT, CAP)), ALU.is_equal), m_p, e + 1)

            def gathered(e):
                e12, e8 = e * FT, e * KT

                def up(g):
                    for j in range(2):
                        dve.wait_ge(m_silu, e12 + g * 2 + (j + 1))
                        s(V.tensor_tensor(M_h[:, ds(g * 2 + j, 1), :], M_s[:, j:j + 1, :],
                                          ps[:, j:j + 1, CAP:2 * CAP], MUL), m_h, e12 + g * 2 + (j + 1))
                repeat(dve, FT // 2, up, s, passed)
                dve.wait_ge(m_pt, e + 1)
                one_hot(e + 1)
                for d in range(KT):
                    dve.wait_ge(m_yh, e8 + (d + 1))
                    for i, (c, w) in enumerate(CT):
                        s(V.scalar_tensor_tensor(M_yl[0:w, i, d * P:(d + 1) * P], ps[0:w, d % 2, i * P:(i + 1) * P],
                                                 M_gate[0:w, i:i + 1], M_yh[0:w, i, d * P:(d + 1) * P].bitcast(F), MUL, SUB),
                          *((m_yl, e8 + (d + 1)) if i else ()))
                for d in range(KT):
                    dve.wait_ge(m_z, e8 + (d + 1))
                    s(V.scalar_tensor_tensor(two(x[:, d, :]), two(x[:, d, :]), ALPHA if isinstance(e, int) else 1.0,
                                             pair(2 + d % 2), MUL, ADD), m_add, e8 + (d + 1))

            over = dve.value_load(R_over[0:1, 0:1], min_val=0, max_val=1)
            with dve.If(over > 0):
                dve.wait_ge(r_pe, TURNED)
                s(V.tensor_copy(R_row[0:NE, 0:TP], ps[0:NE, 5, :]), r_row, 1)
                s(V.tensor_copy(R_row[0:NE, TP:T], ps[0:NE, 6, 0:NS]), r_row, 2)
                experts(NE, S_MOE, HALVES, True, 5)
            with dve.Else():
                s = Serial(dve, dve_chain2)
                lower_tokens(EARLY, 2 * NT)
                dve.wait_ge(r_iota, 16)
                one_hot(0)
                repeat(dve, NE, gathered, s)
                for k in range(KT):
                    add_tile(k, 5)
            dve.end_ifs()
            s = Serial(dve, dve_chain3)
            layer_norm(5)


N_OUT = 2 + 2 * NL + 2


def kernel(**inputs):
    import numpy as np
    import concourse.bacc as bacc
    from concourse.bass_utils import run_bass_kernel_spmd as run

    g = {k: np.asarray(v) for k, v in inputs.items()}

    def feat(a):
        a = a.reshape(-1, a.shape[-1])
        return np.ascontiguousarray(a.reshape(a.shape[0], -1, P).transpose(2, 1, 0))

    def slots(w):
        n = w.shape[1] // P
        return w.reshape(KT, P, n, P).transpose(2, 1, 0, 3).reshape(n, P, KT * P)

    def hidden(gu, down):
        f = gu.shape[1] // 2
        a = np.stack([slots(gu[:, :f]), slots(gu[:, f:])], 1).reshape(-1, P, KT * P)
        t = down.reshape(FT, P, KT, P).transpose(2, 0, 1, 3).reshape(12, KT, P, P)
        return [a, t.transpose(0, 2, 1, 3).reshape(12, P, KT * P)]

    win = slots(g["lru_w_in"][0])
    order = [win[[8 + 2 * b, 9 + 2 * b, 2 * b, 2 * b + 1]] for b in range(BLK)]
    order.append(slots(g["lru_w_out"][0]))
    order += [slots(g[n][0]) for n in ("xa_wk", "xa_wv", "xa_wq", "xa_wo")]
    gu, dn = g["ffn_w_gu"][0], g["ffn_w_down"][0]
    for i in range(HALVES):
        c = slice(i * FF, (i + 1) * FF)
        order += hidden(np.concatenate([gu[:, :2 * FF][:, c], gu[:, 2 * FF:][:, c]], 1), dn[c])
    gin = g["gdn_w_in"][0]
    gs = slots(gin[:, :4096])
    order.append(gs.reshape(4, GH, P, KT * P).transpose(1, 0, 2, 3).reshape(4 * GH, P, KT * P))
    order.append(slots(g["gdn_w_out"][0]))
    order += [slots(g[n][1]) for n in ("xa_wk", "xa_wv", "xa_wq", "xa_wo")]
    for e in range(NE):
        order += hidden(g["moe_w_gu"][0, e], g["moe_w_down"][0, e])
    weights = np.concatenate(order, 0)

    par = np.zeros((P, NPAR), np.float32)

    def put(name, a):
        a = a.reshape(a.shape[0], -1)
        par[:a.shape[0], PO[name][0]:PO[name][0] + a.shape[1]] = a

    put("lcw", g["lru_conv_w"][0].reshape(CW, KT, P).transpose(2, 1, 0))
    put("lcb", feat(g["lru_conv_b"][0][None]))
    put("lgb", g["lru_gate_b"][0].reshape(BLK, 2, 2, P).transpose(3, 0, 2, 1))
    put("lam", feat(g["lru_lambda"][0][None]))
    put("h0", feat(g["state_lru_h"][0]))
    put("lhist", feat(g["state_lru_conv"][0]))
    put("lng", g["ln_g"].reshape(NLN, KT, P).transpose(2, 0, 1))
    put("lnb", g["ln_b"].reshape(NLN, KT, P).transpose(2, 0, 1))
    put("gcw", g["gdn_conv_w"][0].reshape(CW, 3, GH, P).transpose(3, 2, 1, 0))
    put("ng", g["gdn_norm_g"][0][:, None])
    put("router", g["moe_router"][0].reshape(KT, P, NE).transpose(1, 0, 2))
    put("wba", gin[:, 4096:].reshape(KT, P, 2 * GH).transpose(1, 0, 2))
    put("dtb", g["gdn_dt_bias"][0][:, None])
    put("alog", g["gdn_a_log"][0][:, None])
    put("eps5", np.full((P, 1), 1e-5, np.float32))
    put("eps6", np.full((P, 1), 1e-6, np.float32))
    put("iota", np.broadcast_to(np.arange(8, dtype=np.float32), (P, 8)))

    tab = np.zeros((P, NTAB), np.float32)
    i, j = np.arange(P)[None, :], np.arange(P)[:, None]
    tab[:, TO["ident"][0]:TO["ident"][1]] = i == j
    tab[:, TO["ones"][0]:TO["ones"][1]] = 1.0
    tab[:, TO["mincl"][0]:TO["mincl"][1]] = np.where(i >= j, 0.0, NEG)
    for v in range(LEVELS):
        w = 1 << v
        tab[:, TO["levels"][0] + v * P:TO["levels"][0] + (v + 1) * P] = \
            (i // (2 * w) == j // (2 * w)) & (i // w % 2 == 1) & (j // w % 2 == 0)
    si, sj = i[:, :NS], j[:NS]
    tab[:NS, TO["smincl"][0]:TO["smincl"][1]] = np.where((si // TS == sj // TS) & (si >= sj), 0.0, NEG)
    tab[:NS, TO["smask"][0]:TO["smask"][1]] = sj // TS == np.arange(NB)[None, :]

    gw = g["lru_gate_w"][0].reshape(BLK, 2, P, 4, P).transpose(0, 2, 1, 3, 4).reshape(BLK, P, KT * P)
    ck = g["cache_mem_k"].reshape(NL, NB, MEM, KT, P).transpose(0, 1, 4, 3, 2).reshape(NL, NB, P, 2048)
    cv = g["cache_mem_v"].reshape(NL, NB, MT, P, D).transpose(0, 1, 3, 2, 4).reshape(NL, NB, P, 2048)
    ins = {
        "xT": feat(np.concatenate([g["x_prompt"].reshape(TP, D), g["x_sample"].reshape(NS, D)], 0)),
        "weights": weights, "params": par, "tables": tab, "lru_gate": gw,
        "places": np.broadcast_to(np.arange(CAP, dtype=np.float32), (P, CAP)),
        "memT": feat(g["mem_prompt"][0]).reshape(P, -1),
        "cache": np.concatenate([ck, cv], 1),
        "gdn_hist": g["state_gdn_conv"][0].reshape(NB * HIST, 3, GH, P).transpose(2, 3, 1, 0).reshape(GH, P, -1),
        "gdn_s0": g["state_gdn_s"][0].transpose(1, 2, 0, 3).reshape(GH, P, NB * P),
    }
    outs = {"y": (P, KT, T), "lru_conv": (P, KT, HIST + NB * HIST), "lru_h": (P, KT, 1 + NB),
            "mem_k": (NL, P, KT, MEM), "mem_v": (NL, P, MT, D), "gdn_conv": (GH, P, 3 * (HIST + NB * HIST)),
            "gdn_sp": (GH, P, P), "gdn_ss": (GH, P, NB * P)}
    nc = bacc.Bacc("TRN2", target_bir_lowering=False, num_devices=1)
    f32 = mybir.dt.float32
    ins = {k: np.ascontiguousarray(v) for k, v in ins.items()}
    I = {k: nc.dram_tensor(k, v.shape, f32, kind="ExternalInput").ap() for k, v in ins.items()}
    O = {k: nc.dram_tensor("out_" + k, v, f32, kind="ExternalOutput").ap() for k, v in outs.items()}
    I["scratch"] = nc.dram_tensor("scratch", (2, GH, T), f32, kind="Internal").ap()
    trunk(nc, I, O)
    r = run(nc, [ins], core_ids=[0]).results[0]
    r = {k: r["out_" + k] for k in outs}

    y = r["y"].transpose(2, 1, 0).reshape(T, D)
    lc = r["lru_conv"].transpose(2, 1, 0).reshape(-1, D)
    lh = r["lru_h"].transpose(2, 1, 0).reshape(-1, D)
    gc = r["gdn_conv"].reshape(GH, P, 3, -1).transpose(3, 2, 0, 1).reshape(-1, 3 * D)
    mk = r["mem_k"].transpose(0, 3, 2, 1).reshape(NL, 1, MEM, XH, XD)
    mv = r["mem_v"].transpose(0, 2, 1, 3).reshape(NL, 1, MEM, XH, XD)
    ss = r["gdn_ss"].reshape(GH, P, NB, P).transpose(2, 0, 1, 3)
    c = np.ascontiguousarray
    return (c(y[:TP][None]), c(y[TP:].reshape(NB, TS, D)), c(lh[:1][None]), c(lc[:HIST].reshape(1, 1, HIST, D)),
            c(r["gdn_sp"][None, None]), c(gc[:HIST].reshape(1, 1, HIST, 3 * D)), c(mk), c(mv),
            c(lh[1:][None]), c(lc[HIST:].reshape(1, NB, HIST, D)), c(ss[None]), c(gc[HIST:].reshape(1, NB, HIST, 3 * D)))
```
